# Optimizing a Trainium2 kernel written in Bass

```python
import math, functools
import jax, jax.numpy as jnp
from jax import lax
import numpy as np

D_MODEL = 1024
BATCH = 1
SEQ = 256
DEPTH = 2

GRID_W = 64
CTX_LEN = 256
CHUNK = 128
Q_BLOCK = 128
RET_HEADS = 4
RET_DK = 32
RET_DV = 64
GLA_HEADS = 4
GLA_DK = 32
GLA_DV = 64
GLA_LOWRANK = 16
GLA_TAU = 16.0
DIFF_HEADS = 4
DIFF_DH = 64
ROPE_BASE = 10000.0
D_MIX = RET_HEADS * RET_DV + GLA_HEADS * GLA_DV + 2 * DIFF_HEADS * DIFF_DH
IN_WIDTHS = (RET_HEADS * RET_DK, RET_HEADS * RET_DK, RET_HEADS * RET_DV, RET_HEADS * RET_DV,
             GLA_HEADS * GLA_DK, GLA_HEADS * GLA_DK, GLA_HEADS * GLA_DV, GLA_HEADS * GLA_DV, GLA_LOWRANK,
             2 * DIFF_HEADS * DIFF_DH, 2 * DIFF_HEADS * DIFF_DH, 2 * DIFF_HEADS * DIFF_DH)
N_IN = 3088
N_EXPERTS = 64
TOP_K = 6
N_GROUPS = 8
TOPK_GROUPS = 4
D_EXPERT = 256
D_SHARED = 256
ROUTED_SCALE = 2.5
MOE_BLOCK = 128
EPS = 1e-6

kernel_name = 'hybrid_ret_gla_diffattn_moe_dit_block'

def rms_norm(x, g=None):
    xf = x.astype(jnp.float32)
    y = xf * lax.rsqrt(jnp.mean(xf * xf, axis=-1, keepdims=True) + EPS)
    if g is not None:
        y = y * g.astype(jnp.float32)
    return y.astype(x.dtype)

def modulate(x, shift, scale):
    return x * (1.0 + scale) + shift

def split_cols(p):
    offs, acc = [], 0
    for w in IN_WIDTHS[:-1]:
        acc += w
        offs.append(acc)
    return jnp.split(p, offs, axis=-1)

def split_heads(a, h):
    b, t, _ = a.shape
    return a.reshape(b, t, h, -1).transpose(0, 2, 1, 3)

def merge_heads(a):
    b, h, t, d = a.shape
    return a.transpose(0, 2, 1, 3).reshape(b, t, h * d)

def diff_heads(a):
    b, t, _ = a.shape
    return a.reshape(b, t, DIFF_HEADS, 2, DIFF_DH).transpose(0, 2, 3, 1, 4)

def rope_2d(x, row, col):
    d = x.shape[-1]
    half, quarter = d // 2, d // 4
    freqs = ROPE_BASE ** (-jnp.arange(quarter, dtype=jnp.float32) / quarter)

    def rot(xp, pos):
        ang = pos[:, None] * freqs[None, :]
        cos, sin = jnp.cos(ang).astype(x.dtype), jnp.sin(ang).astype(x.dtype)
        x1, x2 = xp[..., :quarter], xp[..., quarter:]
        return jnp.concatenate([x1 * cos - x2 * sin, x1 * sin + x2 * cos], axis=-1)

    return jnp.concatenate([rot(x[..., :half], row), rot(x[..., half:], col)], axis=-1)

def to_chunks(a):
    b, h, t, d = a.shape
    return jnp.moveaxis(a.reshape(b, h, t // CHUNK, CHUNK, d), 2, 0)

def from_chunks(a):
    n, b, h, c, d = a.shape
    return jnp.moveaxis(a, 0, 2).reshape(b, h, n * c, d)

def retention_scan(q, k, v, s0, log_g):
    f32 = jnp.float32
    q, k, v = q.astype(f32), k.astype(f32), v.astype(f32)
    idx = jnp.arange(CHUNK, dtype=f32)
    diff = idx[:, None] - idx[None, :]
    lower = diff >= 0
    dmat = jnp.where(lower, jnp.exp(jnp.where(lower, diff, 0.0)[None] * log_g[:, None, None]), 0.0)
    xi = jnp.exp((idx + 1.0)[None, :] * log_g[:, None])
    zeta = jnp.exp((CHUNK - 1.0 - idx)[None, :] * log_g[:, None])
    g_chunk = jnp.exp(CHUNK * log_g)

    def step(s, inp):
        qc, kc, vc = inp
        att = jnp.einsum('bhid,bhjd->bhij', qc, kc) * dmat
        o = jnp.einsum('bhij,bhje->bhie', att, vc) + jnp.einsum('bhid,bhde->bhie', qc, s) * xi[:, :, None]
        s = s * g_chunk[:, None, None] + jnp.einsum('bhjd,bhje->bhde', kc * zeta[:, :, None], vc)
        return s, o

    s, o = lax.scan(step, s0, (to_chunks(q), to_chunks(k), to_chunks(v)))
    return from_chunks(o), s

def gla_scan(q, k, v, log_a, s0):
    f32 = jnp.float32
    q, k, v, log_a = q.astype(f32), k.astype(f32), v.astype(f32), log_a.astype(f32)
    idx = jnp.arange(CHUNK)
    lower = (idx[:, None] >= idx[None, :])[:, :, None]

    def step(s, inp):
        qc, kc, vc, ac = inp
        b = jnp.cumsum(ac, axis=2)
        rel = b[:, :, :, None, :] - b[:, :, None, :, :]
        decay = jnp.where(lower, jnp.exp(jnp.where(lower, rel, 0.0)), 0.0)
        att = jnp.einsum('bhik,bhjk,bhijk->bhij', qc, kc, decay)
        o = jnp.einsum('bhij,bhje->bhie', att, vc) + jnp.einsum('bhik,bhke->bhie', qc * jnp.exp(b), s)
        b_last = b[:, :, -1:, :]
        s = s * jnp.swapaxes(jnp.exp(b_last), -1, -2) + jnp.einsum(
            'bhjk,bhje->bhke', kc * jnp.exp(b_last - b), vc)
        return s, o

    s, o = lax.scan(step, s0, (to_chunks(q), to_chunks(k), to_chunks(v), to_chunks(log_a)))
    return from_chunks(o), s

def bidirectional_scan(scan_f, scan_b, lat_f, lat_b, ctx_f, ctx_b, s0):
    flip = lambda arrs: tuple(a[:, :, ::-1] for a in arrs)
    o_cf, s_cf = scan_f(*ctx_f, s0)
    o_cb, s_cb = scan_b(*flip(ctx_b), s0)
    o_lf, _ = scan_f(*lat_f, s_cf)
    o_lb, _ = scan_b(*flip(lat_b), s_cb)
    return o_lf + o_lb[:, :, ::-1], o_cf + o_cb[:, :, ::-1]

def diff_attend(q, k, v, lam):
    s = jnp.einsum('bhmqd,bhmkd->bhmqk', q, k).astype(jnp.float32) * (DIFF_DH ** -0.5)
    a = jax.nn.softmax(s, axis=-1)
    w = a[:, :, 0] - lam * a[:, :, 1]
    return jnp.einsum('bhqk,bhke->bhqe', w.astype(v.dtype), v)

def token_mixers(h_lat, h_ctx, w_in, w_out, ret_logit, gla_w, gla_b, gla_g, diff_lam, diff_g,
                 row, col, lam_init, need_ctx):
    f32 = jnp.float32
    dt = h_lat.dtype
    bsz, seq, _ = h_lat.shape
    (rq_l, rk_l, rv_l, rg_l, gq_l, gk_l, gv_l, gr_l, glr_l, dq_l, dk_l, dv_l) = split_cols(h_lat @ w_in)
    (rq_c, rk_c, rv_c, rg_c, gq_c, gk_c, gv_c, gr_c, glr_c, dq_c, dk_c, dv_c) = split_cols(h_ctx @ w_in)
    rope = lambda a: rope_2d(a, row, col)

    log_g = jax.nn.log_sigmoid(ret_logit.astype(f32))
    r_lat = (rope(split_heads(rq_l, RET_HEADS)),
             rope(split_heads(rk_l, RET_HEADS)) * RET_DK ** -0.5,
             split_heads(rv_l, RET_HEADS))
    r_ctx = (split_heads(rq_c, RET_HEADS), split_heads(rk_c, RET_HEADS) * RET_DK ** -0.5,
             split_heads(rv_c, RET_HEADS))
    s0_r = jnp.zeros((bsz, RET_HEADS, RET_DK, RET_DV), f32)
    o_rl, o_rc = bidirectional_scan(functools.partial(retention_scan, log_g=log_g[0]),
                                    functools.partial(retention_scan, log_g=log_g[1]),
                                    r_lat, r_lat, r_ctx, r_ctx, s0_r)

    def log_alpha(lr, direction):
        z = (lr @ gla_w[direction] + gla_b[direction]).astype(f32)
        return split_heads(jax.nn.log_sigmoid(z) / GLA_TAU, GLA_HEADS)

    g_ql, g_kl, g_vl = (split_heads(gq_l, GLA_HEADS) * GLA_DK ** -0.5, split_heads(gk_l, GLA_HEADS),
                        split_heads(gv_l, GLA_HEADS))
    g_qc, g_kc, g_vc = (split_heads(gq_c, GLA_HEADS) * GLA_DK ** -0.5, split_heads(gk_c, GLA_HEADS),
                        split_heads(gv_c, GLA_HEADS))
    s0_g = jnp.zeros((bsz, GLA_HEADS, GLA_DK, GLA_DV), f32)
    o_gl, o_gc = bidirectional_scan(gla_scan, gla_scan,
                                    (g_ql, g_kl, g_vl, log_alpha(glr_l, 0)),
                                    (g_ql, g_kl, g_vl, log_alpha(glr_l, 1)),
                                    (g_qc, g_kc, g_vc, log_alpha(glr_c, 0)),
                                    (g_qc, g_kc, g_vc, log_alpha(glr_c, 1)), s0_g)

    lp = diff_lam.astype(f32)
    lam = jnp.exp(jnp.sum(lp[0] * lp[1])) - jnp.exp(jnp.sum(lp[2] * lp[3])) + lam_init
    dq_lh, dk_lh, dv_lh = rope(diff_heads(dq_l)), rope(diff_heads(dk_l)), split_heads(dv_l, DIFF_HEADS)
    dq_ch, dk_ch, dv_ch = diff_heads(dq_c), diff_heads(dk_c), split_heads(dv_c, DIFF_HEADS)
    k_all = jnp.concatenate([dk_ch, dk_lh], axis=3)
    v_all = jnp.concatenate([dv_ch, dv_lh], axis=2)
    n_qb = seq // Q_BLOCK
    q_blocks = jnp.moveaxis(dq_lh.reshape(bsz, DIFF_HEADS, 2, n_qb, Q_BLOCK, DIFF_DH), 3, 0)
    o_blocks = lax.map(lambda qb: diff_attend(qb, k_all, v_all, lam), q_blocks)
    o_dl = jnp.moveaxis(o_blocks, 0, 2).reshape(bsz, DIFF_HEADS, seq, 2 * DIFF_DH)

    def merge(o_r, g_r, o_g, g_g, o_d):
        ret = merge_heads(rms_norm(o_r)).astype(dt) * jax.nn.silu(g_r)
        gla = merge_heads(rms_norm(o_g, gla_g)).astype(dt) * jax.nn.silu(g_g)
        dif = merge_heads(rms_norm(o_d, diff_g) * (1.0 - lam_init)).astype(dt)
        return jnp.concatenate([ret, gla, dif], axis=-1) @ w_out

    m_lat = merge(o_rl, rg_l, o_gl, gr_l, o_dl)
    m_ctx = merge(o_rc, rg_c, o_gc, gr_c, diff_attend(dq_ch, dk_ch, dv_ch, lam)) if need_ctx else None
    return m_lat, m_ctx

def moe_ffn(t, w_router, router_bias, w_eg, w_eu, w_ed, w_sg, w_su, w_sd):
    n_tok, d = t.shape
    scores = jax.nn.sigmoid(t.astype(jnp.float32) @ w_router.astype(jnp.float32))
    sel = scores + router_bias.astype(jnp.float32)
    grp = sel.reshape(n_tok, N_GROUPS, N_EXPERTS // N_GROUPS)
    grp_score = lax.top_k(grp, 2)[0].sum(-1)
    _, g_idx = lax.top_k(grp_score, TOPK_GROUPS)
    g_mask = jax.nn.one_hot(g_idx, N_GROUPS, dtype=jnp.float32).sum(-2) > 0
    e_mask = jnp.repeat(g_mask, N_EXPERTS // N_GROUPS, axis=-1)
    _, e_idx = lax.top_k(jnp.where(e_mask, sel, -jnp.inf), TOP_K)
    w = jnp.take_along_axis(scores, e_idx, axis=-1)
    w = w / jnp.sum(w, axis=-1, keepdims=True) * ROUTED_SCALE

    n_pairs = n_tok * TOP_K
    flat_e = e_idx.reshape(-1)
    flat_tok = jnp.repeat(jnp.arange(n_tok, dtype=jnp.int32), TOP_K)
    order = jnp.argsort(flat_e, stable=True)
    s_e, s_tok, s_w = flat_e[order], flat_tok[order], w.reshape(-1)[order]
    counts = jnp.bincount(flat_e, length=N_EXPERTS)
    padded = (counts + MOE_BLOCK - 1) // MOE_BLOCK * MOE_BLOCK
    p_end = jnp.cumsum(padded)
    p_start = p_end - padded
    c_start = jnp.cumsum(counts) - counts
    dest = p_start[s_e] + jnp.arange(n_pairs, dtype=jnp.int32) - c_start[s_e]
    n_blocks = (n_pairs + N_EXPERTS * (MOE_BLOCK - 1) + MOE_BLOCK - 1) // MOE_BLOCK
    n_rows = n_blocks * MOE_BLOCK
    row_tok = jnp.full((n_rows,), n_tok, jnp.int32).at[dest].set(s_tok)
    row_w = jnp.zeros((n_rows,), jnp.float32).at[dest].set(s_w)
    block_e = jnp.minimum(jnp.searchsorted(p_end, jnp.arange(n_blocks) * MOE_BLOCK, side='right'),
                          N_EXPERTS - 1).astype(jnp.int32)
    t_pad = jnp.concatenate([t, jnp.zeros((1, d), t.dtype)], axis=0)

    def block_ffn(args):
        b, e = args
        rows = lax.dynamic_slice(row_tok, (b * MOE_BLOCK,), (MOE_BLOCK,))
        xb = t_pad[rows]
        hb = jax.nn.silu(xb @ w_eg[e]) * (xb @ w_eu[e])
        return hb @ w_ed[e]

    y = lax.map(block_ffn, (jnp.arange(n_blocks, dtype=jnp.int32), block_e)).reshape(n_rows, d)
    routed = jax.ops.segment_sum(y * row_w[:, None].astype(y.dtype), row_tok,
                                 num_segments=n_tok + 1)[:n_tok]
    shared = (jax.nn.silu(t @ w_sg) * (t @ w_su)) @ w_sd
    return shared + routed

def setup_inputs(seed: int = 0) -> dict:
    key = jax.random.key(seed)
    ks = jax.random.split(key, 32)
    f32 = jnp.float32
    L, D = DEPTH, D_MODEL
    nrm = lambda k, shape, s: jax.random.normal(k, shape, f32) * s
    gamma = 1.0 - 2.0 ** (-5.0 - jnp.arange(RET_HEADS, dtype=f32))
    ret_logit0 = jnp.log(gamma) - jnp.log1p(-gamma)
    return {
        'x': nrm(ks[0], (BATCH, SEQ, D), 1.0),
        'c': nrm(ks[1], (BATCH, D), 1.0),
        'ctx': nrm(ks[2], (BATCH, CTX_LEN, D), 1.0),
        'c_ctx': nrm(ks[3], (D,), 1.0),
        'w_mod': nrm(ks[4], (L, D, 6 * D), 0.5 * D ** -0.5),
        'b_mod': nrm(ks[5], (L, 6 * D), 0.01),
        'g_pre_mix': 1.0 + nrm(ks[6], (L, D), 0.05),
        'g_post_mix': 1.0 + nrm(ks[7], (L, D), 0.05),
        'g_pre_ffn': 1.0 + nrm(ks[8], (L, D), 0.05),
        'g_post_ffn': 1.0 + nrm(ks[9], (L, D), 0.05),
        'w_in': nrm(ks[10], (L, D, N_IN), D ** -0.5),
        'w_out': nrm(ks[11], (L, D_MIX, D), D_MIX ** -0.5),
        'ret_decay_logit': ret_logit0[None, None, :] + nrm(ks[12], (L, 2, RET_HEADS), 0.1),
        'gla_w_gate': nrm(ks[13], (L, 2, GLA_LOWRANK, GLA_HEADS * GLA_DK), GLA_LOWRANK ** -0.5),
        'gla_b_gate': nrm(ks[14], (L, 2, GLA_HEADS * GLA_DK), 0.1),
        'gla_norm_g': 1.0 + nrm(ks[15], (L, GLA_DV), 0.05),
        'diff_lambda': nrm(ks[16], (L, 4, DIFF_DH), 0.1),
        'diff_norm_g': 1.0 + nrm(ks[17], (L, 2 * DIFF_DH), 0.05),
        'w_router': nrm(ks[18], (L, D, N_EXPERTS), D ** -0.5),
        'router_bias': nrm(ks[19], (L, N_EXPERTS), 0.01),
        'w_exp_gate': nrm(ks[20], (L, N_EXPERTS, D, D_EXPERT), D ** -0.5),
        'w_exp_up': nrm(ks[21], (L, N_EXPERTS, D, D_EXPERT), D ** -0.5),
        'w_exp_down': nrm(ks[22], (L, N_EXPERTS, D_EXPERT, D), D_EXPERT ** -0.5),
        'w_sh_gate': nrm(ks[23], (L, D, D_SHARED), D ** -0.5),
        'w_sh_up': nrm(ks[24], (L, D, D_SHARED), D ** -0.5),
        'w_sh_down': nrm(ks[25], (L, D_SHARED, D), D_SHARED ** -0.5),
    }

def reference(x, c, ctx, c_ctx, w_mod, b_mod, g_pre_mix, g_post_mix, g_pre_ffn, g_post_ffn, w_in, w_out,
              ret_decay_logit, gla_w_gate, gla_b_gate, gla_norm_g, diff_lambda, diff_norm_g,
              w_router, router_bias, w_exp_gate, w_exp_up, w_exp_down, w_sh_gate, w_sh_up, w_sh_down):
    bsz, seq, d = x.shape
    rows = seq // GRID_W
    row = jnp.broadcast_to(jnp.arange(rows, dtype=jnp.float32)[:, None], (rows, GRID_W)).reshape(-1)
    col = jnp.broadcast_to(jnp.arange(GRID_W, dtype=jnp.float32)[None, :], (rows, GRID_W)).reshape(-1)
    cond_l = jax.nn.silu(c)
    cond_c = jax.nn.silu(c_ctx)
    h_ctx = ctx
    for layer in range(DEPTH):
        need_ctx = layer < DEPTH - 1
        lam_init = 0.8 - 0.6 * math.exp(-0.3 * layer)
        mod_l = (cond_l @ w_mod[layer] + b_mod[layer])[:, None, :]
        mod_c = cond_c @ w_mod[layer] + b_mod[layer]
        sh1_l, sc1_l, gt1_l, sh2_l, sc2_l, gt2_l = jnp.split(mod_l, 6, axis=-1)
        sh1_c, sc1_c, gt1_c, sh2_c, sc2_c, gt2_c = jnp.split(mod_c, 6, axis=-1)

        hl = modulate(rms_norm(x, g_pre_mix[layer]), sh1_l, sc1_l)
        hc = modulate(rms_norm(h_ctx, g_pre_mix[layer]), sh1_c, sc1_c)
        m_l, m_c = token_mixers(hl, hc, w_in[layer], w_out[layer], ret_decay_logit[layer],
                                gla_w_gate[layer], gla_b_gate[layer], gla_norm_g[layer],
                                diff_lambda[layer], diff_norm_g[layer], row, col, lam_init, need_ctx)
        x = x + gt1_l * rms_norm(m_l, g_post_mix[layer])
        hl2 = modulate(rms_norm(x, g_pre_ffn[layer]), sh2_l, sc2_l)
        if need_ctx:
            h_ctx = h_ctx + gt1_c * rms_norm(m_c, g_post_mix[layer])
            hc2 = modulate(rms_norm(h_ctx, g_pre_ffn[layer]), sh2_c, sc2_c)
            tokens = jnp.concatenate([hl2.reshape(-1, d), hc2.reshape(-1, d)], axis=0)
        else:
            tokens = hl2.reshape(-1, d)
        f = moe_ffn(tokens, w_router[layer], router_bias[layer], w_exp_gate[layer], w_exp_up[layer],
                    w_exp_down[layer], w_sh_gate[layer], w_sh_up[layer], w_sh_down[layer])
        x = x + gt2_l * rms_norm(f[:bsz * seq].reshape(bsz, seq, d), g_post_ffn[layer])
        if need_ctx:
            h_ctx = h_ctx + gt2_c * rms_norm(f[bsz * seq:].reshape(bsz, -1, d), g_post_ffn[layer])
    return x


_drawn_inputs = setup_inputs


def setup_inputs(seed=0):
    import zlib

    import numpy as np

    out = dict(_drawn_inputs(seed))
    spreads = {}
    factors = {}
    for name, (base, spread) in spreads.items():
        noise = np.random.default_rng([zlib.crc32(name.encode()), seed]).standard_normal(out[name].shape)
        drawn = base * np.exp(spread * noise) if base else spread * noise
        out[name] = __import__('jax').numpy.asarray(drawn.astype(out[name].dtype))
    for name, factor in factors.items():
        out[name] = (out[name] * factor).astype(out[name].dtype)
    return out
```

```python
import math
from contextlib import ExitStack

import numpy as np
import concourse.bass as bass
from concourse import mybir

D = 1024
P = 128
KO = D // P
DEPTH = 2
SEQ = 256
CTX = 256
TOK = SEQ + CTX
TILES = TOK // P
GRID_W = 64
N_IN = 3088
NE = 64
TOPK = 6
NGRP = 8
TOPG = 4
DE = 256
LOWRANK = 16
SLOTS = 64
SLOTW = 3 * KO * DE
NSLOT = 4
EPS = 1e-6
LEVELS = (64, 32, 16, 8, 4, 2, 1)
RET_SCALE = 32 ** -0.5
GLA_SCALE = 32 ** -0.5
DIFF_SCALE = 64 ** -0.5
TAU = 16.0
ROUTED_SCALE = 2.5
IN_LOADS = ((0, 768), (768, 768), (1536, 528), (2064, 512), (2576, 512))
BIG = 1e30


def lam_init(layer):
    return 0.8 - 0.6 * math.exp(-0.3 * layer)


def extra_blocks(tokens):
    n = tokens * TOPK // SLOTS
    return (n + NSLOT - 1) // NSLOT * NSLOT


def shape_constants():
    f = np.float32
    c = {}
    i = np.arange(P)
    c["ident"] = np.eye(P, dtype=f)

    def rope(dh):
        quarter, half = dh // 4, dh // 2
        dd = i % dh
        which, w = dd // half, dd % half
        freqs = (f(10000.0) ** (-np.arange(quarter, dtype=f) / f(quarter))).astype(f)
        t = np.arange(SEQ)
        pos = np.stack([(t // GRID_W).astype(f), (t % GRID_W).astype(f)])
        ang = (pos[which] * freqs[w % quarter][:, None]).astype(f)
        perm = np.zeros((P, P), f)
        first = w < quarter
        for m in range(P):
            if first[m]:
                perm[m + quarter, m] = -1.0
            else:
                perm[m - quarter, m] = 1.0
        return perm, np.cos(ang).astype(f), np.sin(ang).astype(f)

    c["perm_r"], c["cos_r"], c["sin_r"] = rope(32)
    c["perm_d"], c["cos_d"], c["sin_d"] = rope(64)
    t, j = i[:, None], i[None, :]
    c["inc_f"] = (t <= j).astype(f)
    c["exc_f"] = (t > j).astype(f)
    c["inc_b"] = (t >= j).astype(f)
    c["exc_b"] = (t < j).astype(f)
    c["ones"] = np.ones((P, P), f)
    lev, masks = [], []
    for s in LEVELS:
        blk_t, blk_j = t // (2 * s), j // (2 * s)
        same = blk_t == blk_j
        mid = blk_j * 2 * s + s
        second = (j % (2 * s)) >= s
        qf = same & second & (t >= mid) & (t <= j)
        kf = same & ~second & (t > j) & (t < mid)
        qb = same & ~second & (t >= j) & (t < mid)
        kb = same & second & (t >= mid) & (t < j)
        lev += [qf, kf, qb, kb]
        masks.append(same & ((t % (2 * s) >= s) != second))
    c["levels"] = np.concatenate(lev, 1).astype(f)
    c["zero"] = np.zeros((P, 96), f)
    q = np.arange(SEQ)[None, None, :]
    k = (np.arange(2)[None, :, None] * P + i[:, None, None])
    c["dist"] = (q - k).reshape(P, 2 * SEQ).astype(f)
    c["row"] = np.broadcast_to(np.arange(P, dtype=f), (P, P))
    c["tok1"] = (np.arange(TILES)[None, :] * P + i[:, None] + 1).astype(f)
    c["pad"] = np.stack([i + SEQ * (2 - l) + 1 for l in range(DEPTH)], 1).astype(f)
    return c, np.concatenate(masks, 1).astype(f)


CONSTS, MASKS = shape_constants()
COFF, _at = {}, 0
for _k, _v in CONSTS.items():
    COFF[_k] = (_at, _v.shape[1])
    _at += _v.shape[1]
CWIDTH = _at


def hybrid_block(nc, x, c, ctx, c_ctx, w_mod, b_mod, g_pre_mix, g_post_mix, g_pre_ffn, g_post_ffn,
                 w_in, w_out, ret_decay_logit, gla_w_gate, gla_b_gate, gla_norm_g, diff_lambda,
                 diff_norm_g, w_router, router_bias, w_exp_gate, w_exp_up, w_exp_down,
                 w_sh_gate, w_sh_up, w_sh_down, consts, level_masks, out):
    f32, u32, i32 = mybir.dt.float32, mybir.dt.uint32, mybir.dt.int32
    ALU, ACT, AX = mybir.AluOpType, mybir.ActivationFunctionType, mybir.AxisListType
    stack = ExitStack()
    sems = {}

    def sem(name):
        if name not in sems:
            sems[name] = stack.enter_context(nc.semaphore(name))
        return sems[name]

    def sb(name, width, dt=f32, parts=P):
        return stack.enter_context(nc.sbuf_tensor(name, [parts, width], dt))

    with stack:
        X = sb("X", TILES * D)
        hreg = sb("hreg", TILES * D)
        wreg = sb("wreg", 2 * SLOTW)
        qkreg = sb("qkreg", SLOTW)
        vreg = sb("vreg", SLOTW)
        areg = sb("areg", SLOTW)
        tmp = sb("tmp", 4096)
        cst = sb("cst", CWIDTH)
        vecs = sb("vecs", DEPTH * (4 * KO + 6 * KO))
        wrt = sb("wrt", DEPTH * KO * NE)
        rbias = sb("rbias", DEPTH * NE)
        glaw = sb("glaw", DEPTH * 2 * P, parts=LOWRANK + 1)
        glab = glaw[LOWRANK:LOWRANK + 1, :]
        glag = sb("glag", DEPTH * 64)
        diffg = sb("diffg", DEPTH * 128)
        retl = sb("retl", DEPTH * 8)
        lamt = sb("lamt", DEPTH * 8)
        cond = sb("cond", KO * 2)
        condr = sb("condr", KO * 2)
        modc = sb("modc", 6 * KO * 2)
        mskt = sb("mskt", len(LEVELS) * P, mybir.dt.uint8)
        retc = sb("retc", DEPTH * 5 * 4)
        st = sb("st", 512)
        glrT = areg[0:LOWRANK + 1, 6144 - TOK:6144]
        rsc = hreg[:, 3072:4096]
        small = tmp[:, 3448:4096]
        idx = sb("idx", NE + extra_blocks(TOK) + NSLOT, u32)
        wsl = sb("wsl", NE + extra_blocks(TOK) + NSLOT)
        idxb = sb("idxb", NSLOT, u32)
        wb = sb("wb", NSLOT)
        ei8 = sb("ei8", TILES * 8, u32)
        gi8 = sb("gi8", TILES * 8, u32)
        tab = sb("tab", NE + extra_blocks(TOK), i32, parts=1)
        ngt = sb("ngt", 1, i32, parts=1)
        eps = sb("eps", 1)
        bank = [stack.enter_context(nc.psum_tensor(f"bank{i}", [P, 512], f32)) for i in range(8)]

        def const(name, parts=P):
            at, w = COFF[name]
            return cst[0:parts, at:at + w]

        ident = const("ident")
        h2d = [nc.dram_tensor(f"h2_rows{l}", (SEQ * (2 - l) + SLOTS, D), f32).ap() for l in range(DEPTH)]
        accd = [nc.dram_tensor(f"acc_rows{l}", (SEQ * (2 - l) + SLOTS, D), f32).ap() for l in range(DEPTH)]

        Xt = X[:, :].rearrange("p (t d) -> p t d", t=TILES)
        hT = hreg[:, :].rearrange("p (k t) -> p k t", k=KO)
        mix = hreg[:, :].rearrange("p (t d) -> p t d", t=TILES)
        mixT = areg[:, 0:TILES * D].rearrange("p (k t) -> p k t", k=KO)
        slot = [wreg[:, 0:SLOTW], wreg[:, SLOTW:2 * SLOTW], qkreg[:, :], vreg[:, :]]
        qk = qkreg[:, :].rearrange("p (n t) -> p n t", t=TOK)
        RQ, RK, GQ, GK, DQ, DK = 0, 1, 2, 3, 4, 8
        vv = vreg[:, :].rearrange("p (n t w) -> p n t w", n=3, w=512)
        bc = qkreg[:, :].rearrange("p (v s d) -> p v s d", v=3, d=D)
        vec = vecs[:, :].rearrange("p (l n k) -> p l n k", l=DEPTH, k=KO)
        mcol = modc[:, :].rearrange("p (j k s) -> p j k s", j=6, s=2)
        SH1, SC1, GT1, SH2, SC2, GT2 = range(6)
        wr = wrt[:, :].rearrange("p (l k e) -> p l k e", l=DEPTH, e=NE)
        cnd = cond[:, :].rearrange("p (k s) -> p k s", s=2)
        la = tmp[:, 0:1024].rearrange("p (t a) -> p t a", t=TILES)
        Eb = tmp[:, 1024:2048].rearrange("p (t a) -> p t a", t=TILES)
        QKb = [tmp[:, 2048 + 1024 * i:3072 + 1024 * i].rearrange("p (a t) -> p a t", a=2) for i in range(2)]
        attd = areg[:, 0:2048].rearrange("p (h t q) -> p h t q", h=4, q=P)
        atto = areg[:, 2048:4096].rearrange("p (h t q) -> p h t q", h=4, q=P)
        attx = areg[:, 4096:6144].rearrange("p (h t q) -> p h t q", h=4, q=SEQ)

        def ratt(h, kt):
            a = h * 1536
            return areg[:, a + kt * 256:a + kt * 256 + 256] if kt < 2 else \
                areg[:, a + 512 + (kt - 2) * 512:a + 1024 + (kt - 2) * 512]

        levels = const("levels").rearrange("p (v a) -> p v a", a=512)
        masks = mskt[:, :].rearrange("p (v a) -> p v a", a=P)

        full = [sem(f"bank{i}_full") for i in range(8)]
        free = [sem(f"bank{i}_free") for i in range(8)]
        uses, where, turn = [0] * 8, {}, {"g": 0, "l": 0}
        pools = {"g": (0, 1, 2, 3, 4, 5), "l": (6, 7)}

        def bank_of(pe, key, pool="g"):
            b = pools[pool][turn[pool] % len(pools[pool])]
            turn[pool] += 1
            where[key] = (b, uses[b])
            if uses[b]:
                pe.wait_ge(free[b], uses[b])
            uses[b] += 1
            return bank[b]

        def done(ins, key):
            ins.then_inc(full[where[key][0]], 1)

        def product(eng, key):
            b, n = where[key]
            eng.wait_ge(full[b], n + 1)
            return bank[b]

        def release(ins, key):
            ins.then_inc(free[where[key][0]], 1)

        def taken(eng, key):
            b, n = where[key]
            eng.wait_ge(free[b], n + 1)

        def ge(eng, s, v):
            if not (isinstance(v, int) and v <= 0):
                eng.wait_ge(s, v)

        class Chain:
            def __init__(self, eng, name):
                self.eng, self.s, self.n = eng, sem(name), 0

            def __call__(self, ins):
                self.n += 1
                ins.then_inc(self.s, 1)
                self.eng.wait_ge(self.s, self.n)

            def mark(self, ins):
                self.n += 1
                ins.then_inc(self.s, 1)

            def wait(self):
                if self.n:
                    self.eng.wait_ge(self.s, self.n)

        BOOT_LOADS = 28
        def boot(eng):
            eng.wait_ge(sem("boot_loaded"), 16 * BOOT_LOADS)

        def last_use(l, i):
            return {8: ("v", l, 0, 3), 9: ("v", l, 1, 3), 10: ("qk", l, DQ + 3), 11: ("qk", l, DK + 3),
                    12: ("v", l, 2, 3), 13: ("m", l, 0, nt_of(l) - 1)}[i]

        block = stack.enter_context(nc.Block())

        def nt_of(l):
            return TILES if l < DEPTH - 1 else 2

        def streams(l):
            return (0, 1) if l < DEPTH - 1 else (0,)

        def shared_stored(eng, l):
            for par in range(2):
                eng.wait_ge(sem(f"sh_stored{l}_{par}"), 16 * nt_of(l) // 2)

        def x_ready(eng, l, t):
            if l == 0:
                boot(eng)
            else:
                eng.wait_ge(sem(f"x_done{l - 1}"), t + 1)

        @block.tensor
        def _(pe):
            mm, tr = nc.tensor.matmul, nc.tensor.transpose
            boot(pe)
            pe.wait_ge(sem("cond_done"), 1)
            for l in range(DEPTH):
                nt = nt_of(l)
                ntok = nt * P
                loads = {0: 0, 1: 0}

                def loaded(i, n=1):
                    loads[i % 2] += 16 * n
                    pe.wait_ge(sem(f"w{l}_{i % 2}_loaded"), loads[i % 2])
                    return slot[i % 2]

                pm = bank_of(pe, ("mod", l), "l")
                mm(pm[:, 0:96], ident, const("zero"), start=True, stop=False)
                for k in range(KO):
                    w = loaded(k).rearrange("p (j n k) -> p j n k", j=6, k=KO)
                    for j in range(6):
                        for o in range(KO):
                            at = (j * KO + o) * 2
                            last = mm(pm[:, at:at + 2], w[:, j, :, o], cnd[:, k, :], start=False,
                                      stop=(k == KO - 1 and j == 5 and o == KO - 1))
                    if k < KO - 1:
                        last.then_inc(sem(f"mod{l}_chunk"), 1)
                    else:
                        done(last, ("mod", l))

                for t in range(TILES):
                    pe.wait_ge(sem(f"xn1_{l}"), t + 1)
                    for half in range(2):
                        b = bank_of(pe, ("t1", l, t, half))
                        xn = tmp[:, (t % 2) * D:(t % 2 + 1) * D].rearrange("p (n k) -> p n k", k=KO)
                        for i in range(4):
                            last = tr(b[:, i * P:(i + 1) * P], xn[:, :, half * 4 + i], ident)
                        done(last, ("t1", l, t, half))

                for t in range(TILES):
                    taken(pe, ("t1", l, t, 0))
                    taken(pe, ("t1", l, t, 1))

                def project_T(w, col, n, key):
                    b = bank_of(pe, key)
                    for k in range(KO):
                        last = mm(b[0:n, :], w[:, k, col:col + n], hT[:, k, :], start=(k == 0), stop=(k == KO - 1))
                    done(last, key)

                def project(w, col, t, key):
                    b = bank_of(pe, key)
                    for k in range(KO):
                        last = mm(b[:, :], hT[:, k, t * P:(t + 1) * P], w[:, k, col:col + 512],
                                  start=(k == 0), stop=(k == KO - 1))
                    done(last, key)

                def rope(n):
                    taken(pe, ("qk", l, n))
                    b = bank_of(pe, ("rope", l, n))
                    done(mm(b[:, 0:SEQ], const("perm_r" if n < 4 else "perm_d"), qk[:, n, 0:SEQ],
                            start=True, stop=True), ("rope", l, n))

                for i, (_, width) in enumerate(IN_LOADS):
                    w = loaded(KO + i)[:, 0:KO * width].rearrange("p (k n) -> p k n", k=KO)
                    if i < 2:
                        project_T(w, 0, P, ("qk", l, 2 * i))
                        project_T(w, P, P, ("qk", l, 2 * i + 1))
                        for t in range(TILES):
                            project(w, 2 * P, t, ("v", l, i, t))
                        if i == 0:
                            rope(RQ)
                            rope(RK)
                    elif i == 2:
                        project_T(w, 0, LOWRANK, ("glr", l))
                        for h in range(4):
                            project_T(w, LOWRANK + h * P, P, ("qk", l, DQ + h))
                        for h in range(4):
                            rope(DQ + h)
                    elif i == 3:
                        for h in range(4):
                            project_T(w, h * P, P, ("qk", l, DK + h))
                        for h in range(4):
                            rope(DK + h)
                    else:
                        for t in range(TILES):
                            project(w, 0, t, ("v", l, 2, t))

                taken(pe, ("glr", l))
                pe.wait_ge(sem(f"ones_row{l}"), 16)
                for t in range(TILES):
                    b = bank_of(pe, ("z", l, t))
                    done(mm(b[:, 0:256], glrT[:, t * P:(t + 1) * P], glaw[:, l * 256:(l + 1) * 256], start=True, stop=True),
                         ("z", l, t))

                def gla_scores(v, q_of, k_of, tiles):
                    for h in range(4):
                        b = bank_of(pe, ("gs", l, v, h))
                        r = slice(32 * h, 32 * h + 32)
                        for t in range(nt):
                            last = mm(b[:, t * P:(t + 1) * P], k_of(r, t), q_of(r, tiles[t]), start=True, stop=True)
                        done(last, ("gs", l, v, h))

                own = list(range(4))
                other = [1, 0, 3, 2]
                taken(pe, ("qk", l, GQ))
                taken(pe, ("qk", l, GK))
                gla_scores("d", lambda r, t: qk[r, GQ, t * P:(t + 1) * P], lambda r, t: qk[r, GK, t * P:(t + 1) * P], own)
                for t in range(TILES):
                    taken(pe, ("z", l, t))

                def decays(v):
                    for p in range(nt // 2):
                        b = bank_of(pe, ("E", l, v, p))
                        for i in range(2):
                            t = 2 * p + i
                            af, ab = la[:, t, 0:P], la[:, t, P:2 * P]
                            o = b[:, i * 256:(i + 1) * 256]
                            if v < len(LEVELS):
                                mm(o, af, levels[:, v, 0:256], start=True, stop=False)
                                last = mm(o, ab, levels[:, v, 256:512], start=False, stop=True)
                            elif i == 0:
                                mm(o[:, 0:P], ab, const("inc_b"), start=True, stop=True)
                                last = mm(o[:, P:256], af, const("exc_f"), start=True, stop=True)
                            else:
                                mm(o[:, 0:P], af, const("inc_f"), start=True, stop=True)
                                last = mm(o[:, P:256], ab, const("exc_b"), start=True, stop=True)
                        done(last, ("E", l, v, p))

                NL = len(LEVELS) + 1
                decays(0)
                for v in range(NL):
                    if v + 1 < NL:
                        decays(v + 1)
                    pe.wait_ge(sem(f"gla_qk{l}"), v + 1)
                    buf = QKb[v % 2]
                    gla_scores(v, lambda r, t: buf[r, 0, t * P:(t + 1) * P],
                               lambda r, t: buf[r, 1, t * P:(t + 1) * P], own if v < NL - 1 else other)
                for p in range(2):
                    b = bank_of(pe, ("E", l, "x", p))
                    sides = (("inc_f", "inc_b"), ("exc_f", "exc_b"))[p]
                    for i in range(2):
                        t = 2 * p + i
                        between = ((None, 1), (0, None))[i] if p == 0 else ((3, None), (None, 2))[i]
                        for d in range(2):
                            o = b[:, i * 256 + d * P:i * 256 + (d + 1) * P]
                            whole = between[d]
                            last = mm(o, la[:, t, d * P:(d + 1) * P], const(sides[d]), start=True, stop=whole is None)
                            if whole is not None:
                                last = mm(o, la[:, whole, d * P:(d + 1) * P], const("ones"), start=False, stop=True)
                    done(last, ("E", l, "x", p))
                pe.wait_ge(sem(f"gla_qk{l}"), NL + 1)
                buf = QKb[NL % 2]
                for h in range(4):
                    b = bank_of(pe, ("gs", l, "x", h))
                    r = slice(32 * h, 32 * h + 32)
                    for kt in range(2):
                        for d in range(2):
                            last = mm(b[:, kt * SEQ:(kt + 1) * SEQ], buf[r, 1, d * SEQ + kt * P:d * SEQ + (kt + 1) * P],
                                      buf[r, 0, d * SEQ:(d + 1) * SEQ], start=(d == 0), stop=(d == 1))
                    done(last, ("gs", l, "x", h))
                for h in range(4):
                    taken(pe, ("gs", l, NL - 2, h))
                    taken(pe, ("gs", l, NL - 1, h))
                    taken(pe, ("gs", l, "x", h))
                for t in range(TILES):
                    taken(pe, ("v", l, 1, t))
                for t in range(nt):
                    b = bank_of(pe, ("og", l, t))
                    for h in range(4):
                        terms = [(attd[:, h, t, :], t), (atto[:, h, t ^ 1, :], t ^ 1)]
                        if t < 2:
                            terms += [(attx[:, h, kt, t * P:(t + 1) * P], 2 + kt) for kt in range(2)]
                        for n, (a, kt) in enumerate(terms):
                            last = mm(b[:, h * 64:(h + 1) * 64], a, vv[:, 1, kt, h * 64:(h + 1) * 64],
                                      start=(n == 0), stop=(n == len(terms) - 1))
                    done(last, ("og", l, t))

                pe.wait_ge(sem(f"roped{l}"), 2)
                for h in range(4):
                    r = slice(32 * h, 32 * h + 32)
                    for kt in range(TILES):
                        b = bank_of(pe, ("rs", l, h, kt))
                        n = SEQ if kt < 2 else ntok
                        done(mm(b[:, 0:n], qk[r, RK, kt * P:(kt + 1) * P], qk[r, RQ, 0:n], start=True, stop=True),
                             ("rs", l, h, kt))
                for t in range(TILES):
                    taken(pe, ("v", l, 0, t))
                    for h in range(4):
                        taken(pe, ("rs", l, h, t))
                for t in range(nt):
                    b = bank_of(pe, ("or", l, t))
                    for h in range(4):
                        kts = (0, 1, 2, 3) if t < 2 else (2, 3)
                        for n, kt in enumerate(kts):
                            last = mm(b[:, h * 64:(h + 1) * 64], ratt(h, kt)[:, t * P:(t + 1) * P],
                                      vv[:, 0, kt, h * 64:(h + 1) * 64], start=(n == 0), stop=(n == len(kts) - 1))
                    done(last, ("or", l, t))

                pe.wait_ge(sem(f"roped{l}"), 10)
                units = [(t, h) for t in range(nt) for h in range(4)]

                def diff_scores(t, h):
                    k0 = 0 if t < 2 else SEQ
                    for m in range(2):
                        b = bank_of(pe, ("ds", l, t, h, m))
                        r = slice(64 * m, 64 * m + 64)
                        done(mm(b[:, 0:TOK - k0], qk[r, DQ + h, t * P:(t + 1) * P], qk[r, DK + h, k0:TOK],
                                start=True, stop=True), ("ds", l, t, h, m))

                diff_scores(*units[0])
                for t in range(TILES):
                    taken(pe, ("v", l, 2, t))
                for u, (t, h) in enumerate(units):
                    if u + 1 < len(units):
                        diff_scores(*units[u + 1])
                    kts = (0, 1, 2, 3) if t < 2 else (2, 3)
                    pe.wait_ge(sem(f"diff_w{l}"), u + 1)
                    b = bank_of(pe, ("wt", l, u))
                    for n in range(len(kts)):
                        last = tr(b[:, n * P:(n + 1) * P], tmp[:, (u % 2) * 1024:(u % 2) * 1024 + 512][:, n * P:(n + 1) * P], ident)
                    done(last, ("wt", l, u))
                    if h == 0:
                        ob = bank_of(pe, ("do", l, t), "l")
                    taken(pe, ("wt", l, u))
                    WT = tmp[:, 2048 + (u % 2) * 512:2560 + (u % 2) * 512]
                    for n, kt in enumerate(kts):
                        last = mm(ob[:, h * P:(h + 1) * P], WT[:, n * P:(n + 1) * P], vv[:, 2, kt, h * P:(h + 1) * P],
                                  start=(n == 0), stop=(n == len(kts) - 1))
                    if h == 3:
                        done(last, ("do", l, t))
                    else:
                        last.then_inc(sem(f"diff_o{l}"), 1)

                for t in range(nt):
                    pe.wait_ge(sem(f"mixed{l}"), t + 1)
                    for half in range(2):
                        b = bank_of(pe, ("t2", l, t, half))
                        mv = mix[:, t, :].rearrange("p (n k) -> p n k", k=KO)
                        for i in range(4):
                            last = tr(b[:, i * P:(i + 1) * P], mv[:, :, half * 4 + i], ident)
                        done(last, ("t2", l, t, half))

                def broadcast(j, s, key):
                    for half in range(2):
                        b = bank_of(pe, key + (half,))
                        for i in range(4):
                            last = mm(b[:, i * P:(i + 1) * P], mcol[:, j, half * 4 + i, s:s + 1].to_broadcast([P, P]),
                                      ident, start=True, stop=True)
                        done(last, key + (half,))

                for j in (GT1, SC2, SH2):
                    for s in streams(l):
                        broadcast(j, s, ("bc", l, j, s))
                for t in range(nt):
                    taken(pe, ("t2", l, t, 0))
                    taken(pe, ("t2", l, t, 1))
                for half in range(2):
                    w = loaded(13 + half)[:, 0:4096].rearrange("p (k n) -> p k n", k=KO)
                    for t in range(nt):
                        b = bank_of(pe, ("m", l, half, t))
                        for k in range(KO):
                            last = mm(b[:, :], mixT[:, k, t * P:(t + 1) * P], w[:, k, :], start=(k == 0), stop=(k == KO - 1))
                        done(last, ("m", l, half, t))
                for t in range(nt):
                    pe.wait_ge(sem(f"h2_{l}"), t + 1)
                    for half in range(2):
                        b = bank_of(pe, ("t3", l, t, half))
                        hv = tmp[:, (t % 2) * D:(t % 2 + 1) * D].rearrange("p (n k) -> p n k", k=KO)
                        for i in range(4):
                            last = tr(b[:, i * P:(i + 1) * P], hv[:, :, half * 4 + i], ident)
                        done(last, ("t3", l, t, half))
                for t in range(nt):
                    taken(pe, ("t3", l, t, 0))
                    taken(pe, ("t3", l, t, 1))
                b = bank_of(pe, ("rt", l))
                for t in range(nt):
                    for k in range(KO):
                        last = mm(b[:, t * NE:(t + 1) * NE], mixT[:, k, t * P:(t + 1) * P], wr[:, l, k, :],
                                  start=(k == 0), stop=(k == KO - 1))
                done(last, ("rt", l))
                wsh = loaded(15, 3)
                wgu = wsh[:, 0:4096].rearrange("p (w k n m) -> p w k n m", w=2, k=KO, m=2)
                for m in range(2):
                    for w in range(2):
                        b = bank_of(pe, ("sh", l, m, w))
                        for k in range(KO):
                            last = mm(b[:, 0:ntok], wgu[:, w, k, :, m], mixT[:, k, 0:ntok], start=(k == 0), stop=(k == KO - 1))
                        done(last, ("sh", l, m, w))
                msk = rsc[:, 256:512]
                pe.wait_ge(sem(f"masked{l}"), 1)
                b = bank_of(pe, ("rank", l))
                for t in range(nt):
                    for n, u in enumerate(range(t + 1)):
                        last = mm(b[:, t * NE:(t + 1) * NE], const("exc_b") if u == t else const("ones"),
                                  msk[:, u * NE:(u + 1) * NE], start=(n == 0), stop=(n == t))
                done(last, ("rank", l))
                b = bank_of(pe, ("cnt", l))
                for t in range(nt):
                    last = mm(b[0:NE, 0:1], msk[:, t * NE:(t + 1) * NE], const("ones")[:, 0:1], start=(t == 0), stop=(t == nt - 1))
                done(last, ("cnt", l))
                nx = extra_blocks(ntok)
                nbt = NE + nx + NSLOT
                xcol = small[0:NE, 0:1]
                pe.wait_ge(sem(f"xcol{l}"), 1)
                b = bank_of(pe, ("xs", l))
                done(mm(b[:, 0:NE], xcol.to_broadcast([NE, P]), const("exc_b", NE)[:, 0:NE], start=True, stop=True), ("xs", l))
                b = bank_of(pe, ("xe", l))
                done(mm(b[0:NE, 0:1], const("inc_f", NE)[:, 0:NE], xcol, start=True, stop=True), ("xe", l))
                b = bank_of(pe, ("nx", l))
                done(mm(b[0:1, 0:1], xcol, const("ones", NE)[:, 0:1], start=True, stop=True), ("nx", l))
                pe.wait_ge(sem(f"ended{l}"), 1)
                b = bank_of(pe, ("be", l))
                done(mm(b[0:1, 0:nx], const("ones", NE)[:, 0:1], small[0:NE, 128:128 + nx], start=True, stop=True), ("be", l))
                wd = wsh[:, 4096:6144].rearrange("p (m n) -> p m n", m=2)
                pe.wait_ge(sem(f"shared_h{l}"), 2)
                for t in range(nt):
                    for half in range(2):
                        b = bank_of(pe, ("sd", l, t, half))
                        for m in range(2):
                            last = mm(b[:, :], areg[:, 4096 + m * 512 + t * P:4096 + m * 512 + (t + 1) * P],
                                      wd[:, m, half * 512:(half + 1) * 512], start=(m == 0), stop=(m == 1))
                        done(last, ("sd", l, t, half))
                b = bank_of(pe, ("slot", l), "l")
                Lh = hreg[:, 1536:3072].rearrange("p (n s) -> p n s", s=SLOTS)
                for t in range(nt):
                    pe.wait_ge(sem(f"onehots{l}"), t + 1)
                    Hh = tmp[:, 2048:2048 + TOPK * 2 * nbt].rearrange("p (k a) -> p k a", k=TOPK)
                    for k in range(TOPK):
                        last = mm(b[0:SLOTS, 0:2 * nbt], Lh[:, t * TOPK + k, :], Hh[:, k, :],
                                  start=(t == 0 and k == 0), stop=(t == nt - 1 and k == TOPK - 1))
                    if t < nt - 1:
                        last.then_inc(sem(f"slots_used{l}"), 1)
                    else:
                        done(last, ("slot", l))

                for i in range(8):
                    pe.wait_ge(free[i], uses[i])
                pe.wait_ge(sem(f"routed{l}"), 1)
                ng = pe.value_load(ngt[0:1, 0:1], min_val=0, max_val=nx // NSLOT) + NE // NSLOT

                def tokens_T(b, par):
                    ge(pe, sem(f"gathered{l}_{par}"), (b + 2 - par) * 8)
                    ge(pe, sem(f"xT_copied{l}"), b - 1)
                    xg = hreg[0:SLOTS, par * D:(par + 1) * D].rearrange("p (n k) -> p n k", k=KO)
                    mm(bank[par][:, 0:SLOTS], xg[:, :, 0], ident[0:SLOTS, 0:SLOTS], start=True, stop=True)
                    for k in range(1, KO):
                        last = tr(bank[par][:, k * SLOTS:(k + 1) * SLOTS], xg[:, :, k], ident[0:SLOTS, 0:SLOTS])
                    last.then_inc(sem(f"xT{l}"), 1)

                def gate_up(b, g, j):
                    pe.wait_ge(sem(f"we{l}_{j}_loaded"), (g + 1) * 48)
                    ge(pe, sem(f"xT_copied{l}"), b + 1)
                    ge(pe, sem(f"hidden{l}"), b - 1)
                    w = slot[j][:, 0:4096].rearrange("p (w k n m) -> p w k n m", w=2, k=KO, m=2)
                    xT = hreg[:, 2048 + (j % 2) * 512:2560 + (j % 2) * 512].rearrange("p (k s) -> p k s", k=KO)
                    for a in range(2):
                        for m in range(2):
                            for k in range(KO):
                                last = mm(bank[2 + j % 2][:, (a * 2 + m) * SLOTS:(a * 2 + m + 1) * SLOTS],
                                          w[:, a, k, :, m], xT[:, k, :], start=(k == 0), stop=(k == KO - 1))
                    last.then_inc(sem(f"gate_up{l}"), 1)

                def down(b, j):
                    ge(pe, sem(f"hidden{l}"), b + 1)
                    ge(pe, sem(f"y0_out{l}"), b - 1)
                    ge(pe, sem(f"y1_out{l}"), b - 1)
                    w = slot[j][:, 4096:6144].rearrange("p (m n) -> p m n", m=2)
                    hid = hreg[:, 3072 + (j % 2) * 128:3200 + (j % 2) * 128]
                    for half in range(2):
                        for m in range(2):
                            last = mm(bank[4 + 2 * (j % 2) + half][0:SLOTS, :], hid[:, m * SLOTS:(m + 1) * SLOTS],
                                      w[:, m, half * 512:(half + 1) * 512], start=(m == 0), stop=(m == 1))
                    last.then_inc(sem(f"down{l}"), 1)

                def group(g):
                    for j in range(NSLOT):
                        b = g * NSLOT + j
                        tokens_T(b + 1, (j + 1) % 2)
                        gate_up(b, g, j)
                        if not (isinstance(b, int) and b == 0):
                            down(b - 1, (j - 1) % NSLOT)

                tokens_T(0, 0)
                group(0)
                with pe.Fori(1, ng) as g:
                    group(g)
                down(ng * NSLOT - 1, NSLOT - 1)
                pe.wait_ge(sem(f"y0_out{l}"), ng * NSLOT)
                pe.wait_ge(sem(f"y1_out{l}"), ng * NSLOT)
                pe.wait_ge(sem(f"xT_copied{l}"), ng * NSLOT + 1)
                for s in streams(l):
                    broadcast(GT2, s, ("bc", l, GT2, s))

        @block.sync
        def _(sp):
            n = [0]

            def load(dst, src):
                n[0] += 1
                sp.dma_start(dst, src).then_inc(sem("boot_loaded"), 16)

            load(cst[:, :], consts)
            load(Xt[:, 0:2, :], x[0].rearrange("(t p) d -> p t d", p=P))
            load(Xt[:, 2:4, :], ctx[0].rearrange("(t p) d -> p t d", p=P))
            cr = condr[:, :].rearrange("p (s k) -> p s k", s=2)
            load(cr[:, 0, :], c[0].rearrange("(p k) -> p k", k=KO))
            load(cr[:, 1, :], c_ctx.rearrange("(p k) -> p k", k=KO))
            for i, g in enumerate((g_pre_mix, g_post_mix, g_pre_ffn, g_post_ffn)):
                load(vec[:, :, i, :], g.rearrange("l (p k) -> p l k", k=KO))
            for l in range(DEPTH):
                load(vec[:, l, 4:10, :], b_mod[l].rearrange("(j p k) -> p j k", j=6, k=KO))
                load(wr[:, l, :, :], w_router[l].rearrange("(p k) e -> p k e", k=KO))
                load(glaw[0:LOWRANK, l * 256:(l + 1) * 256].rearrange("r (d a) -> r d a", d=2), gla_w_gate[l].rearrange("d r a -> r d a"))
                load(glab[:, l * 256:(l + 1) * 256], gla_b_gate[l].rearrange("(o d) a -> o (d a)", o=1))
                load(rbias[:, l * NE:(l + 1) * NE], router_bias[l].partition_broadcast(P))
                load(glag[:, l * 64:(l + 1) * 64], gla_norm_g[l].partition_broadcast(P))
                load(diffg[:, l * 128:(l + 1) * 128], diff_norm_g[l].partition_broadcast(P))
                load(tmp[:, l * 256:(l + 1) * 256], diff_lambda[l].rearrange("a b -> (a b)").partition_broadcast(P))
                load(retl[:, l * 8:(l + 1) * 8], ret_decay_logit[l].rearrange("a b -> (a b)").partition_broadcast(P))
            load(hreg[:, 0:len(LEVELS) * P], level_masks)
            assert n[0] == BOOT_LOADS
            for l in range(DEPTH):
                nt = nt_of(l)
                if l:
                    sp_ng = ng_prev
                def slot_free(i):
                    if i < 2:
                        if l:
                            sp.wait_ge(sem(f"down{l - 1}"), sp_ng * NSLOT)
                        return
                    before = i - 2
                    if before < KO - 1:
                        sp.wait_ge(sem(f"mod{l}_chunk"), before + 1)
                    elif before == KO - 1:
                        product(sp, ("mod", l))
                    else:
                        product(sp, last_use(l, before))

                for k in range(KO):
                    slot_free(k)
                    sp.dma_start(slot[k % 2], w_mod[l].rearrange("(p k) n -> p k n", k=KO)[:, k, :])\
                        .then_inc(sem(f"w{l}_{k % 2}_loaded"), 16)
                for i, (col, width) in enumerate(IN_LOADS):
                    slot_free(KO + i)
                    s = (KO + i) % 2
                    sp.dma_start(slot[s][:, 0:KO * width].rearrange("p (k n) -> p k n", k=KO),
                                 w_in[l].rearrange("(p k) n -> p k n", k=KO)[:, :, col:col + width])\
                        .then_inc(sem(f"w{l}_{s}_loaded"), 16)
                for half in range(2):
                    slot_free(13 + half)
                    s = (13 + half) % 2
                    sp.dma_start(slot[s][:, 0:4096].rearrange("p (k n) -> p k n", k=KO),
                                 w_out[l].rearrange("(p k) n -> p k n", k=KO)[:, :, half * 512:(half + 1) * 512])\
                        .then_inc(sem(f"w{l}_{s}_loaded"), 16)
                slot_free(15)
                for dst, src in ((slot[1][:, 0:2048], w_sh_gate[l].rearrange("(p k) n -> p (k n)", k=KO)),
                                 (slot[1][:, 2048:4096], w_sh_up[l].rearrange("(p k) n -> p (k n)", k=KO)),
                                 (slot[1][:, 4096:6144], w_sh_down[l].rearrange("(p m) n -> p (m n)", m=2))):
                    sp.dma_start(dst, src).then_inc(sem(f"w{l}_1_loaded"), 16)

                def expert(e, j):
                    for at, w in ((0, w_exp_gate), (2048, w_exp_up)):
                        sp.dma_start(slot[j][:, at:at + 2048], w[l, bass.ds(e, 1)].rearrange("o (p k) n -> p (o k n)", k=KO))\
                            .then_inc(sem(f"we{l}_{j}_loaded"), 16)
                    sp.dma_start(slot[j][:, 4096:6144], w_exp_down[l, bass.ds(e, 1)].rearrange("o (p m) n -> p (o m n)", m=2))\
                        .then_inc(sem(f"we{l}_{j}_loaded"), 16)

                product(sp, ("m", l, 1, nt - 1))
                expert(0, 0)
                sp.wait_ge(sem(f"h2_{l}"), nt)
                expert(2, 2)
                expert(3, 3)
                product(sp, ("sd", l, nt - 1, 1))
                expert(1, 1)
                HAND = NE // NSLOT - 1
                with sp.Fori(1, HAND) as g:
                    for j in range(NSLOT):
                        sp.wait_ge(sem(f"down{l}"), (g - 1) * NSLOT + j + 1)
                        expert(g * NSLOT + j, j)
                sp.wait_ge(sem(f"routed{l}"), 1)
                ng = sp.value_load(ngt[0:1, 0:1], min_val=0, max_val=extra_blocks(nt * P) // NSLOT) + NE // NSLOT
                with sp.Fori(HAND, ng) as g:
                    for j in range(NSLOT):
                        e = sp.value_load(tab[0:1, bass.ds(g * NSLOT + j, 1)], min_val=0, max_val=NE - 1)
                        sp.wait_ge(sem(f"down{l}"), (g - 1) * NSLOT + j + 1)
                        expert(e, j)
                ng_prev = ng
                sp.wait_ge(sem(f"scattered{l}"), ng * NSLOT * 16)
                sp.dma_start(areg[:, 0:nt * D].rearrange("p (t d) -> p t d", t=nt),
                             accd[l][0:nt * P, :].rearrange("(t p) d -> p t d", p=P)).then_inc(sem(f"sums{l}"), 16)
            for t in range(2):
                sp.wait_ge(sem(f"x_done{DEPTH - 1}"), t + 1)
                sp.dma_start(out[0, t * P:(t + 1) * P, :], Xt[:, t, :]).then_inc(sem("stored"), 16)
            sp.wait_ge(sem("stored"), 32)

        @block.scalar
        def _(act):
            A = nc.scalar.activation
            chain = Chain(act, "act_chain")
            boot(act)
            A(cnd.rearrange("p k s -> p s k"), condr[:, :].rearrange("p (s k) -> p s k", s=2), ACT.Silu)\
                .then_inc(sem("cond_done"), 1)
            act.wait_ge(sem("boot_sums"), 1)
            chain(A(small[:, 0:16], small[:, 0:16], ACT.Exp))
            A(small[:, 0:16], small[:, 0:16], ACT.Ln, bias=1.0)
            A(lamt[:, 4:8], lamt[:, 0:4], ACT.Exp).then_inc(sem("boot_exps"), 1)
            act.wait_ge(sem("boot_ready"), 1)
            for l in range(DEPTH):
                nt = nt_of(l)
                ntok = nt * P
                nx = extra_blocks(ntok)

                def copy(out_, in_, key, scale=1.0, func=ACT.Copy):
                    release(A(out_, in_, func, scale=scale), key)

                def root_mean_square(src, junk, s, name):
                    chain(A(junk, src, ACT.Square, accum_out=st[:, s:s + 1]))
                    A(st[:, s + 1:s + 2], st[:, s:s + 1], ACT.Sqrt, scale=1.0 / D, bias=eps[:, 0:1])\
                        .then_inc(sem(name), 1)

                for t in range(TILES):
                    x_ready(act, l, t)
                    root_mean_square(Xt[:, t, :], tmp[:, 2048:3072], 2 * t, f"rms1_{l}")
                ones_at = COFF["ones"][0]
                act.dma_start(glrT[LOWRANK:LOWRANK + 1, :].rearrange("o (n a) -> o n a", a=P),
                              consts[0:1, ones_at:ones_at + P].unsqueeze(1).to_broadcast([1, TILES, P]))\
                    .then_inc(sem(f"ones_row{l}"), 16)
                act.wait_ge(sem(f"modded{l}"), 1)
                for t in range(TILES):
                    s = 0 if t < 2 else 1
                    for half in range(2):
                        key = ("t1", l, t, half)
                        b = product(act, key)
                        for i in range(4):
                            k = half * 4 + i
                            last = A(hT[:, k, t * P:(t + 1) * P], b[:, i * P:(i + 1) * P], ACT.Identity,
                                     scale=mcol[:, SC1, k, s:s + 1], bias=mcol[:, SH1, k, s:s + 1])
                        release(last, key)
                def read_v(i, t):
                    key = ("v", l, i, t)
                    b = product(act, key)
                    A(vv[:, i, t, 0:256], b[:, 0:256], ACT.Copy)
                    copy(vv[:, i, t, 256:512], b[:, 256:512], key, func=ACT.Silu)

                for i in range(2):
                    copy(qk[:, 2 * i, :], product(act, ("qk", l, 2 * i))[:, :], ("qk", l, 2 * i), GLA_SCALE if i else 1.0)
                    copy(qk[:, 2 * i + 1, :], product(act, ("qk", l, 2 * i + 1))[:, :], ("qk", l, 2 * i + 1), 1.0 if i else RET_SCALE)
                    for t in range(TILES):
                        read_v(i, t)
                copy(glrT[0:LOWRANK, :], product(act, ("glr", l))[0:LOWRANK, :], ("glr", l))
                for n in range(4):
                    copy(qk[:, DQ + n, :], product(act, ("qk", l, DQ + n))[:, :], ("qk", l, DQ + n))
                for n in range(4):
                    copy(qk[:, DK + n, :], product(act, ("qk", l, DK + n))[:, :], ("qk", l, DK + n))
                for t in range(TILES):
                    copy(vv[:, 2, t, :], product(act, ("v", l, 2, t))[:, :], ("v", l, 2, t))
                for t in range(TILES):
                    if t >= 2:
                        taken(act, ("z", l, t - 2))
                    a = tmp[:, 1024 + (t % 2) * 512:1280 + (t % 2) * 512]
                    chain(A(a, product(act, ("z", l, t))[:, 0:256], ACT.Abs))
                    chain(A(a, a, ACT.Exp, scale=-1.0))
                    A(a, a, ACT.Ln, bias=1.0).then_inc(sem(f"lnz{l}"), 1)
                NL = len(LEVELS) + 1
                for t in range(TILES):
                    taken(act, ("z", l, t))
                for v in list(range(NL)) + ["x"]:
                    n = NL if v == "x" else v
                    ge(act, sem(f"gla_qk{l}"), n)
                    for p in range(2 if v == "x" else nt // 2):
                        key = ("E", l, v, p)
                        copy(Eb[:, 2 * p:2 * p + 2, :], product(act, key)[:, :].rearrange("p (t a) -> p t a", t=2), key,
                             1.0 / TAU, ACT.Exp)
                for t in range(nt):
                    copy(mix[:, t, 256:512], product(act, ("og", l, t))[:, 0:256], ("og", l, t))
                dist = const("dist")
                act.wait_ge(sem(f"ret_dist{l}"), 1)
                for h in range(4):
                    if h >= 1:
                        act.wait_ge(sem(f"ret_D{l}"), h)
                    lgf, lgb, nlb, c256f, c256b = (retc[:, (l * 5 + a) * 4 + h:(l * 5 + a) * 4 + h + 1] for a in range(5))
                    E4 = tmp[:, 2048:4096].rearrange("p (n a) -> p n a", n=4)
                    A(E4[:, 0, :], tmp[:, 0:512], ACT.Exp, scale=lgf)
                    A(E4[:, 1, :], tmp[:, 512:1024], ACT.Exp, scale=lgb)
                    A(E4[:, 2, :], dist, ACT.Exp, scale=lgf, bias=c256f)
                    A(E4[:, 3, :], dist, ACT.Exp, scale=nlb, bias=c256b).then_inc(sem(f"ret_E{l}"), 1)
                for t in range(nt):
                    copy(mix[:, t, 0:256], product(act, ("or", l, t))[:, 0:256], ("or", l, t))
                units = [(t, h) for t in range(nt) for h in range(4)]

                def exps(u):
                    t, h = units[u]
                    nk = TOK if t < 2 else CTX
                    if u >= 2:
                        product(act, ("wt", l, u - 2))
                    for m in range(2):
                        key = ("ds", l, t, h, m)
                        act.wait_ge(sem(f"diff_max{l}"), u + 1)
                        last = A(tmp[:, (u % 2) * 1024 + m * 512:(u % 2) * 1024 + m * 512 + nk], product(act, key)[:, 0:nk],
                                 ACT.Exp, scale=DIFF_SCALE, bias=st[:, 64 + 8 * u + m:65 + 8 * u + m],
                                 accum_out=st[:, 66 + 8 * u + m:67 + 8 * u + m])
                        release(last, key)

                exps(0)
                for u, (t, h) in enumerate(units):
                    if u + 1 < len(units):
                        exps(u + 1)
                    nk = TOK if t < 2 else CTX
                    key = ("wt", l, u)
                    b = product(act, key)
                    if u >= 2:
                        if units[u - 2][1] == 3:
                            product(act, ("do", l, units[u - 2][0]))
                        else:
                            act.wait_ge(sem(f"diff_o{l}"), 3 * units[u - 2][0] + units[u - 2][1] + 1)
                    copy(tmp[:, 2048 + (u % 2) * 512:2048 + (u % 2) * 512 + nk], b[:, 0:nk], key)
                    if h == 3:
                        copy(mix[:, t, 512:1024], product(act, ("do", l, t))[:, :], ("do", l, t))
                for t in range(nt):
                    taken(act, ("og", l, t))
                    taken(act, ("or", l, t))
                    taken(act, ("do", l, t))
                for t in range(nt):
                    if t >= 2:
                        act.wait_ge(sem(f"head_ss{l}"), t - 1)
                    A(tmp[:, (t % 2) * D:(t % 2 + 1) * D], mix[:, t, :], ACT.Square).then_inc(sem(f"head_sq{l}"), 1)
                for t in range(nt):
                    act.wait_ge(sem(f"head_ss{l}"), t + 1)
                    o = 256 + 32 * t
                    A(st[:, o + 12:o + 20], st[:, o:o + 8], ACT.Sqrt, scale=1.0 / 64, bias=eps[:, 0:1])
                    A(st[:, o + 20:o + 24], st[:, o + 8:o + 12], ACT.Sqrt, scale=1.0 / 128, bias=eps[:, 0:1])\
                        .then_inc(sem(f"head_rms{l}"), 1)
                for t in range(nt):
                    for half in range(2):
                        key = ("t2", l, t, half)
                        copy(mixT[:, half * 4:half * 4 + 4, t * P:(t + 1) * P],
                             product(act, key)[:, :].rearrange("p (k n) -> p k n", k=4), key)

                def read_row(dst, key):
                    for half in range(2):
                        k = key + (half,)
                        copy(dst.rearrange("p (n k) -> p k n", k=KO)[:, half * 4:half * 4 + 4, :],
                             product(act, k)[:, :].rearrange("p (k n) -> p k n", k=4), k)

                for v, j in enumerate((GT1, SC2, SH2)):
                    for s in streams(l):
                        read_row(bc[:, v, s, :], ("bc", l, j, s))
                for half in range(2):
                    for t in range(nt):
                        key = ("m", l, half, t)
                        copy(mix[:, t, half * 512:(half + 1) * 512], product(act, key)[:, :], key)
                for t in range(nt):
                    taken(act, ("m", l, 0, t))
                    taken(act, ("m", l, 1, t))
                    root_mean_square(mix[:, t, :], tmp[:, 3072:4096], 8 + 2 * t, f"rms2_{l}")
                for t in range(nt):
                    act.wait_ge(sem(f"x_mid{l}"), t + 1)
                    root_mean_square(Xt[:, t, :], tmp[:, 3072:4096], 16 + 2 * t, f"rms3_{l}")
                for t in range(nt):
                    for half in range(2):
                        key = ("t3", l, t, half)
                        copy(mixT[:, half * 4:half * 4 + 4, t * P:(t + 1) * P],
                             product(act, key)[:, :].rearrange("p (k n) -> p k n", k=4), key)
                copy(rsc[:, 0:nt * NE], product(act, ("rt", l))[:, 0:nt * NE], ("rt", l), func=ACT.Sigmoid)
                for m in range(2):
                    key = ("sh", l, m, 0)
                    copy(areg[:, 5120 + m * 512:5120 + m * 512 + ntok], product(act, key)[:, 0:ntok], key, func=ACT.Silu)
                for t in range(nt):
                    act.wait_ge(sem(f"h2_stored{l}"), 16 * nt)
                    if t >= 2:
                        act.wait_ge(sem(f"sh_stored{l}_{t % 2}"), 16 * (t // 2))
                    for half in range(2):
                        key = ("sd", l, t, half)
                        copy(tmp[:, (t % 2) * D + half * 512:(t % 2) * D + (half + 1) * 512], product(act, key)[:, :], key)
                    taken(act, ("sd", l, t, 1))
                    act.dma_start(accd[l][t * P:(t + 1) * P, :], tmp[:, (t % 2) * D:(t % 2 + 1) * D])\
                        .then_inc(sem(f"sh_stored{l}_{t % 2}"), 16)
                shared_stored(act, l)
                act.wait_ge(sem(f"routed{l}"), 1)
                ng = act.value_load(ngt[0:1, 0:1], min_val=0, max_val=nx // NSLOT) + NE // NSLOT

                def gate(b, j):
                    act.wait_ge(sem(f"gate_up{l}"), b + 1)
                    ge(act, sem(f"hidden{l}"), b - 1)
                    A(hreg[:, 3328 + (j % 2) * 128:3456 + (j % 2) * 128], bank[2 + j % 2][:, 0:2 * SLOTS], ACT.Silu)\
                        .then_inc(sem(f"gated{l}"), 1)

                def y_out(b, j):
                    ge(act, sem(f"down{l}"), b + 1)
                    ge(act, sem(f"scattered{l}"), (b - 1) * 16)
                    ge(act, sem(f"picked{l}"), 2 * (b + 1))
                    A(tmp[0:SLOTS, (j % 2) * D:(j % 2) * D + 512], bank[4 + 2 * (j % 2)][0:SLOTS, :], ACT.Copy,
                      scale=wb[0:SLOTS, j:j + 1]).then_inc(sem(f"y0_out{l}"), 1)

                def group(g):
                    for j in range(NSLOT):
                        b = g * NSLOT + j
                        gate(b, j)
                        if not (isinstance(b, int) and b == 0):
                            y_out(b - 1, (j - 1) % NSLOT)

                group(0)
                with act.Fori(1, ng) as g:
                    group(g)
                y_out(ng * NSLOT - 1, NSLOT - 1)
                for s in streams(l):
                    read_row(qkreg[:, s * D:(s + 1) * D], ("bc", l, GT2, s))
                act.wait_ge(sem(f"sums{l}"), 16)
                for t in range(nt):
                    root_mean_square(areg[:, t * D:(t + 1) * D], tmp[:, 3072:4096], 24 + 2 * t, f"rms4_{l}")

        @block.vector
        def _(dve):
            V = nc.vector
            TT, TS, STT = V.tensor_tensor, V.tensor_scalar, V.scalar_tensor_tensor
            link = Chain(dve, "dve_chain")

            def total(out_, in_):
                return V.tensor_reduce(out_, in_, AX.X, ALU.add)

            V.memset(eps[:, :], EPS)
            V.memset(areg[0:SLOTS, 0:D], 0.0).then_inc(sem("zeroed"), 1)
            boot(dve)
            V.tensor_copy(mskt[:, :], hreg[:, 0:len(LEVELS) * P])
            STT(small[:, 0:16], retl[:, :], -1.0, retl[:, :], ALU.mult, ALU.min)
            TS(small[:, 16:32], retl[:, :], 0.0, None, ALU.min)
            lp = tmp[:, 0:512].rearrange("p (n two a) -> p n two a", two=2, a=64)
            prod4 = tmp[:, 512:768].rearrange("p (n a) -> p n a", a=64)
            link(TT(prod4, lp[:, :, 0, :], lp[:, :, 1, :], ALU.mult))
            total(lamt[:, 0:4], prod4).then_inc(sem("boot_sums"), 1)
            dve.wait_ge(sem("boot_exps"), 1)
            r5 = retc[:, :].rearrange("p (l a h) -> p l a h", l=DEPTH, a=5)
            zmin = small[:, 16:32].rearrange("p (l a h) -> p l a h", l=DEPTH, a=2)
            lnz = small[:, 0:16].rearrange("p (l a h) -> p l a h", l=DEPTH, a=2)
            e4 = lamt[:, 4:8].rearrange("p (l a) -> p l a", l=DEPTH)
            for l in range(DEPTH):
                TT(lamt[:, 8 + l:9 + l], e4[:, l, 1:2], e4[:, l, 0:1], ALU.subtract)
                TS(diffg[:, l * 128:(l + 1) * 128], diffg[:, l * 128:(l + 1) * 128], 1.0 - lam_init(l), None, ALU.mult)
                link(TT(r5[:, l, 0:2, :], zmin[:, l], lnz[:, l], ALU.subtract))
                TS(lamt[:, 8 + l:9 + l], lamt[:, 8 + l:9 + l], -lam_init(l), None, ALU.add)
                TS(r5[:, l, 2, :], r5[:, l, 1, :], -1.0, None, ALU.mult)
                last = TS(r5[:, l, 3:5, :], r5[:, l, 0:2, :], float(SEQ), None, ALU.mult)
            link(last)
            dve.wait_ge(sem("padded"), 16 * 2 * DEPTH)
            V.tensor_copy(lamt[:, 12:13], lamt[:, 8:9]).then_inc(sem("boot_ready"), 1)

            for l in range(DEPTH):
                nt = nt_of(l)
                ntok = nt * P
                nx = extra_blocks(ntok)
                nbt = NE + nx + NSLOT

                def normalised(t):
                    dve.wait_ge(sem(f"rms1_{l}"), t + 1)
                    link(V.reciprocal(st[:, 32 + t:33 + t], st[:, 2 * t + 1:2 * t + 2]))
                    if t >= 2:
                        product(dve, ("t1", l, t - 2, 1))
                    TS(tmp[:, (t % 2) * D:(t % 2 + 1) * D], Xt[:, t, :], st[:, 32 + t:33 + t], None, ALU.mult)\
                        .then_inc(sem(f"xn1_{l}"), 1)

                normalised(0)
                normalised(1)
                key = ("mod", l)
                b = product(dve, key)
                release(TT(modc[:, :].rearrange("p (n s) -> p n s", s=2), b[:, 0:96].rearrange("p (n s) -> p n s", s=2),
                           vec[:, l, 4:10, :].rearrange("p j k -> p (j k)").unsqueeze(2).to_broadcast([P, 48, 2]), ALU.add), key)
                taken(dve, key)
                for j, g in ((SC1, 0), (GT1, 1), (SC2, 2), (GT2, 3)):
                    gain = vec[:, l, g, :].unsqueeze(2).to_broadcast([P, KO, 2])
                    last = STT(mcol[:, j], mcol[:, j], 1.0 if j in (SC1, SC2) else 0.0, gain, ALU.add, ALU.mult)
                last.then_inc(sem(f"modded{l}"), 1)
                normalised(2)
                normalised(3)
                for i, n in enumerate((RQ, RK, 4, 5, 6, 7, 8, 9, 10, 11)):
                    key = ("rope", l, n)
                    b = product(dve, key)
                    part = tmp[:, 2048 + 256 * (i % 2):2304 + 256 * (i % 2)]
                    c_, s_ = (const("cos_r"), const("sin_r")) if n < 4 else (const("cos_d"), const("sin_d"))
                    release(TT(part, b[:, 0:SEQ], s_, ALU.mult), key)
                    link(TT(qk[:, n, 0:SEQ], qk[:, n, 0:SEQ], c_, ALU.mult))
                    taken(dve, key)
                    TT(qk[:, n, 0:SEQ], qk[:, n, 0:SEQ], part, ALU.add).then_inc(sem(f"roped{l}"), 1)
                for t in range(TILES):
                    key = ("z", l, t)
                    dve.wait_ge(sem(f"lnz{l}"), t + 1)
                    b = product(dve, key)
                    a = 1024 + (t % 2) * 512
                    release(STT(la[:, t, :], b[:, 0:256], 0.0, tmp[:, a:a + 256], ALU.min, ALU.subtract), key)
                for h in range(4):
                    key = ("gs", l, "d", h)
                    b = product(dve, key)
                    release(STT(attd[:, h, 0:nt, :], b[:, 0:ntok].rearrange("p (t a) -> p t a", t=nt), 2.0,
                                ident.unsqueeze(1).to_broadcast([P, nt, P]), ALU.mult, ALU.mult), key)
                NL = len(LEVELS) + 1

                def tiles_of(a):
                    return a.rearrange("p (t a) -> p t a", a=P)

                def decayed(v):
                    for p in range(nt // 2):
                        taken(dve, ("E", l, v, p))
                    buf = QKb[v % 2]
                    TT(tiles_of(buf[:, 0, 0:ntok]), Eb[:, 0:nt, 0:P], tiles_of(qk[:, GQ, 0:ntok]), ALU.mult)
                    TT(tiles_of(buf[:, 1, 0:ntok]), Eb[:, 0:nt, P:2 * P], tiles_of(qk[:, GK, 0:ntok]), ALU.mult)\
                        .then_inc(sem(f"gla_qk{l}"), 1)

                def decayed_across():
                    for p in range(2):
                        taken(dve, ("E", l, "x", p))
                    buf = QKb[NL % 2]
                    for d in range(2):
                        TT(tiles_of(buf[:, 0, d * SEQ:(d + 1) * SEQ]), Eb[:, 0:2, d * P:(d + 1) * P],
                           tiles_of(qk[:, GQ, 0:SEQ]), ALU.mult)
                        last = TT(tiles_of(buf[:, 1, d * SEQ:(d + 1) * SEQ]), Eb[:, 2:4, d * P:(d + 1) * P],
                                  tiles_of(qk[:, GK, SEQ:TOK]), ALU.mult)
                    last.then_inc(sem(f"gla_qk{l}"), 1)

                decayed(0)
                for v in range(NL):
                    if v + 1 < NL:
                        decayed(v + 1)
                    else:
                        decayed_across()
                    for h in range(4):
                        key = ("gs", l, v, h)
                        b = product(dve, key)
                        data = b[:, 0:ntok].rearrange("p (t a) -> p t a", t=nt)
                        if v < NL - 1:
                            taken(dve, ("gs", l, v - 1 if v else "d", h))
                            release(V.copy_predicated(attd[:, h, 0:nt, :],
                                                      masks[:, v, :].unsqueeze(1).to_broadcast([P, nt, P]), data), key)
                        else:
                            release(V.tensor_copy(atto[:, h, 0:nt, :], data), key)
                for h in range(4):
                    key = ("gs", l, "x", h)
                    b = product(dve, key)
                    release(V.tensor_copy(attx[:, h, :, :].rearrange("p t q -> p (t q)"), b[:, :]), key)
                dist = const("dist")
                TS(tmp[:, 0:512], dist, 0.0, None, ALU.max)
                TS(tmp[:, 512:1024], dist, -1.0, 0.0, ALU.mult, ALU.max).then_inc(sem(f"ret_dist{l}"), 1)
                product(dve, ("og", l, nt - 1))
                D4 = tmp[:, 1024:2048].rearrange("p (a n q) -> p a n q", a=2, n=2)
                E4 = tmp[:, 2048:4096].rearrange("p (n a q) -> p n a q", n=4, a=2)
                for h in range(4):
                    dve.wait_ge(sem(f"ret_E{l}"), h + 1)
                    if h:
                        taken(dve, ("rs", l, h - 1, 2))
                        taken(dve, ("rs", l, h - 1, 3))
                    e0, e1 = tmp[:, 2048:2560], tmp[:, 2560:3072]
                    TT(D4[:, :, 0, :], E4[:, 2], E4[:, 3], ALU.add)
                    STT(e0, dist, 0.0, e0, ALU.is_ge, ALU.mult)
                    link(STT(e1, dist, 0.0, e1, ALU.is_le, ALU.mult))
                    link(TT(D4[:, :, 1, :], E4[:, 0], E4[:, 1], ALU.add))
                    V.tensor_copy(lamt[:, 13:14], lamt[:, 8:9]).then_inc(sem(f"ret_D{l}"), 1)
                    for kt in range(TILES):
                        key = ("rs", l, h, kt)
                        b = product(dve, key)
                        if kt < 2:
                            ins = TT(ratt(h, kt), b[:, 0:SEQ], D4[:, kt, 1, :], ALU.mult)
                        else:
                            at = 1024 + (kt - 2) * 512
                            ins = TT(ratt(h, kt)[:, 0:ntok], b[:, 0:ntok], tmp[:, at:at + ntok], ALU.mult)
                        release(ins, key)
                units = [(t, h) for t in range(nt) for h in range(4)]

                def maxima(u):
                    t, h = units[u]
                    nk = TOK if t < 2 else CTX
                    o = 64 + 8 * u
                    for m in range(2):
                        b = product(dve, ("ds", l, t, h, m))
                        last = V.tensor_reduce(st[:, o + 4 + m:o + 5 + m], b[:, 0:nk], AX.X, ALU.max)
                    link(last)
                    TS(st[:, o:o + 2], st[:, o + 4:o + 6], -DIFF_SCALE, None, ALU.mult).then_inc(sem(f"diff_max{l}"), 1)

                maxima(0)
                for u, (t, h) in enumerate(units):
                    if u + 1 < len(units):
                        maxima(u + 1)
                    nk = TOK if t < 2 else CTX
                    o = 64 + 8 * u
                    taken(dve, ("ds", l, t, h, 0))
                    taken(dve, ("ds", l, t, h, 1))
                    link(V.reciprocal(st[:, o + 6:o + 8], st[:, o + 2:o + 4]))
                    link(TS(st[:, o + 7:o + 8], st[:, o + 7:o + 8], lamt[:, 8 + l:9 + l], None, ALU.mult))
                    p0 = tmp[:, (u % 2) * 1024:(u % 2) * 1024 + nk]
                    p1 = tmp[:, (u % 2) * 1024 + 512:(u % 2) * 1024 + 512 + nk]
                    link(TS(p1, p1, st[:, o + 7:o + 8], None, ALU.mult))
                    STT(p0, p0, st[:, o + 6:o + 7], p1, ALU.mult, ALU.add).then_inc(sem(f"diff_w{l}"), 1)
                for t in range(nt):
                    dve.wait_ge(sem(f"head_sq{l}"), t + 1)
                    sq = tmp[:, (t % 2) * D:(t % 2 + 1) * D]
                    o = 256 + 32 * t
                    total(st[:, o:o + 8], sq[:, 0:512].rearrange("p (n a) -> p n a", a=64))
                    total(st[:, o + 8:o + 12], sq[:, 512:1024].rearrange("p (n a) -> p n a", a=128))\
                        .then_inc(sem(f"head_ss{l}"), 1)
                for t in range(nt):
                    o = 256 + 32 * t
                    dve.wait_ge(sem(f"head_rms{l}"), t + 1)
                    link(V.reciprocal(st[:, o + 12:o + 24], st[:, o + 12:o + 24]))
                    m8 = mix[:, t, 0:512].rearrange("p (n a) -> p n a", a=64)
                    m4 = mix[:, t, 512:1024].rearrange("p (n a) -> p n a", a=128)
                    TT(m8, m8, st[:, o + 12:o + 20].unsqueeze(2).to_broadcast([P, 8, 64]), ALU.mult)
                    link(TT(m4, m4, st[:, o + 20:o + 24].unsqueeze(2).to_broadcast([P, 4, 128]), ALU.mult))
                    TT(mix[:, t, 0:256], mix[:, t, 0:256], vv[:, 0, t, 256:512], ALU.mult)
                    link(TT(mix[:, t, 256:512], mix[:, t, 256:512], vv[:, 1, t, 256:512], ALU.mult))
                    g4 = mix[:, t, 256:512].rearrange("p (n a) -> p n a", a=64)
                    TT(g4, g4, glag[:, l * 64:(l + 1) * 64].unsqueeze(1).to_broadcast([P, 4, 64]), ALU.mult)
                    TT(m4, m4, diffg[:, l * 128:(l + 1) * 128].unsqueeze(1).to_broadcast([P, 4, 128]), ALU.mult)\
                        .then_inc(sem(f"mixed{l}"), 1)
                for s in streams(l):
                    for j in (GT1, SC2, SH2):
                        taken(dve, ("bc", l, j, s, 0))
                        taken(dve, ("bc", l, j, s, 1))
                for t in range(nt):
                    s = 0 if t < 2 else 1
                    dve.wait_ge(sem(f"rms2_{l}"), t + 1)
                    link(V.reciprocal(st[:, 32 + t:33 + t], st[:, 9 + 2 * t:10 + 2 * t]))
                    link(STT(mix[:, t, :], mix[:, t, :], st[:, 32 + t:33 + t], bc[:, 0, s, :], ALU.mult, ALU.mult))
                    TT(Xt[:, t, :], Xt[:, t, :], mix[:, t, :], ALU.add).then_inc(sem(f"x_mid{l}"), 1)
                for t in range(nt):
                    s = 0 if t < 2 else 1
                    dve.wait_ge(sem(f"rms3_{l}"), t + 1)
                    link(V.reciprocal(st[:, 36 + t:37 + t], st[:, 17 + 2 * t:18 + 2 * t]))
                    h2 = tmp[:, (t % 2) * D:(t % 2 + 1) * D]
                    if t >= 2:
                        product(dve, ("t3", l, t - 2, 1))
                        dve.wait_ge(sem(f"h2_stored{l}"), 16 * (t - 1))
                    link(STT(h2, Xt[:, t, :], st[:, 36 + t:37 + t], bc[:, 1, s, :], ALU.mult, ALU.mult))
                    TT(h2, h2, bc[:, 2, s, :], ALU.add).then_inc(sem(f"h2_{l}"), 1)

                row = const("row")

                def per(a, w):
                    return a.rearrange("p (t a) -> p t a", a=w)

                sig, msk = per(rsc[:, 0:nt * NE], NE), per(rsc[:, 256:256 + nt * NE], NE)
                sel, sc8 = rsc[:, 512:512 + nt * NE], rsc[:, 768:768 + nt * NE]
                taken(dve, ("rt", l))
                link(TT(per(sel, NE), sig, rbias[:, l * NE:(l + 1) * NE].unsqueeze(1).to_broadcast([P, nt, NE]), ALU.add))
                for n in range(nt * NGRP):
                    last = V.max(sc8[:, n * 8:(n + 1) * 8], sel[:, n * 8:(n + 1) * 8])
                link(last)
                top = sc8.rearrange("p (n a) -> p n a", a=8)
                gs = small[:, 320:320 + nt * 8]
                link(TT(gs.unsqueeze(2), top[:, :, 0:1], top[:, :, 1:2], ALU.add))
                gm = small[:, 352:352 + nt * 8]
                for t in range(nt):
                    last = V.max(gm[:, t * 8:(t + 1) * 8], gs[:, t * 8:(t + 1) * 8])
                link(last)
                for t in range(nt):
                    last = V.max_index(gi8[:, t * 8:(t + 1) * 8], gm[:, t * 8:(t + 1) * 8], gs[:, t * 8:(t + 1) * 8])
                link(last)
                gif = small[:, 384:384 + nt * 8]
                link(V.tensor_copy(gif, gi8[:, 0:nt * 8]))
                eq = hreg[:, 0:nt * 32].rearrange("p (t g k) -> p t g k", g=NGRP, k=TOPG)
                link(TT(eq, row[:, 0:8].unsqueeze(1).unsqueeze(3).to_broadcast([P, nt, 8, TOPG]),
                        per(gif, 8)[:, :, 0:TOPG].unsqueeze(2).to_broadcast([P, nt, 8, TOPG]), ALU.is_equal))
                gmask = small[:, 416:416 + nt * 8]
                link(total(gmask, hreg[:, 0:nt * 32].rearrange("p (n k) -> p n k", k=TOPG)))
                link(TS(gmask, gmask, BIG, -BIG, ALU.mult, ALU.add))
                link(TT(top, sel.rearrange("p (n a) -> p n a", a=8), gmask.unsqueeze(2).to_broadcast([P, nt * 8, 8]), ALU.add))
                em = small[:, 448:448 + nt * 8]
                for t in range(nt):
                    last = V.max(em[:, t * 8:(t + 1) * 8], sc8[:, t * NE:(t + 1) * NE])
                link(last)
                for t in range(nt):
                    last = V.max_index(ei8[:, t * 8:(t + 1) * 8], em[:, t * 8:(t + 1) * 8], sc8[:, t * NE:(t + 1) * NE])
                link(last)
                eif = small[:, 480:480 + nt * 8]
                link(V.tensor_copy(eif, ei8[:, 0:nt * 8]))
                e6 = per(eif, 8)[:, :, 0:TOPK]
                n6 = nt * TOPK
                OH = hreg[:, 0:n6 * NE].rearrange("p (t k e) -> p t k e", k=TOPK, e=NE)
                PR = hreg[:, 1536:1536 + n6 * NE]
                PR4 = PR.rearrange("p (t k e) -> p t k e", k=TOPK, e=NE)
                PR3 = PR.rearrange("p (n e) -> p n e", e=NE)
                full4 = [P, nt, TOPK, NE]
                link(TT(OH, row[:, 0:NE].unsqueeze(1).unsqueeze(1).to_broadcast(full4), e6.unsqueeze(3).to_broadcast(full4), ALU.is_equal))
                total(msk, OH.rearrange("p t k e -> p t e k")).then_inc(sem(f"masked{l}"), 1)
                link(TT(PR4, OH, sig.unsqueeze(2).to_broadcast(full4), ALU.mult))
                w6, rk, xs, q6, lo = (small[:, 512 + 24 * i:512 + 24 * i + n6] for i in range(5))
                link(total(w6, PR3))
                link(total(small[:, 4:4 + nt], per(w6, TOPK)))
                link(V.reciprocal(small[:, 8:8 + nt], small[:, 4:4 + nt]))
                link(STT(per(w6, TOPK), per(w6, TOPK), ROUTED_SCALE, small[:, 8:8 + nt].unsqueeze(2).to_broadcast([P, nt, TOPK]),
                         ALU.mult, ALU.mult))
                for m in range(2):
                    taken(dve, ("sh", l, m, 0))
                    key = ("sh", l, m, 1)
                    b = product(dve, key)
                    ins = TT(areg[:, 4096 + m * 512:4096 + m * 512 + ntok], areg[:, 5120 + m * 512:5120 + m * 512 + ntok],
                             b[:, 0:ntok], ALU.mult)
                    release(ins, key)
                    taken(dve, key)
                    V.tensor_copy(lamt[:, 14:15], lamt[:, 8:9]).then_inc(sem(f"shared_h{l}"), 1)
                b = product(dve, ("rank", l))
                release(TT(PR4, OH, per(b[:, 0:nt * NE], NE).unsqueeze(2).to_broadcast(full4), ALU.mult), ("rank", l))
                taken(dve, ("rank", l))
                link(total(rk, PR3))
                b = product(dve, ("cnt", l))
                release(V.tensor_copy(small[0:NE, 1:2], b[0:NE, 0:1]), ("cnt", l))
                taken(dve, ("cnt", l))
                K = ntok // SLOTS - 1
                link(TS(small[0:NE, 200:200 + K], row[0:NE, 1:1 + K], float(SLOTS), small[0:NE, 1:2], ALU.mult, ALU.is_lt))
                total(small[0:NE, 0:1], small[0:NE, 200:200 + K]).then_inc(sem(f"xcol{l}"), 1)
                b = product(dve, ("xs", l))
                release(TT(PR4, OH, b[:, 0:NE].unsqueeze(1).unsqueeze(1).to_broadcast(full4), ALU.mult), ("xs", l))
                taken(dve, ("xs", l))
                link(total(xs, PR3))
                b = product(dve, ("xe", l))
                release(V.tensor_copy(small[0:NE, 2:3], b[0:NE, 0:1]), ("xe", l))
                taken(dve, ("xe", l))
                TS(small[0:NE, 128:128 + nx], row[0:NE, 0:nx], small[0:NE, 2:3], None, ALU.is_ge).then_inc(sem(f"ended{l}"), 1)
                b = product(dve, ("nx", l))
                release(V.tensor_copy(small[0:1, 3:4], b[0:1, 0:1]), ("nx", l))
                taken(dve, ("nx", l))
                ngr = nx // NSLOT
                link(TS(small[0:1, 232:232 + ngr], row[0:1, 0:ngr], float(NSLOT), small[0:1, 3:4], ALU.mult, ALU.is_lt))
                link(total(small[0:1, 12:13], small[0:1, 232:232 + ngr]))
                V.tensor_copy(ngt[:, :], small[0:1, 12:13])
                b = product(dve, ("be", l))
                release(TS(small[0:1, 256:256 + nx], b[0:1, 0:nx], float(NE - 1), None, ALU.min), ("be", l))
                taken(dve, ("be", l))
                V.tensor_copy(tab[:, NE:NE + nx], small[0:1, 256:256 + nx])
                V.tensor_copy(tab[:, 0:NE], row[0:1, 0:NE])
                link(TS(q6, rk, float(SLOTS), None, ALU.is_ge))
                for j in range(2, K + 1):
                    link(STT(q6, rk, float(SLOTS * j), q6, ALU.is_ge, ALU.add))
                STT(lo, q6, -float(SLOTS), rk, ALU.mult, ALU.add)
                link(TT(xs, xs, q6, ALU.add))
                link(STT(per(xs, TOPK), per(xs, TOPK), float(NE - 1), e6, ALU.add, ALU.subtract))
                link(STT(xs, q6, 0.0, xs, ALU.is_gt, ALU.mult))
                link(TT(per(xs, TOPK), per(xs, TOPK), e6, ALU.add))
                Lh = hreg[:, 1536:1536 + n6 * SLOTS].rearrange("p (n s) -> p n s", s=SLOTS)
                TT(Lh, row[:, 0:SLOTS].unsqueeze(1).to_broadcast([P, n6, SLOTS]), lo.unsqueeze(2).to_broadcast([P, n6, SLOTS]),
                   ALU.is_equal)
                Hh = tmp[:, 2048:2048 + TOPK * 2 * nbt].rearrange("p (k a) -> p k a", k=TOPK)
                for t in range(nt):
                    if t:
                        dve.wait_ge(sem(f"slots_used{l}"), t)
                    shape = [P, TOPK, nbt]
                    link(TT(Hh[:, :, 0:nbt], row[:, 0:nbt].unsqueeze(1).to_broadcast(shape),
                            xs[:, t * TOPK:(t + 1) * TOPK].unsqueeze(2).to_broadcast(shape), ALU.is_equal))
                    link(TT(Hh[:, :, nbt:2 * nbt], Hh[:, :, 0:nbt],
                            w6[:, t * TOPK:(t + 1) * TOPK].unsqueeze(2).to_broadcast(shape), ALU.mult))
                    TS(Hh[:, :, 0:nbt], Hh[:, :, 0:nbt], const("tok1")[:, t:t + 1], None, ALU.mult)\
                        .then_inc(sem(f"onehots{l}"), 1)
                key = ("slot", l)
                b = product(dve, key)
                link(TS(rsc[0:SLOTS, 512:512 + nbt], b[0:SLOTS, 0:nbt], 0.0, const("pad")[0:SLOTS, l:l + 1], ALU.is_equal, ALU.mult))
                link(STT(rsc[0:SLOTS, 640:640 + nbt], b[0:SLOTS, 0:nbt], -1.0, rsc[0:SLOTS, 512:512 + nbt], ALU.add, ALU.add))
                release(V.tensor_copy(wsl[0:SLOTS, 0:nbt], b[0:SLOTS, nbt:2 * nbt]), key)
                V.tensor_copy(idx[0:SLOTS, 0:nbt], rsc[0:SLOTS, 640:640 + nbt]).then_inc(sem(f"routed{l}"), 1)
                dve.wait_ge(sem(f"routed{l}"), 1)
                shared_stored(dve, l)
                ng = dve.value_load(ngt[0:1, 0:1], min_val=0, max_val=nx // NSLOT) + NE // NSLOT

                def copy_T(b, par):
                    ge(dve, sem(f"xT{l}"), b + 1)
                    ge(dve, sem(f"gate_up{l}"), b - 1)
                    V.tensor_copy(hreg[:, 2048 + par * 512:2560 + par * 512], bank[par][:, :]).then_inc(sem(f"xT_copied{l}"), 1)

                def hidden(b, j):
                    ge(dve, sem(f"gated{l}"), b + 1)
                    ge(dve, sem(f"down{l}"), b - 1)
                    TT(hreg[:, 3072 + (j % 2) * 128:3200 + (j % 2) * 128], hreg[:, 3328 + (j % 2) * 128:3456 + (j % 2) * 128],
                       bank[2 + j % 2][:, 2 * SLOTS:4 * SLOTS], ALU.mult).then_inc(sem(f"hidden{l}"), 1)

                def y_out(b, j):
                    ge(dve, sem(f"down{l}"), b + 1)
                    ge(dve, sem(f"scattered{l}"), (b - 1) * 16)
                    ge(dve, sem(f"picked{l}"), 2 * (b + 1))
                    TS(tmp[0:SLOTS, (j % 2) * D + 512:(j % 2 + 1) * D], bank[5 + 2 * (j % 2)][0:SLOTS, :],
                       wb[0:SLOTS, j:j + 1], None, ALU.mult).then_inc(sem(f"y1_out{l}"), 1)

                def group(g):
                    for j in range(NSLOT):
                        b = g * NSLOT + j
                        copy_T(b + 1, (j + 1) % 2)
                        hidden(b, j)
                        if not (isinstance(b, int) and b == 0):
                            y_out(b - 1, (j - 1) % NSLOT)

                copy_T(0, 0)
                group(0)
                with dve.Fori(1, ng) as g:
                    group(g)
                y_out(ng * NSLOT - 1, NSLOT - 1)
                for s in streams(l):
                    taken(dve, ("bc", l, GT2, s, 0))
                    taken(dve, ("bc", l, GT2, s, 1))
                for t in range(nt):
                    s = 0 if t < 2 else 1
                    dve.wait_ge(sem(f"rms4_{l}"), t + 1)
                    link(V.reciprocal(st[:, 40 + t:41 + t], st[:, 25 + 2 * t:26 + 2 * t]))
                    f = areg[:, t * D:(t + 1) * D]
                    link(STT(f, f, st[:, 40 + t:41 + t], qkreg[:, s * D:(s + 1) * D], ALU.mult, ALU.mult))
                    TT(Xt[:, t, :], Xt[:, t, :], f, ALU.add).then_inc(sem(f"x_done{l}"), 1)

        @block.gpsimd
        def _(pool):
            G = nc.gpsimd
            pool.wait_ge(sem("zeroed"), 1)
            for l in range(DEPTH):
                n = nt_of(l) * P
                for dst in (h2d[l], accd[l]):
                    pool.dma_start(dst[n:n + SLOTS, :], areg[0:SLOTS, 0:D]).then_inc(sem("padded"), 16)
            pool.wait_ge(sem("padded"), 16 * 2 * DEPTH)
            for l in range(DEPTH):
                nt = nt_of(l)
                nx = extra_blocks(nt * P)
                for t in range(nt):
                    pool.wait_ge(sem(f"h2_{l}"), t + 1)
                    pool.dma_start(h2d[l][t * P:(t + 1) * P, :], tmp[:, (t % 2) * D:(t % 2 + 1) * D])\
                        .then_inc(sem(f"h2_stored{l}"), 16)
                    pool.wait_ge(sem(f"h2_stored{l}"), 16 * (t + 1))
                pool.wait_ge(sem(f"routed{l}"), 1)
                ng = pool.value_load(ngt[0:1, 0:1], min_val=0, max_val=nx // NSLOT) + NE // NSLOT

                def waited():
                    pool.sem_inc(sem(f"turns{l}"), 1)

                def gather(b, j):
                    G.tensor_copy(wb[0:SLOTS, j:j + 1], wsl[0:SLOTS, bass.ds(b, 1)]).then_inc(sem(f"picked{l}"), 1)
                    G.tensor_copy(idxb[0:SLOTS, j:j + 1], idx[0:SLOTS, bass.ds(b, 1)]).then_inc(sem(f"picked{l}"), 1)
                    ge(pool, sem(f"picked{l}"), 2 * (b + 1))
                    ge(pool, sem(f"xT{l}"), b - 1)
                    waited()
                    par = j % 2
                    G.indirect_dma_start(hreg[0:SLOTS, par * D:(par + 1) * D], None, h2d[l],
                                         bass.IndirectOffsetOnAxis(ap=idxb[0:SLOTS, j:j + 1], axis=0))\
                        .then_inc(sem(f"gathered{l}_{par}"), 16)

                def scatter(b, j):
                    ge(pool, sem(f"y0_out{l}"), b + 1)
                    ge(pool, sem(f"y1_out{l}"), b + 1)
                    ge(pool, sem(f"scattered{l}"), b * 16)
                    waited()
                    par = j % 2
                    G.indirect_dma_start(accd[l], bass.IndirectOffsetOnAxis(ap=idxb[0:SLOTS, j:j + 1], axis=0),
                                         tmp[0:SLOTS, par * D:(par + 1) * D], None, compute_op=ALU.add)\
                        .then_inc(sem(f"scattered{l}"), 16)

                def group(g):
                    for j in range(NSLOT):
                        b = g * NSLOT + j
                        gather(b + 1, (j + 1) % NSLOT)
                        if not (isinstance(b, int) and b == 0):
                            scatter(b - 1, (j - 1) % NSLOT)

                gather(0, 0)
                shared_stored(pool, l)
                group(0)
                with pool.Fori(1, ng) as g:
                    group(g)
                scatter(ng * NSLOT - 1, NSLOT - 1)


_INS = ['x', 'c', 'ctx', 'c_ctx', 'w_mod', 'b_mod', 'g_pre_mix', 'g_post_mix', 'g_pre_ffn', 'g_post_ffn', 'w_in',
        'w_out', 'ret_decay_logit', 'gla_w_gate', 'gla_b_gate', 'gla_norm_g', 'diff_lambda', 'diff_norm_g',
        'w_router', 'router_bias', 'w_exp_gate', 'w_exp_up', 'w_exp_down', 'w_sh_gate', 'w_sh_up', 'w_sh_down']


def kernel(**inputs):
    import concourse.bacc as bacc
    from concourse.bass_utils import run_bass_kernel_spmd

    nc = bacc.Bacc("TRN2", target_bir_lowering=False, num_devices=1)
    arrays = {name: np.ascontiguousarray(inputs[name]) for name in _INS}
    arrays["shape_tables"] = np.ascontiguousarray(np.concatenate(list(CONSTS.values()), axis=1))
    arrays["level_masks"] = MASKS
    args = [nc.dram_tensor(f"in_{n}", a.shape, mybir.dt.from_np(a.dtype), kind="ExternalInput").ap()
            for n, a in arrays.items()]
    out = nc.dram_tensor("out", (1, SEQ, D), mybir.dt.float32, kind="ExternalOutput").ap()
    hybrid_block(nc, *args, out)
    r = run_bass_kernel_spmd(nc, [{f"in_{n}": a for n, a in arrays.items()}], core_ids=[0])
    return r.results[0]["out"]
```

```python
import math
from contextlib import ExitStack

import numpy as np
import concourse.bass as bass
from concourse import mybir

D = 1024
P = 128
KO = D // P
DEPTH = 2
SEQ = 256
CTX = 256
TOK = SEQ + CTX
TILES = TOK // P
GRID_W = 64
N_IN = 3088
NE = 64
TOPK = 6
NGRP = 8
TOPG = 4
DE = 256
LOWRANK = 16
SLOTS = 64
SLOTW = 3 * KO * DE
NSLOT = 4
EPS = 1e-6
LEVELS = (64, 32, 16, 8, 4, 2, 1)
RET_SCALE = 32 ** -0.5
GLA_SCALE = 32 ** -0.5
DIFF_SCALE = 64 ** -0.5
TAU = 16.0
ROUTED_SCALE = 2.5
IN_LOADS = ((0, 768), (768, 768), (1536, 528), (2064, 512), (2576, 512))
BIG = 1e30
ROUND = 2.0 ** 23


def lam_init(layer):
    return 0.8 - 0.6 * math.exp(-0.3 * layer)


def extra_blocks(tokens):
    n = tokens * TOPK // SLOTS
    return (n + NSLOT - 1) // NSLOT * NSLOT


def shape_constants():
    f = np.float32
    c = {}
    i = np.arange(P)
    c["ident"] = np.eye(P, dtype=f)

    def rope(dh):
        quarter, half = dh // 4, dh // 2
        dd = i % dh
        which, w = dd // half, dd % half
        freqs = (f(10000.0) ** (-np.arange(quarter, dtype=f) / f(quarter))).astype(f)
        t = np.arange(SEQ)
        pos = np.stack([(t // GRID_W).astype(f), (t % GRID_W).astype(f)])
        ang = (pos[which] * freqs[w % quarter][:, None]).astype(f)
        perm = np.zeros((P, P), f)
        first = w < quarter
        for m in range(P):
            if first[m]:
                perm[m + quarter, m] = -1.0
            else:
                perm[m - quarter, m] = 1.0
        return perm, np.cos(ang).astype(f), np.sin(ang).astype(f)

    c["perm_r"], c["cos_r"], c["sin_r"] = rope(32)
    c["perm_d"], c["cos_d"], c["sin_d"] = rope(64)
    t, j = i[:, None], i[None, :]
    c["inc_f"] = (t <= j).astype(f)
    c["exc_f"] = (t > j).astype(f)
    c["inc_b"] = (t >= j).astype(f)
    c["exc_b"] = (t < j).astype(f)
    c["ones"] = np.ones((P, P), f)
    lev, masks = [], []
    for s in LEVELS:
        blk_t, blk_j = t // (2 * s), j // (2 * s)
        same = blk_t == blk_j
        mid = blk_j * 2 * s + s
        second = (j % (2 * s)) >= s
        qf = same & second & (t >= mid) & (t <= j)
        kf = same & ~second & (t > j) & (t < mid)
        qb = same & ~second & (t >= j) & (t < mid)
        kb = same & second & (t >= mid) & (t < j)
        lev += [qf, kf, qb, kb]
        masks.append(same & ((t % (2 * s) >= s) != second))
    c["levels"] = np.concatenate(lev, 1).astype(f)
    q = np.arange(SEQ)[None, None, :]
    k = (np.arange(2)[None, :, None] * P + i[:, None, None])
    c["dist"] = (q - k).reshape(P, 2 * SEQ).astype(f)
    c["row"] = np.broadcast_to(np.arange(P, dtype=f), (P, P))
    c["tok1"] = (np.arange(TILES)[None, :] * P + i[:, None] + 1).astype(f)
    return c, np.concatenate(masks, 1).astype(f)


CONSTS, MASKS = shape_constants()
COFF, _at = {}, 0
for _k, _v in CONSTS.items():
    COFF[_k] = (_at, _v.shape[1])
    _at += _v.shape[1]
CWIDTH = _at


def hybrid_block(nc, x, c, ctx, c_ctx, w_mod, b_mod, g_pre_mix, g_post_mix, g_pre_ffn, g_post_ffn,
                 w_in, w_out, ret_decay_logit, gla_w_gate, gla_b_gate, gla_norm_g, diff_lambda,
                 diff_norm_g, w_router, router_bias, w_exp_gate, w_exp_up, w_exp_down,
                 w_sh_gate, w_sh_up, w_sh_down, consts, level_masks, out):
    f32, u32, i32 = mybir.dt.float32, mybir.dt.uint32, mybir.dt.int32
    ALU, ACT, AX = mybir.AluOpType, mybir.ActivationFunctionType, mybir.AxisListType
    stack = ExitStack()
    sems = {}

    def sem(name):
        if name not in sems:
            sems[name] = stack.enter_context(nc.semaphore(name))
        return sems[name]

    def sb(name, width, dt=f32, parts=P):
        return stack.enter_context(nc.sbuf_tensor(name, [parts, width], dt))

    def nt_of(l):
        return TILES if l < DEPTH - 1 else 2

    with stack:
        X = sb("X", TILES * D)
        hreg = sb("hreg", TILES * D)
        wreg = sb("wreg", 2 * SLOTW)
        qkreg = sb("qkreg", SLOTW)
        vreg = sb("vreg", SLOTW)
        areg = sb("areg", SLOTW)
        tmp = sb("tmp", 4096)
        cst = sb("cst", CWIDTH)
        vecs = sb("vecs", DEPTH * (4 * KO + 6 * KO))
        wrt = sb("wrt", DEPTH * KO * NE)
        rbias = sb("rbias", DEPTH * NE)
        glaw = sb("glaw", DEPTH * 2 * P, parts=LOWRANK + 1)
        glab = glaw[LOWRANK:LOWRANK + 1, :]
        glag = sb("glag", DEPTH * 64)
        diffg = sb("diffg", DEPTH * 128)
        retl = sb("retl", DEPTH * 8)
        lamt = sb("lamt", DEPTH * 8)
        cond = sb("cond", KO * 32)
        condr = sb("condr", KO * 2)
        modc = sb("modc", DEPTH * 6 * KO * 2)
        mskt = sb("mskt", len(LEVELS) * P, mybir.dt.uint8)
        retc = sb("retc", DEPTH * 5 * 4)
        st = sb("st", 384)
        glrT = areg[0:LOWRANK + 1, 6144 - TOK:6144]
        rsc = hreg[:, 3072:4096]
        small = tmp[:, 3448:4096]
        idx = sb("idx", (NE + extra_blocks(TOK) + NSLOT) // 2, u32)
        idxb = sb("idxb", 2, u32)
        back = sb("back", TILES * TOPK, u32)
        ei8 = sb("ei8", TILES * 8, u32)
        gi8 = sb("gi8", TILES * 8, u32)
        tab = sb("tab", NE + extra_blocks(TOK), i32, parts=1)
        ngt = sb("ngt", 1, i32, parts=1)
        eps = sb("eps", 1)
        bank = [stack.enter_context(nc.psum_tensor(f"bank{i}", [P, 512], f32)) for i in range(8)]

        def const(name, parts=P):
            at, w = COFF[name]
            return cst[0:parts, at:at + w]

        ident = const("ident")
        h2d = [nc.dram_tensor(f"h2_rows{l}", (nt_of(l) * P, D), f32).ap() for l in range(DEPTH)]
        yd = [nc.dram_tensor(f"expert_rows{l}", ((NE + extra_blocks(nt_of(l) * P)) * SLOTS, D), f32).ap()
              for l in range(DEPTH)]
        xgb = [hreg[:, i * D:(i + 1) * D] for i in range(2)]
        xTb = [hreg[:, (2 + i) * D:(3 + i) * D] for i in range(2)]
        yb = [tmp[:, i * 512:(i + 1) * 512] for i in range(NSLOT)]
        silub, hidb, hidTb = ([tmp[:, at + i * P:at + (i + 1) * P] for i in range(2)] for at in (2048, 2304, 2560))
        NBACK = 8
        backb = [(vreg[:, i * D:(i + 1) * D] if i < 6 else qkreg[:, (i - 4) * D:(i - 3) * D]) for i in range(NBACK)]

        Xt = X[:, :].rearrange("p (t d) -> p t d", t=TILES)
        hT = hreg[:, :].rearrange("p (k t) -> p k t", k=KO)
        mix = hreg[:, :].rearrange("p (t d) -> p t d", t=TILES)
        mixT = areg[:, 0:TILES * D].rearrange("p (k t) -> p k t", k=KO)
        slot = [wreg[:, 0:SLOTW], wreg[:, SLOTW:2 * SLOTW], qkreg[:, :], vreg[:, :]]
        qk = qkreg[:, :].rearrange("p (n t) -> p n t", t=TOK)
        RQ, RK, GQ, GK, DQ, DK = 0, 1, 2, 3, 4, 8
        vv = vreg[:, :].rearrange("p (n t w) -> p n t w", n=3, w=512)
        bc = qkreg[:, :].rearrange("p (v s d) -> p v s d", v=3, d=D)
        vec = vecs[:, :].rearrange("p (l n k) -> p l n k", l=DEPTH, k=KO)
        mods = modc[:, :].rearrange("p (l j k s) -> p l j k s", l=DEPTH, j=6, s=2)
        modb = [tmp[:, 3072 + i * P:3072 + (i + 1) * P] for i in range(2)]
        SH1, SC1, GT1, SH2, SC2, GT2 = range(6)
        wr = wrt[:, :].rearrange("p (l k e) -> p l k e", l=DEPTH, e=NE)
        cnd = cond[:, :].rearrange("p (k s) -> p k s", s=32)
        la = tmp[:, 0:1024].rearrange("p (t a) -> p t a", t=TILES)
        Eb = tmp[:, 1024:2048].rearrange("p (t a) -> p t a", t=TILES)
        QKb = [tmp[:, 2048 + 1024 * i:3072 + 1024 * i].rearrange("p (a t) -> p a t", a=2) for i in range(2)]
        attd = areg[:, 0:2048].rearrange("p (h t q) -> p h t q", h=4, q=P)
        atto = areg[:, 2048:4096].rearrange("p (h t q) -> p h t q", h=4, q=P)
        attx = areg[:, 4096:6144].rearrange("p (h t q) -> p h t q", h=4, q=SEQ)

        def ratt(h, kt):
            a = h * 1536
            return areg[:, a + kt * 256:a + kt * 256 + 256] if kt < 2 else \
                areg[:, a + 512 + (kt - 2) * 512:a + 1024 + (kt - 2) * 512]

        levels = const("levels").rearrange("p (v a) -> p v a", a=512)
        masks = mskt[:, :].rearrange("p (v a) -> p v a", a=P)

        full = [sem(f"bank{i}_full") for i in range(8)]
        free = [sem(f"bank{i}_free") for i in range(8)]
        uses, where, turn = [0] * 8, {}, {"g": 0, "l": 0, "m": 0}
        pools = {"g": (0, 1, 2, 3, 4, 5), "l": (6,), "m": (7,)}

        def bank_of(pe, key, pool="g"):
            b = pools[pool][turn[pool] % len(pools[pool])]
            turn[pool] += 1
            where[key] = (b, uses[b])
            if uses[b]:
                pe.wait_ge(free[b], uses[b])
            uses[b] += 1
            return bank[b]

        def done(ins, key):
            ins.then_inc(full[where[key][0]], 1)

        def product(eng, key):
            b, n = where[key]
            eng.wait_ge(full[b], n + 1)
            return bank[b]

        def release(ins, key):
            ins.then_inc(free[where[key][0]], 1)

        def taken(eng, key):
            b, n = where[key]
            eng.wait_ge(free[b], n + 1)

        def ge(eng, s, v):
            if not (isinstance(v, int) and v <= 0):
                eng.wait_ge(s, v)

        class Chain:
            def __init__(self, eng, name):
                self.eng, self.s, self.n = eng, sem(name), 0

            def __call__(self, ins):
                self.n += 1
                ins.then_inc(self.s, 1)
                self.eng.wait_ge(self.s, self.n)

            def mark(self, ins):
                self.n += 1
                ins.then_inc(self.s, 1)

            def wait(self):
                if self.n:
                    self.eng.wait_ge(self.s, self.n)

        BOOT_LOADS = 26
        def boot(eng):
            eng.wait_ge(sem("boot_loaded"), 16 * BOOT_LOADS)

        def static_loads(l):
            return [("mod", n, i) for n in ([0] if l == 0 else []) for i in range(12)] + \
                [("in", l, i) for i in range(len(IN_LOADS))] + \
                [("mod", n, i) for n in range(l + 1, min(l + 2, DEPTH)) for i in range(12)] + \
                [("out", l, 0), ("out", l, 1), ("sh", l, 0)]

        def loaded(eng, l, item):
            loads = static_loads(l)
            n = loads.index(item)
            dmas = sum(3 if loads[m][0] == "sh" else 1 for m in range(n % 2, n + 1, 2))
            eng.wait_ge(sem(f"w{l}_{n % 2}_loaded"), 16 * dmas)
            return slot[n % 2]

        def last_use(item):
            kind, l, i = item
            if kind == "mod":
                return "modp", l, i
            if kind == "in":
                return (("v", l, 0, 3), ("v", l, 1, 3), ("qk", l, DQ + 3), ("qk", l, DK + 3), ("v", l, 2, 3))[i]
            return "m", l, i, nt_of(l) - 1

        block = stack.enter_context(nc.Block())

        def streams(l):
            return (0, 1) if l < DEPTH - 1 else (0,)

        def x_ready(eng, l, t):
            if l == 0:
                boot(eng)
            else:
                eng.wait_ge(sem(f"x_done{l - 1}"), t + 1)

        @block.tensor
        def _(pe):
            mm, tr = nc.tensor.matmul, nc.tensor.transpose
            pe.wait_ge(sem("cond_done"), 1)
            for l in range(DEPTH):
                nt = nt_of(l)
                ntok = nt * P
                mcol = mods[:, l]

                def mod_rows(at, n, i):
                    b = bank_of(pe, ("modp", n, i), "g" if n == 0 else "m")
                    w = loaded(pe, at, ("mod", n, i))[:, 0:4096].rearrange("p (k n c) -> p k c n", k=KO, c=KO)
                    for k in range(KO):
                        for g in range(4):
                            last = mm(b[32 * g:32 * g + 32, 0:P].rearrange("p (a n) -> p a n", a=2), cnd[:, k, :],
                                      w[:, k, 2 * g:2 * g + 2, :], start=(k == 0), stop=(k == KO - 1))
                    done(last, ("modp", n, i))

                def mod_turned(n, i):
                    taken(pe, ("modp", n, i))
                    b = bank_of(pe, ("modt", n, i))
                    r = slice(i % 2 * 64, i % 2 * 64 + 64)
                    pick = ident.rearrange("p (g r) -> p g r", r=32)[:, :, 0:2]
                    for a in range(2):
                        last = mm(b[r, a * 8:(a + 1) * 8].rearrange("p (g s) -> p g s", s=2), modb[i % 2][:, a * 64:(a + 1) * 64],
                                  pick, start=True, stop=True)
                    done(last, ("modt", n, i))

                if l == 0:
                    for i in range(12):
                        mod_rows(0, 0, i)
                        if i == 0:
                            boot(pe)
                        else:
                            mod_turned(0, i - 1)
                    mod_turned(0, 11)

                for t in range(TILES):
                    pe.wait_ge(sem(f"xn1_{l}"), t + 1)
                    for half in range(2):
                        b = bank_of(pe, ("t1", l, t, half))
                        xn = tmp[:, (t % 2) * D:(t % 2 + 1) * D].rearrange("p (n k) -> p n k", k=KO)
                        for i in range(4):
                            last = tr(b[:, i * P:(i + 1) * P], xn[:, :, half * 4 + i], ident)
                        done(last, ("t1", l, t, half))

                for t in range(TILES):
                    taken(pe, ("t1", l, t, 0))
                    taken(pe, ("t1", l, t, 1))

                def project_T(w, col, n, key, cols=TOK):
                    b = bank_of(pe, key)
                    for k in range(KO):
                        last = mm(b[0:n, 0:cols], w[:, k, col:col + n], hT[:, k, 0:cols], start=(k == 0), stop=(k == KO - 1))
                    done(last, key)

                def project(w, col, t, key, cols=512):
                    b = bank_of(pe, key)
                    for k in range(KO):
                        last = mm(b[:, 0:cols], hT[:, k, t * P:(t + 1) * P], w[:, k, col:col + cols],
                                  start=(k == 0), stop=(k == KO - 1))
                    done(last, key)

                def rope(n):
                    taken(pe, ("qk", l, n))
                    b = bank_of(pe, ("rope", l, n))
                    done(mm(b[:, 0:SEQ], const("perm_r" if n < 4 else "perm_d"), qk[:, n, 0:SEQ],
                            start=True, stop=True), ("rope", l, n))

                for i, (_, width) in enumerate(IN_LOADS):
                    w = loaded(pe, l, ("in", l, i))[:, 0:KO * width].rearrange("p (k n) -> p k n", k=KO)
                    if i < 2:
                        project_T(w, 0, P, ("qk", l, 2 * i), ntok)
                        project_T(w, P, P, ("qk", l, 2 * i + 1))
                        for t in range(TILES):
                            project(w, 2 * P, t, ("v", l, i, t), 512 if t < nt else 256)
                        if i == 0:
                            rope(RQ)
                            rope(RK)
                    elif i == 2:
                        project_T(w, 0, LOWRANK, ("glr", l))
                        for h in range(4):
                            project_T(w, LOWRANK + h * P, P, ("qk", l, DQ + h), ntok)
                        for h in range(4):
                            rope(DQ + h)
                    elif i == 3:
                        for h in range(4):
                            project_T(w, h * P, P, ("qk", l, DK + h))
                        for h in range(4):
                            rope(DK + h)
                    else:
                        for t in range(TILES):
                            project(w, 0, t, ("v", l, 2, t))

                taken(pe, ("glr", l))
                pe.wait_ge(sem(f"ones_row{l}"), 16)
                for t in range(TILES):
                    b = bank_of(pe, ("z", l, t))
                    done(mm(b[:, 0:256], glrT[:, t * P:(t + 1) * P], glaw[:, l * 256:(l + 1) * 256], start=True, stop=True),
                         ("z", l, t))

                def gla_scores(v, q_of, k_of, tiles):
                    bs = [bank_of(pe, ("gs", l, v, h)) for h in range(4)]
                    for t in range(nt):
                        for h in range(4):
                            r = slice(32 * h, 32 * h + 32)
                            last = mm(bs[h][:, t * P:(t + 1) * P], k_of(r, t), q_of(r, tiles[t]), start=True, stop=True)
                            if t == nt - 1:
                                done(last, ("gs", l, v, h))

                own = list(range(4))
                other = [1, 0, 3, 2]
                taken(pe, ("qk", l, GQ))
                taken(pe, ("qk", l, GK))
                gla_scores("d", lambda r, t: qk[r, GQ, t * P:(t + 1) * P], lambda r, t: qk[r, GK, t * P:(t + 1) * P], own)
                for t in range(TILES):
                    taken(pe, ("z", l, t))

                def decays(v):
                    for p in range(nt // 2):
                        b = bank_of(pe, ("E", l, v, p))
                        for i in range(2):
                            t = 2 * p + i
                            af, ab = la[:, t, 0:P], la[:, t, P:2 * P]
                            o = b[:, i * 256:(i + 1) * 256]
                            if v < len(LEVELS):
                                mm(o, af, levels[:, v, 0:256], start=True, stop=False)
                                last = mm(o, ab, levels[:, v, 256:512], start=False, stop=True)
                            elif i == 0:
                                mm(o[:, 0:P], ab, const("inc_b"), start=True, stop=True)
                                last = mm(o[:, P:256], af, const("exc_f"), start=True, stop=True)
                            else:
                                mm(o[:, 0:P], af, const("inc_f"), start=True, stop=True)
                                last = mm(o[:, P:256], ab, const("exc_b"), start=True, stop=True)
                        done(last, ("E", l, v, p))

                NL = len(LEVELS) + 1
                decays(0)
                for v in range(NL):
                    if v + 1 < NL:
                        decays(v + 1)
                    pe.wait_ge(sem(f"gla_qk{l}"), v + 1)
                    buf = QKb[v % 2]
                    gla_scores(v, lambda r, t: buf[r, 0, t * P:(t + 1) * P],
                               lambda r, t: buf[r, 1, t * P:(t + 1) * P], own if v < NL - 1 else other)
                for p in range(2):
                    b = bank_of(pe, ("E", l, "x", p))
                    sides = (("inc_f", "inc_b"), ("exc_f", "exc_b"))[p]
                    for i in range(2):
                        t = 2 * p + i
                        between = ((None, 1), (0, None))[i] if p == 0 else ((3, None), (None, 2))[i]
                        for d in range(2):
                            o = b[:, i * 256 + d * P:i * 256 + (d + 1) * P]
                            whole = between[d]
                            last = mm(o, la[:, t, d * P:(d + 1) * P], const(sides[d]), start=True, stop=whole is None)
                            if whole is not None:
                                last = mm(o, la[:, whole, d * P:(d + 1) * P], const("ones"), start=False, stop=True)
                    done(last, ("E", l, "x", p))
                pe.wait_ge(sem(f"gla_qk{l}"), NL + 1)
                buf = QKb[NL % 2]
                bs = [bank_of(pe, ("gs", l, "x", h)) for h in range(4)]
                for kt in range(2):
                    for d in range(2):
                        for h in range(4):
                            r = slice(32 * h, 32 * h + 32)
                            last = mm(bs[h][:, kt * SEQ:(kt + 1) * SEQ], buf[r, 1, d * SEQ + kt * P:d * SEQ + (kt + 1) * P],
                                      buf[r, 0, d * SEQ:(d + 1) * SEQ], start=(d == 0), stop=(d == 1))
                            if kt == 1 and d == 1:
                                done(last, ("gs", l, "x", h))
                for h in range(4):
                    taken(pe, ("gs", l, NL - 2, h))
                    taken(pe, ("gs", l, NL - 1, h))
                    taken(pe, ("gs", l, "x", h))
                for t in range(TILES):
                    taken(pe, ("v", l, 1, t))
                for t in range(nt):
                    b = bank_of(pe, ("og", l, t))
                    for h in range(4):
                        terms = [(attd[:, h, t, :], t), (atto[:, h, t ^ 1, :], t ^ 1)]
                        if t < 2:
                            terms += [(attx[:, h, kt, t * P:(t + 1) * P], 2 + kt) for kt in range(2)]
                        for n, (a, kt) in enumerate(terms):
                            last = mm(b[:, h * 64:(h + 1) * 64], a, vv[:, 1, kt, h * 64:(h + 1) * 64],
                                      start=(n == 0), stop=(n == len(terms) - 1))
                    done(last, ("og", l, t))

                pe.wait_ge(sem(f"roped{l}"), 2)
                for h in range(4):
                    r = slice(32 * h, 32 * h + 32)
                    for kt in range(TILES):
                        b = bank_of(pe, ("rs", l, h, kt))
                        n = SEQ if kt < 2 else ntok
                        done(mm(b[:, 0:n], qk[r, RK, kt * P:(kt + 1) * P], qk[r, RQ, 0:n], start=True, stop=True),
                             ("rs", l, h, kt))
                for t in range(TILES):
                    taken(pe, ("v", l, 0, t))
                    for h in range(4):
                        taken(pe, ("rs", l, h, t))
                for t in range(nt):
                    b = bank_of(pe, ("or", l, t))
                    for h in range(4):
                        kts = (0, 1, 2, 3) if t < 2 else (2, 3)
                        for n, kt in enumerate(kts):
                            last = mm(b[:, h * 64:(h + 1) * 64], ratt(h, kt)[:, t * P:(t + 1) * P],
                                      vv[:, 0, kt, h * 64:(h + 1) * 64], start=(n == 0), stop=(n == len(kts) - 1))
                    done(last, ("or", l, t))

                pe.wait_ge(sem(f"roped{l}"), 10)
                units = [(t, h) for t in range(nt) for h in range(4)]

                def diff_scores(t, h):
                    k0 = 0 if t < 2 else SEQ
                    for m in range(2):
                        b = bank_of(pe, ("ds", l, t, h, m))
                        r = slice(64 * m, 64 * m + 64)
                        done(mm(b[:, 0:TOK - k0], qk[r, DQ + h, t * P:(t + 1) * P], qk[r, DK + h, k0:TOK],
                                start=True, stop=True), ("ds", l, t, h, m))

                def diff_out(u):
                    t, h = units[u]
                    kts = (0, 1, 2, 3) if t < 2 else (2, 3)
                    if h == 0:
                        bank_of(pe, ("do", l, t), "l")
                    ob = bank[where[("do", l, t)][0]]
                    taken(pe, ("wt", l, u))
                    WT = tmp[:, 2048 + (u % 2) * 512:2560 + (u % 2) * 512]
                    for n, kt in enumerate(kts):
                        last = mm(ob[:, h * P:(h + 1) * P], WT[:, n * P:(n + 1) * P], vv[:, 2, kt, h * P:(h + 1) * P],
                                  start=(n == 0), stop=(n == len(kts) - 1))
                    if h == 3:
                        done(last, ("do", l, t))
                    else:
                        last.then_inc(sem(f"diff_o{l}"), 1)

                diff_scores(*units[0])
                diff_scores(*units[1])
                for t in range(TILES):
                    taken(pe, ("v", l, 2, t))
                for u, (t, h) in enumerate(units):
                    kts = (0, 1, 2, 3) if t < 2 else (2, 3)
                    if u + 2 < len(units):
                        diff_scores(*units[u + 2])
                    pe.wait_ge(sem(f"diff_w{l}"), u + 1)
                    b = bank_of(pe, ("wt", l, u))
                    for n in range(len(kts)):
                        last = tr(b[:, n * P:(n + 1) * P], tmp[:, (u % 2) * 1024:(u % 2) * 1024 + 512][:, n * P:(n + 1) * P], ident)
                    done(last, ("wt", l, u))
                    if l + 1 < DEPTH and u < 12:
                        mod_rows(l, l + 1, u)
                    if l + 1 < DEPTH and 0 < u <= 12:
                        mod_turned(l + 1, u - 1)
                    if u:
                        diff_out(u - 1)
                diff_out(len(units) - 1)

                for t in range(nt):
                    pe.wait_ge(sem(f"mixed{l}"), t + 1)
                    for half in range(2):
                        b = bank_of(pe, ("t2", l, t, half))
                        mv = mix[:, t, :].rearrange("p (n k) -> p n k", k=KO)
                        for i in range(4):
                            last = tr(b[:, i * P:(i + 1) * P], mv[:, :, half * 4 + i], ident)
                        done(last, ("t2", l, t, half))

                def broadcast(j, s, key):
                    for half in range(2):
                        b = bank_of(pe, key + (half,))
                        for i in range(4):
                            last = mm(b[:, i * P:(i + 1) * P], mcol[:, j, half * 4 + i, s:s + 1].to_broadcast([P, P]),
                                      ident, start=True, stop=True)
                        done(last, key + (half,))

                for j in (GT1, SC2, SH2):
                    for s in streams(l):
                        broadcast(j, s, ("bc", l, j, s))
                for t in range(nt):
                    taken(pe, ("t2", l, t, 0))
                    taken(pe, ("t2", l, t, 1))
                w2 = [loaded(pe, l, ("out", l, half))[:, 0:4096].rearrange("p (k n) -> p k n", k=KO) for half in range(2)]

                def h2_T(t):
                    pe.wait_ge(sem(f"h2_{l}"), t + 1)
                    for half in range(2):
                        b = bank_of(pe, ("t3", l, t, half))
                        hv = tmp[:, (t % 2) * D:(t % 2 + 1) * D].rearrange("p (n k) -> p n k", k=KO)
                        for i in range(4):
                            last = tr(b[:, i * P:(i + 1) * P], hv[:, :, half * 4 + i], ident)
                        done(last, ("t3", l, t, half))

                for t in range(nt):
                    for half in range(2):
                        b = bank_of(pe, ("m", l, half, t))
                        for k in range(KO):
                            last = mm(b[:, :], mixT[:, k, t * P:(t + 1) * P], w2[half][:, k, :], start=(k == 0), stop=(k == KO - 1))
                        done(last, ("m", l, half, t))
                    if t:
                        h2_T(t - 1)
                h2_T(nt - 1)
                for t in range(nt):
                    taken(pe, ("t3", l, t, 0))
                    taken(pe, ("t3", l, t, 1))
                b = bank_of(pe, ("rt", l))
                for t in range(nt):
                    for k in range(KO):
                        last = mm(b[:, t * NE:(t + 1) * NE], mixT[:, k, t * P:(t + 1) * P], wr[:, l, k, :],
                                  start=(k == 0), stop=(k == KO - 1))
                done(last, ("rt", l))
                wsh = loaded(pe, l, ("sh", l, 0))
                wgu = wsh[:, 0:4096].rearrange("p (w k n m) -> p w k n m", w=2, k=KO, m=2)
                for m in range(2):
                    for w in range(2):
                        b = bank_of(pe, ("sh", l, m, w))
                        for k in range(KO):
                            last = mm(b[:, 0:ntok], wgu[:, w, k, :, m], mixT[:, k, 0:ntok], start=(k == 0), stop=(k == KO - 1))
                        done(last, ("sh", l, m, w))
                msk = rsc[:, 256:512]
                pe.wait_ge(sem(f"masked{l}"), 1)
                b = bank_of(pe, ("rank", l))
                for t in range(nt):
                    for n, u in enumerate(range(t + 1)):
                        last = mm(b[:, t * NE:(t + 1) * NE], const("exc_b") if u == t else const("ones"),
                                  msk[:, u * NE:(u + 1) * NE], start=(n == 0), stop=(n == t))
                done(last, ("rank", l))
                b = bank_of(pe, ("cnt", l))
                for t in range(nt):
                    last = mm(b[0:NE, 0:1], msk[:, t * NE:(t + 1) * NE], const("ones")[:, 0:1], start=(t == 0), stop=(t == nt - 1))
                done(last, ("cnt", l))
                nx = extra_blocks(ntok)
                npr = (NE + nx + NSLOT) // 2
                xcol = small[0:NE, 0:1]
                pe.wait_ge(sem(f"xcol{l}"), 1)
                b = bank_of(pe, ("xs", l))
                done(mm(b[:, 0:NE], xcol.to_broadcast([NE, P]), const("exc_b", NE)[:, 0:NE], start=True, stop=True), ("xs", l))
                b = bank_of(pe, ("xe", l))
                done(mm(b[0:NE, 0:1], const("inc_f", NE)[:, 0:NE], xcol, start=True, stop=True), ("xe", l))
                b = bank_of(pe, ("nx", l))
                done(mm(b[0:1, 0:1], xcol, const("ones", NE)[:, 0:1], start=True, stop=True), ("nx", l))
                pe.wait_ge(sem(f"ended{l}"), 1)
                b = bank_of(pe, ("be", l))
                done(mm(b[0:1, 0:nx], const("ones", NE)[:, 0:1], small[0:NE, 128:128 + nx], start=True, stop=True), ("be", l))
                wd = wsh[:, 4096:6144].rearrange("p (m n) -> p m n", m=2)
                pe.wait_ge(sem(f"shared_h{l}"), 2)
                for t in range(nt):
                    for half in range(2):
                        b = bank_of(pe, ("sd", l, t, half))
                        for m in range(2):
                            last = mm(b[:, :], areg[:, 4096 + m * 512 + t * P:4096 + m * 512 + (t + 1) * P],
                                      wd[:, m, half * 512:(half + 1) * 512], start=(m == 0), stop=(m == 1))
                        done(last, ("sd", l, t, half))
                b = bank_of(pe, ("slot", l), "l")
                Lh = hreg[:, 0:nt * TOPK * P].rearrange("p (n s) -> p n s", s=P)
                Hh = tmp[:, 2048:2048 + nt * TOPK * npr].rearrange("p (n a) -> p n a", a=npr)
                pe.wait_ge(sem(f"onehots{l}"), 1)
                for i in range(nt * TOPK):
                    last = mm(b[:, 0:npr], Lh[:, i, :], Hh[:, i, :], start=(i == 0), stop=(i == nt * TOPK - 1))
                done(last, ("slot", l))

                for i in range(8):
                    pe.wait_ge(free[i], uses[i])
                pe.wait_ge(sem(f"routed{l}"), 1)
                ng = pe.value_load(ngt[0:1, 0:1], min_val=0, max_val=nx // NSLOT) + NE // NSLOT

                def tokens_T(q, par):
                    ge(pe, sem(f"gathered{l}_{par}"), (q + 2 - par) * 8)
                    ge(pe, sem(f"xT0_copied{l}"), q)
                    ge(pe, sem(f"xT1_copied{l}"), q)
                    xg = xgb[par].rearrange("p (n k) -> p n k", k=KO)
                    mm(bank[0][:, 0:P], xg[:, :, 0], ident, start=True, stop=True)
                    for k in range(1, KO):
                        last = tr(bank[k // 4][:, k % 4 * P:(k % 4 + 1) * P], xg[:, :, k], ident)
                    last.then_inc(sem(f"xT{l}"), 1)

                def gate_up(b, j, ks):
                    w = slot[j][:, 0:4096].rearrange("p (a k n) -> p a k n", a=2, k=KO)
                    xT = xTb[j // 2].rearrange("p (k s) -> p k s", k=KO)[:, :, j % 2 * SLOTS:(j % 2 + 1) * SLOTS]
                    for k in ks:
                        for m in range(2):
                            last = mm(bank[2 + j % 2][m * SLOTS:(m + 1) * SLOTS, 0:2 * P].rearrange("p (a n) -> p a n", a=2),
                                      xT[:, k, :], w[:, :, k, m * P:(m + 1) * P], start=(k == 0), stop=(k == KO - 1))
                    return last

                def hidden_T(b, j):
                    ge(pe, sem(f"hidden{l}"), b + 1)
                    ge(pe, sem(f"hidT_copied{l}"), b - 1)
                    mm(bank[4 + j % 2][:, 0:P], hidb[j % 2], ident, start=True, stop=True).then_inc(sem(f"hidT{l}"), 1)

                def down(b, j):
                    ge(pe, sem(f"hidT_copied{l}"), b + 1)
                    ge(pe, sem(f"y_out{l}"), b - 1)
                    w = slot[j][:, 4096:6144].rearrange("p (m n) -> p m n", m=2)
                    for m in range(2):
                        for half in range(2):
                            last = mm(bank[6 + j % 2][half * SLOTS:(half + 1) * SLOTS, :], hidTb[j % 2][:, m * SLOTS:(m + 1) * SLOTS],
                                      w[:, m, half * 512:(half + 1) * 512], start=(m == 0), stop=(m == 1))
                    last.then_inc(sem(f"down{l}"), 1)

                def group(g):
                    for j in range(NSLOT):
                        b = g * NSLOT + j
                        first = isinstance(b, int) and b == 0
                        if j % 2:
                            tokens_T(g * 2 + (j + 1) // 2, (j + 1) // 2 % 2)
                        pe.wait_ge(sem(f"we{l}_{j}_loaded"), (g + 1) * 48)
                        if j % 2 == 0:
                            ge(pe, sem(f"xT0_copied{l}"), g * 2 + j // 2 + 1)
                            ge(pe, sem(f"xT1_copied{l}"), g * 2 + j // 2 + 1)
                        ge(pe, sem(f"hidden{l}"), b - 1)
                        gate_up(b, j, range(KO // 2))
                        if not first:
                            hidden_T(b - 1, (j - 1) % NSLOT)
                        gate_up(b, j, range(KO // 2, KO)).then_inc(sem(f"gate_up{l}"), 1)
                        if not first:
                            down(b - 1, (j - 1) % NSLOT)

                tokens_T(0, 0)
                group(0)
                with pe.Fori(1, ng) as g:
                    group(g)
                hidden_T(ng * NSLOT - 1, NSLOT - 1)
                down(ng * NSLOT - 1, NSLOT - 1)
                pe.wait_ge(sem(f"y_out{l}"), ng * NSLOT)
                pe.wait_ge(sem(f"hidT_copied{l}"), ng * NSLOT)
                pe.wait_ge(sem(f"xT0_copied{l}"), ng * 2 + 1)
                pe.wait_ge(sem(f"xT1_copied{l}"), ng * 2 + 1)
                for s in streams(l):
                    broadcast(GT2, s, ("bc", l, GT2, s))

        @block.sync
        def _(sp):
            n = [0]

            def load(dst, src):
                n[0] += 1
                sp.dma_start(dst, src).then_inc(sem("boot_loaded"), 16)

            cr = condr[:, :].rearrange("p (s k) -> p s k", s=2)
            sp.dma_start(cr[:, 0, :], c[0].rearrange("(p k) -> p k", k=KO)).then_inc(sem("cond_loaded"), 16)
            sp.dma_start(cr[:, 1, :], c_ctx.rearrange("(p k) -> p k", k=KO)).then_inc(sem("cond_loaded"), 16)

            def boot_loads():
                load(Xt[:, 0:2, :], x[0].rearrange("(t p) d -> p t d", p=P))
                load(cst[:, :], consts)
                load(Xt[:, 2:4, :], ctx[0].rearrange("(t p) d -> p t d", p=P))
                for i, g in enumerate((g_pre_mix, g_post_mix, g_pre_ffn, g_post_ffn)):
                    load(vec[:, :, i, :], g.rearrange("l (p k) -> p l k", k=KO))
                for l in range(DEPTH):
                    load(vec[:, l, 4:10, :], b_mod[l].rearrange("(j p k) -> p j k", j=6, k=KO))
                    load(wr[:, l, :, :], w_router[l].rearrange("(p k) e -> p k e", k=KO))
                    load(glaw[0:LOWRANK, l * 256:(l + 1) * 256].rearrange("r (d a) -> r d a", d=2),
                         gla_w_gate[l].rearrange("d r a -> r d a"))
                    load(glab[:, l * 256:(l + 1) * 256], gla_b_gate[l].rearrange("(o d) a -> o (d a)", o=1))
                    load(rbias[:, l * NE:(l + 1) * NE], router_bias[l].partition_broadcast(P))
                    load(glag[:, l * 64:(l + 1) * 64], gla_norm_g[l].partition_broadcast(P))
                    load(diffg[:, l * 128:(l + 1) * 128], diff_norm_g[l].partition_broadcast(P))
                    load(tmp[:, l * 256:(l + 1) * 256], diff_lambda[l].rearrange("a b -> (a b)").partition_broadcast(P))
                    load(retl[:, l * 8:(l + 1) * 8], ret_decay_logit[l].rearrange("a b -> (a b)").partition_broadcast(P))
                load(hreg[:, 0:len(LEVELS) * P], level_masks)
                assert n[0] == BOOT_LOADS

            for l in range(DEPTH):
                nt = nt_of(l)
                loads = static_loads(l)
                for m, item in enumerate(loads):
                    if m >= 2:
                        product(sp, last_use(loads[m - 2]))
                    elif l:
                        sp.wait_ge(sem(f"down{l - 1}"), ng_before * NSLOT)
                    kind, lw, i = item
                    to, s = slot[m % 2], sem(f"w{l}_{m % 2}_loaded")
                    if kind == "mod":
                        sp.dma_start(to[:, 0:4096].rearrange("p (k n) -> p k n", k=KO),
                                     w_mod[lw].rearrange("(p k) n -> p k n", k=KO)[:, :, i * 512:(i + 1) * 512]).then_inc(s, 16)
                    elif kind == "in":
                        col, width = IN_LOADS[i]
                        sp.dma_start(to[:, 0:KO * width].rearrange("p (k n) -> p k n", k=KO),
                                     w_in[l].rearrange("(p k) n -> p k n", k=KO)[:, :, col:col + width]).then_inc(s, 16)
                    elif kind == "out":
                        sp.dma_start(to[:, 0:4096].rearrange("p (k n) -> p k n", k=KO),
                                     w_out[l].rearrange("(p k) n -> p k n", k=KO)[:, :, i * 512:(i + 1) * 512]).then_inc(s, 16)
                    else:
                        for dst, src in ((to[:, 0:2048], w_sh_gate[l].rearrange("(p k) n -> p (k n)", k=KO)),
                                         (to[:, 2048:4096], w_sh_up[l].rearrange("(p k) n -> p (k n)", k=KO)),
                                         (to[:, 4096:6144], w_sh_down[l].rearrange("(p m) n -> p (m n)", m=2))):
                            sp.dma_start(dst, src).then_inc(s, 16)
                    if l == 0 and m == 1:
                        boot_loads()

                def expert(e, j):
                    for at, w in ((0, w_exp_gate), (2048, w_exp_up)):
                        sp.dma_start(slot[j][:, at:at + 2048], w[l, bass.ds(e, 1)].rearrange("o (p k) n -> p (o k n)", k=KO))\
                            .then_inc(sem(f"we{l}_{j}_loaded"), 16)
                    sp.dma_start(slot[j][:, 4096:6144].rearrange("p (m n) -> p m n", m=2), w_exp_down[l, bass.ds(e, 1)].rearrange("o (m p) n -> p (o m) n", m=2))\
                        .then_inc(sem(f"we{l}_{j}_loaded"), 16)

                product(sp, ("m", l, 1, nt - 1))
                expert(0, 0)
                sp.wait_ge(sem(f"h2_{l}"), nt)
                expert(2, 2)
                expert(3, 3)
                product(sp, ("sd", l, nt - 1, 1))
                expert(1, 1)
                HAND = NE // NSLOT - 1
                with sp.Fori(1, HAND) as g:
                    for j in range(NSLOT):
                        sp.wait_ge(sem(f"down{l}"), (g - 1) * NSLOT + j + 1)
                        expert(g * NSLOT + j, j)
                sp.wait_ge(sem(f"routed{l}"), 1)
                ng = sp.value_load(ngt[0:1, 0:1], min_val=0, max_val=extra_blocks(nt * P) // NSLOT) + NE // NSLOT
                with sp.Fori(HAND, ng) as g:
                    for j in range(NSLOT):
                        e = sp.value_load(tab[0:1, bass.ds(g * NSLOT + j, 1)], min_val=0, max_val=NE - 1)
                        sp.wait_ge(sem(f"down{l}"), (g - 1) * NSLOT + j + 1)
                        expert(e, j)
                ng_before = ng
            for t in range(2):
                sp.wait_ge(sem(f"x_done{DEPTH - 1}"), t + 1)
                sp.dma_start(out[0, t * P:(t + 1) * P, :], Xt[:, t, :]).then_inc(sem("stored"), 16)
            sp.wait_ge(sem("stored"), 32)

        @block.scalar
        def _(act):
            A = nc.scalar.activation
            chain = Chain(act, "act_chain")
            act.wait_ge(sem("cond_loaded"), 32)
            act.wait_ge(sem("cond_padded"), 1)
            A(cnd[:, :, 0:2].rearrange("p k s -> p s k"), condr[:, :].rearrange("p (s k) -> p s k", s=2), ACT.Silu)\
                .then_inc(sem("cond_done"), 1)
            act.wait_ge(sem("boot_sums"), 1)
            chain(A(small[:, 0:16], small[:, 0:16], ACT.Exp))
            A(small[:, 0:16], small[:, 0:16], ACT.Ln, bias=1.0)
            A(lamt[:, 4:8], lamt[:, 0:4], ACT.Exp).then_inc(sem("boot_exps"), 1)
            act.wait_ge(sem("boot_ready"), 1)
            for l in range(DEPTH):
                nt = nt_of(l)
                ntok = nt * P
                nx = extra_blocks(ntok)

                def copy(out_, in_, key, scale=1.0, func=ACT.Copy):
                    release(A(out_, in_, func, scale=scale), key)

                def root_mean_square(src, junk, s, name):
                    chain(A(junk, src, ACT.Square, accum_out=st[:, s:s + 1]))
                    A(st[:, s + 1:s + 2], st[:, s:s + 1], ACT.Sqrt, scale=1.0 / D, bias=eps[:, 0:1])\
                        .then_inc(sem(name), 1)

                for t in range(TILES):
                    x_ready(act, l, t)
                    root_mean_square(Xt[:, t, :], tmp[:, 2048:3072], 2 * t, f"rms1_{l}")
                ones_at = COFF["ones"][0]
                act.dma_start(glrT[LOWRANK:LOWRANK + 1, :].rearrange("o (n a) -> o n a", a=P),
                              consts[0:1, ones_at:ones_at + P].unsqueeze(1).to_broadcast([1, TILES, P]))\
                    .then_inc(sem(f"ones_row{l}"), 16)
                act.wait_ge(sem(f"modded{l}"), 1)
                mcol = mods[:, l]
                for t in range(TILES):
                    s = 0 if t < 2 else 1
                    for half in range(2):
                        key = ("t1", l, t, half)
                        b = product(act, key)
                        for i in range(4):
                            k = half * 4 + i
                            last = A(hT[:, k, t * P:(t + 1) * P], b[:, i * P:(i + 1) * P], ACT.Identity,
                                     scale=mcol[:, SC1, k, s:s + 1], bias=mcol[:, SH1, k, s:s + 1])
                        release(last, key)
                def read_v(i, t):
                    key = ("v", l, i, t)
                    b = product(act, key)
                    if t < nt:
                        A(vv[:, i, t, 256:512], b[:, 256:512], ACT.Silu)
                    copy(vv[:, i, t, 0:256], b[:, 0:256], key)

                for i in range(2):
                    copy(qk[:, 2 * i, 0:ntok], product(act, ("qk", l, 2 * i))[:, 0:ntok], ("qk", l, 2 * i), GLA_SCALE if i else 1.0)
                    copy(qk[:, 2 * i + 1, :], product(act, ("qk", l, 2 * i + 1))[:, :], ("qk", l, 2 * i + 1), 1.0 if i else RET_SCALE)
                    for t in range(TILES):
                        read_v(i, t)
                copy(glrT[0:LOWRANK, :], product(act, ("glr", l))[0:LOWRANK, :], ("glr", l))
                for n in range(4):
                    copy(qk[:, DQ + n, 0:ntok], product(act, ("qk", l, DQ + n))[:, 0:ntok], ("qk", l, DQ + n))
                for n in range(4):
                    copy(qk[:, DK + n, :], product(act, ("qk", l, DK + n))[:, :], ("qk", l, DK + n))
                for t in range(TILES):
                    copy(vv[:, 2, t, :], product(act, ("v", l, 2, t))[:, :], ("v", l, 2, t))
                for t in range(TILES):
                    if t >= 2:
                        taken(act, ("z", l, t - 2))
                    a = tmp[:, 1024 + (t % 2) * 512:1280 + (t % 2) * 512]
                    chain(A(a, product(act, ("z", l, t))[:, 0:256], ACT.Abs))
                    chain(A(a, a, ACT.Exp, scale=-1.0))
                    A(a, a, ACT.Ln, bias=1.0).then_inc(sem(f"lnz{l}"), 1)
                NL = len(LEVELS) + 1
                for t in range(TILES):
                    taken(act, ("z", l, t))
                for v in list(range(NL)) + ["x"]:
                    n = NL if v == "x" else v
                    ge(act, sem(f"gla_qk{l}"), n)
                    for p in range(2 if v == "x" else nt // 2):
                        key = ("E", l, v, p)
                        copy(Eb[:, 2 * p:2 * p + 2, :], product(act, key)[:, :].rearrange("p (t a) -> p t a", t=2), key,
                             1.0 / TAU, ACT.Exp)
                for t in range(nt):
                    copy(mix[:, t, 256:512], product(act, ("og", l, t))[:, 0:256], ("og", l, t))
                dist = const("dist")
                act.wait_ge(sem(f"ret_dist{l}"), 1)
                for h in range(4):
                    if h >= 1:
                        act.wait_ge(sem(f"ret_D{l}"), h)
                    lgf, lgb, nlb, c256f, c256b = (retc[:, (l * 5 + a) * 4 + h:(l * 5 + a) * 4 + h + 1] for a in range(5))
                    E4 = tmp[:, 2048:4096].rearrange("p (n a) -> p n a", n=4)
                    A(E4[:, 0, :], tmp[:, 0:512], ACT.Exp, scale=lgf)
                    A(E4[:, 1, :], tmp[:, 512:1024], ACT.Exp, scale=lgb)
                    A(E4[:, 2, :], dist, ACT.Exp, scale=lgf, bias=c256f)
                    A(E4[:, 3, :], dist, ACT.Exp, scale=nlb, bias=c256b).then_inc(sem(f"ret_E{l}"), 1)
                for t in range(nt):
                    copy(mix[:, t, 0:256], product(act, ("or", l, t))[:, 0:256], ("or", l, t))
                units = [(t, h) for t in range(nt) for h in range(4)]

                def exps(u):
                    t, h = units[u]
                    nk = TOK if t < 2 else CTX
                    if u >= 2:
                        product(act, ("wt", l, u - 2))
                    for m in range(2):
                        key = ("ds", l, t, h, m)
                        act.wait_ge(sem(f"diff_max{l}"), u + 1)
                        last = A(tmp[:, (u % 2) * 1024 + m * 512:(u % 2) * 1024 + m * 512 + nk], product(act, key)[:, 0:nk],
                                 ACT.Exp, scale=DIFF_SCALE, bias=st[:, 64 + 8 * u + m:65 + 8 * u + m],
                                 accum_out=st[:, 66 + 8 * u + m:67 + 8 * u + m])
                        release(last, key)

                def diff_read(t):
                    copy(mix[:, t, 512:1024], product(act, ("do", l, t))[:, :], ("do", l, t))

                exps(0)
                for u, (t, h) in enumerate(units):
                    if u + 1 < len(units):
                        exps(u + 1)
                    nk = TOK if t < 2 else CTX
                    key = ("wt", l, u)
                    b = product(act, key)
                    if u >= 2:
                        if units[u - 2][1] == 3:
                            product(act, ("do", l, units[u - 2][0]))
                        else:
                            act.wait_ge(sem(f"diff_o{l}"), 3 * units[u - 2][0] + units[u - 2][1] + 1)
                    copy(tmp[:, 2048 + (u % 2) * 512:2048 + (u % 2) * 512 + nk], b[:, 0:nk], key)
                    if u and h == 0:
                        diff_read(t - 1)
                diff_read(nt - 1)
                for t in range(nt):
                    taken(act, ("og", l, t))
                    taken(act, ("or", l, t))
                    taken(act, ("do", l, t))
                for t in range(nt):
                    if t >= 2:
                        act.wait_ge(sem(f"head_ss{l}"), t - 1)
                    A(tmp[:, (t % 2) * D:(t % 2 + 1) * D], mix[:, t, :], ACT.Square).then_inc(sem(f"head_sq{l}"), 1)
                for t in range(nt):
                    act.wait_ge(sem(f"head_ss{l}"), t + 1)
                    o = 256 + 32 * t
                    A(st[:, o + 12:o + 20], st[:, o:o + 8], ACT.Sqrt, scale=1.0 / 64, bias=eps[:, 0:1])
                    A(st[:, o + 20:o + 24], st[:, o + 8:o + 12], ACT.Sqrt, scale=1.0 / 128, bias=eps[:, 0:1])\
                        .then_inc(sem(f"head_rms{l}"), 1)
                for t in range(nt):
                    for half in range(2):
                        key = ("t2", l, t, half)
                        copy(mixT[:, half * 4:half * 4 + 4, t * P:(t + 1) * P],
                             product(act, key)[:, :].rearrange("p (k n) -> p k n", k=4), key)

                def read_row(dst, key):
                    for half in range(2):
                        k = key + (half,)
                        copy(dst.rearrange("p (n k) -> p k n", k=KO)[:, half * 4:half * 4 + 4, :],
                             product(act, k)[:, :].rearrange("p (k n) -> p k n", k=4), k)

                def read_h2_T(t):
                    for half in range(2):
                        key = ("t3", l, t, half)
                        copy(mixT[:, half * 4:half * 4 + 4, t * P:(t + 1) * P],
                             product(act, key)[:, :].rearrange("p (k n) -> p k n", k=4), key)

                for v, j in enumerate((GT1, SC2, SH2)):
                    for s in streams(l):
                        read_row(bc[:, v, s, :], ("bc", l, j, s))
                for t in range(nt):
                    for half in range(2):
                        key = ("m", l, half, t)
                        copy(mix[:, t, half * 512:(half + 1) * 512], product(act, key)[:, :], key)
                    taken(act, ("m", l, 0, t))
                    taken(act, ("m", l, 1, t))
                    root_mean_square(mix[:, t, :], tmp[:, 3072:4096], 8 + 2 * t, f"rms2_{l}")
                    act.wait_ge(sem(f"x_mid{l}"), t + 1)
                    root_mean_square(Xt[:, t, :], tmp[:, 2048:3072], 16 + 2 * t, f"rms3_{l}")
                    if t:
                        read_h2_T(t - 1)
                read_h2_T(nt - 1)
                copy(rsc[:, 0:nt * NE], product(act, ("rt", l))[:, 0:nt * NE], ("rt", l), func=ACT.Sigmoid)
                for m in range(2):
                    key = ("sh", l, m, 0)
                    copy(areg[:, 5120 + m * 512:5120 + m * 512 + ntok], product(act, key)[:, 0:ntok], key, func=ACT.Silu)
                for t in range(nt):
                    for half in range(2):
                        key = ("sd", l, t, half)
                        copy(areg[:, t * D + half * 512:t * D + (half + 1) * 512], product(act, key)[:, :], key)
                    taken(act, ("sd", l, t, 1))
                act.wait_ge(sem(f"h2_stored{l}"), 16 * nt)
                act.wait_ge(sem(f"routed{l}"), 1)
                ng = act.value_load(ngt[0:1, 0:1], min_val=0, max_val=nx // NSLOT) + NE // NSLOT

                def copy_T(q, par):
                    ge(act, sem(f"xT{l}"), q + 1)
                    ge(act, sem(f"gate_up{l}"), 2 * q - 2)
                    A(xTb[par][:, 0:512], bank[0][:, :], ACT.Copy).then_inc(sem(f"xT0_copied{l}"), 1)

                def gate(b, j):
                    act.wait_ge(sem(f"gate_up{l}"), b + 1)
                    ge(act, sem(f"hidden{l}"), b - 1)
                    A(silub[j % 2], bank[2 + j % 2][:, 0:P], ACT.Silu).then_inc(sem(f"gated{l}"), 1)

                def store(b, j):
                    ge(act, sem(f"y_out{l}"), b + 1)
                    for half in range(2):
                        act.dma_start(yd[l][bass.ds(b * SLOTS, SLOTS), half * 512:(half + 1) * 512],
                                      yb[j][half * SLOTS:(half + 1) * SLOTS, :]).then_inc(sem(f"y_stored{l}_{j}"), 16)

                def group(g):
                    for j in range(NSLOT):
                        b = g * NSLOT + j
                        if j % 2:
                            copy_T(g * 2 + (j + 1) // 2, (j + 1) // 2 % 2)
                        gate(b, j)
                        if not (isinstance(b, int) and b == 0):
                            store(b - 1, (j - 1) % NSLOT)

                copy_T(0, 0)
                group(0)
                with act.Fori(1, ng) as g:
                    group(g)
                store(ng * NSLOT - 1, NSLOT - 1)
                act.wait_ge(sem(f"down{l}"), ng * NSLOT)
                for s in streams(l):
                    read_row(qkreg[:, s * D:(s + 1) * D], ("bc", l, GT2, s))
                for t in range(nt):
                    act.wait_ge(sem(f"added{l}"), (t + 1) * TOPK)
                    root_mean_square(areg[:, t * D:(t + 1) * D], tmp[:, 2048:3072], 24 + 2 * t, f"rms4_{l}")

        @block.vector
        def _(dve):
            V = nc.vector
            TT, TS, STT = V.tensor_tensor, V.tensor_scalar, V.scalar_tensor_tensor
            link = Chain(dve, "dve_chain")

            def total(out_, in_):
                return V.tensor_reduce(out_, in_, AX.X, ALU.add)

            V.memset(cond[:, :], 0.0).then_inc(sem("cond_padded"), 1)
            V.memset(eps[:, :], EPS)
            V.memset(areg[:, 0:512], 0.0).then_inc(sem("zeroed"), 1)
            boot(dve)
            V.tensor_copy(mskt[:, :], hreg[:, 0:len(LEVELS) * P])
            STT(small[:, 0:16], retl[:, :], -1.0, retl[:, :], ALU.mult, ALU.min)
            TS(small[:, 16:32], retl[:, :], 0.0, None, ALU.min)
            lp = tmp[:, 0:512].rearrange("p (n two a) -> p n two a", two=2, a=64)
            prod4 = tmp[:, 512:768].rearrange("p (n a) -> p n a", a=64)
            link(TT(prod4, lp[:, :, 0, :], lp[:, :, 1, :], ALU.mult))
            total(lamt[:, 0:4], prod4).then_inc(sem("boot_sums"), 1)
            dve.wait_ge(sem("boot_exps"), 1)
            r5 = retc[:, :].rearrange("p (l a h) -> p l a h", l=DEPTH, a=5)
            zmin = small[:, 16:32].rearrange("p (l a h) -> p l a h", l=DEPTH, a=2)
            lnz = small[:, 0:16].rearrange("p (l a h) -> p l a h", l=DEPTH, a=2)
            e4 = lamt[:, 4:8].rearrange("p (l a) -> p l a", l=DEPTH)
            for l in range(DEPTH):
                TT(lamt[:, 8 + l:9 + l], e4[:, l, 1:2], e4[:, l, 0:1], ALU.subtract)
                TS(diffg[:, l * 128:(l + 1) * 128], diffg[:, l * 128:(l + 1) * 128], 1.0 - lam_init(l), None, ALU.mult)
                link(TT(r5[:, l, 0:2, :], zmin[:, l], lnz[:, l], ALU.subtract))
                TS(lamt[:, 8 + l:9 + l], lamt[:, 8 + l:9 + l], -lam_init(l), None, ALU.add)
                TS(r5[:, l, 2, :], r5[:, l, 1, :], -1.0, None, ALU.mult)
                last = TS(r5[:, l, 3:5, :], r5[:, l, 0:2, :], float(SEQ), None, ALU.mult)
            link(last)
            V.tensor_copy(lamt[:, 12:13], lamt[:, 8:9]).then_inc(sem("boot_ready"), 1)

            for l in range(DEPTH):
                nt = nt_of(l)
                ntok = nt * P
                nx = extra_blocks(ntok)
                npr = (NE + nx + NSLOT) // 2

                def normalised(t):
                    dve.wait_ge(sem(f"rms1_{l}"), t + 1)
                    link(V.reciprocal(st[:, 32 + t:33 + t], st[:, 2 * t + 1:2 * t + 2]))
                    if t >= 2:
                        product(dve, ("t1", l, t - 2, 1))
                    TS(tmp[:, (t % 2) * D:(t % 2 + 1) * D], Xt[:, t, :], st[:, 32 + t:33 + t], None, ALU.mult)\
                        .then_inc(sem(f"xn1_{l}"), 1)

                def mod_copy(n, i):
                    key = ("modp", n, i)
                    b = product(dve, key)
                    if i >= 2:
                        product(dve, ("modt", n, i - 2))
                    release(V.tensor_copy(modb[i % 2], b[:, 0:P]), key)

                def mod_column(n, i):
                    key = ("modt", n, i)
                    b = product(dve, key)
                    r = slice(i % 2 * 64, i % 2 * 64 + 64)
                    release(TT(mods[r, n, i // 2].rearrange("p (g a) s -> p a g s", a=2),
                               b[r, 0:16].rearrange("p (a g s) -> p a g s", a=2, s=2),
                               vec[r, n, 4 + i // 2, :].rearrange("p (g a) -> p a g", a=2).unsqueeze(3).to_broadcast([64, 2, 4, 2]),
                               ALU.add), key)

                def mod_gains(n):
                    for i in range(12):
                        taken(dve, ("modt", n, i))
                    for j, g in ((SC1, 0), (GT1, 1), (SC2, 2), (GT2, 3)):
                        gain = vec[:, n, g, :].unsqueeze(2).to_broadcast([P, KO, 2])
                        last = STT(mods[:, n, j], mods[:, n, j], 1.0 if j in (SC1, SC2) else 0.0, gain, ALU.add, ALU.mult)
                    last.then_inc(sem(f"modded{n}"), 1)

                normalised(0)
                normalised(1)
                if l == 0:
                    for i in range(12):
                        mod_copy(0, i)
                        if i:
                            mod_column(0, i - 1)
                    mod_column(0, 11)
                    mod_gains(0)
                normalised(2)
                normalised(3)
                for i, n in enumerate((RQ, RK, 4, 5, 6, 7, 8, 9, 10, 11)):
                    key = ("rope", l, n)
                    b = product(dve, key)
                    part = tmp[:, 2048 + 256 * (i % 2):2304 + 256 * (i % 2)]
                    c_, s_ = (const("cos_r"), const("sin_r")) if n < 4 else (const("cos_d"), const("sin_d"))
                    release(TT(part, b[:, 0:SEQ], s_, ALU.mult), key)
                    link(TT(qk[:, n, 0:SEQ], qk[:, n, 0:SEQ], c_, ALU.mult))
                    taken(dve, key)
                    TT(qk[:, n, 0:SEQ], qk[:, n, 0:SEQ], part, ALU.add).then_inc(sem(f"roped{l}"), 1)
                for t in range(TILES):
                    key = ("z", l, t)
                    dve.wait_ge(sem(f"lnz{l}"), t + 1)
                    b = product(dve, key)
                    a = 1024 + (t % 2) * 512
                    release(STT(la[:, t, :], b[:, 0:256], 0.0, tmp[:, a:a + 256], ALU.min, ALU.subtract), key)
                if l == 0:
                    dve.wait_ge(sem("cleared"), 16 * DEPTH)
                for h in range(4):
                    key = ("gs", l, "d", h)
                    b = product(dve, key)
                    release(STT(attd[:, h, 0:nt, :], b[:, 0:ntok].rearrange("p (t a) -> p t a", t=nt), 2.0,
                                ident.unsqueeze(1).to_broadcast([P, nt, P]), ALU.mult, ALU.mult), key)
                NL = len(LEVELS) + 1

                def tiles_of(a):
                    return a.rearrange("p (t a) -> p t a", a=P)

                def decayed(v):
                    for p in range(nt // 2):
                        taken(dve, ("E", l, v, p))
                    buf = QKb[v % 2]
                    TT(tiles_of(buf[:, 0, 0:ntok]), Eb[:, 0:nt, 0:P], tiles_of(qk[:, GQ, 0:ntok]), ALU.mult)
                    TT(tiles_of(buf[:, 1, 0:ntok]), Eb[:, 0:nt, P:2 * P], tiles_of(qk[:, GK, 0:ntok]), ALU.mult)\
                        .then_inc(sem(f"gla_qk{l}"), 1)

                def decayed_across():
                    for p in range(2):
                        taken(dve, ("E", l, "x", p))
                    buf = QKb[NL % 2]
                    for d in range(2):
                        TT(tiles_of(buf[:, 0, d * SEQ:(d + 1) * SEQ]), Eb[:, 0:2, d * P:(d + 1) * P],
                           tiles_of(qk[:, GQ, 0:SEQ]), ALU.mult)
                        last = TT(tiles_of(buf[:, 1, d * SEQ:(d + 1) * SEQ]), Eb[:, 2:4, d * P:(d + 1) * P],
                                  tiles_of(qk[:, GK, SEQ:TOK]), ALU.mult)
                    last.then_inc(sem(f"gla_qk{l}"), 1)

                decayed(0)
                for v in range(NL):
                    if v + 1 < NL:
                        decayed(v + 1)
                    else:
                        decayed_across()
                    for h in range(4):
                        key = ("gs", l, v, h)
                        b = product(dve, key)
                        data = b[:, 0:ntok].rearrange("p (t a) -> p t a", t=nt)
                        if v < NL - 1:
                            taken(dve, ("gs", l, v - 1 if v else "d", h))
                            release(V.copy_predicated(attd[:, h, 0:nt, :],
                                                      masks[:, v, :].unsqueeze(1).to_broadcast([P, nt, P]), data), key)
                        else:
                            release(V.tensor_copy(atto[:, h, 0:nt, :], data), key)
                for h in range(4):
                    key = ("gs", l, "x", h)
                    b = product(dve, key)
                    release(V.tensor_copy(attx[:, h, :, :].rearrange("p t q -> p (t q)"), b[:, :]), key)
                dist = const("dist")
                TS(tmp[:, 0:512], dist, 0.0, None, ALU.max)
                TS(tmp[:, 512:1024], dist, -1.0, 0.0, ALU.mult, ALU.max).then_inc(sem(f"ret_dist{l}"), 1)
                product(dve, ("og", l, nt - 1))
                D4 = tmp[:, 1024:2048].rearrange("p (a n q) -> p a n q", a=2, n=2)
                E4 = tmp[:, 2048:4096].rearrange("p (n a q) -> p n a q", n=4, a=2)
                for h in range(4):
                    dve.wait_ge(sem(f"ret_E{l}"), h + 1)
                    if h:
                        taken(dve, ("rs", l, h - 1, 2))
                        taken(dve, ("rs", l, h - 1, 3))
                    e0, e1 = tmp[:, 2048:2560], tmp[:, 2560:3072]
                    TT(D4[:, :, 0, :], E4[:, 2], E4[:, 3], ALU.add)
                    STT(e0, dist, 0.0, e0, ALU.is_ge, ALU.mult)
                    link(STT(e1, dist, 0.0, e1, ALU.is_le, ALU.mult))
                    link(TT(D4[:, :, 1, :], E4[:, 0], E4[:, 1], ALU.add))
                    V.tensor_copy(lamt[:, 13:14], lamt[:, 8:9]).then_inc(sem(f"ret_D{l}"), 1)
                    for kt in range(TILES):
                        key = ("rs", l, h, kt)
                        b = product(dve, key)
                        if kt < 2:
                            ins = TT(ratt(h, kt), b[:, 0:SEQ], D4[:, kt, 1, :], ALU.mult)
                        else:
                            at = 1024 + (kt - 2) * 512
                            ins = TT(ratt(h, kt)[:, 0:ntok], b[:, 0:ntok], tmp[:, at:at + ntok], ALU.mult)
                        release(ins, key)
                units = [(t, h) for t in range(nt) for h in range(4)]

                def maxima(u):
                    t, h = units[u]
                    nk = TOK if t < 2 else CTX
                    o = 64 + 8 * u
                    for m in range(2):
                        b = product(dve, ("ds", l, t, h, m))
                        last = V.tensor_reduce(st[:, o + 4 + m:o + 5 + m], b[:, 0:nk], AX.X, ALU.max)
                    link(last)
                    TS(st[:, o:o + 2], st[:, o + 4:o + 6], -DIFF_SCALE, None, ALU.mult).then_inc(sem(f"diff_max{l}"), 1)

                maxima(0)
                for u, (t, h) in enumerate(units):
                    if u + 1 < len(units):
                        maxima(u + 1)
                    if l + 1 < DEPTH and 1 <= u <= 12:
                        mod_copy(l + 1, u - 1)
                    if l + 1 < DEPTH and 2 <= u <= 13:
                        mod_column(l + 1, u - 2)
                    nk = TOK if t < 2 else CTX
                    o = 64 + 8 * u
                    taken(dve, ("ds", l, t, h, 0))
                    taken(dve, ("ds", l, t, h, 1))
                    link(V.reciprocal(st[:, o + 6:o + 8], st[:, o + 2:o + 4]))
                    link(TS(st[:, o + 7:o + 8], st[:, o + 7:o + 8], lamt[:, 8 + l:9 + l], None, ALU.mult))
                    p0 = tmp[:, (u % 2) * 1024:(u % 2) * 1024 + nk]
                    p1 = tmp[:, (u % 2) * 1024 + 512:(u % 2) * 1024 + 512 + nk]
                    link(TS(p1, p1, st[:, o + 7:o + 8], None, ALU.mult))
                    STT(p0, p0, st[:, o + 6:o + 7], p1, ALU.mult, ALU.add).then_inc(sem(f"diff_w{l}"), 1)
                if l + 1 < DEPTH:
                    mod_gains(l + 1)
                for t in range(nt):
                    dve.wait_ge(sem(f"head_sq{l}"), t + 1)
                    sq = tmp[:, (t % 2) * D:(t % 2 + 1) * D]
                    o = 256 + 32 * t
                    total(st[:, o:o + 8], sq[:, 0:512].rearrange("p (n a) -> p n a", a=64))
                    total(st[:, o + 8:o + 12], sq[:, 512:1024].rearrange("p (n a) -> p n a", a=128))\
                        .then_inc(sem(f"head_ss{l}"), 1)
                for t in range(nt):
                    o = 256 + 32 * t
                    dve.wait_ge(sem(f"head_rms{l}"), t + 1)
                    link(V.reciprocal(st[:, o + 12:o + 24], st[:, o + 12:o + 24]))
                    m8 = mix[:, t, 0:512].rearrange("p (n a) -> p n a", a=64)
                    m4 = mix[:, t, 512:1024].rearrange("p (n a) -> p n a", a=128)
                    TT(m8, m8, st[:, o + 12:o + 20].unsqueeze(2).to_broadcast([P, 8, 64]), ALU.mult)
                    link(TT(m4, m4, st[:, o + 20:o + 24].unsqueeze(2).to_broadcast([P, 4, 128]), ALU.mult))
                    TT(mix[:, t, 0:256], mix[:, t, 0:256], vv[:, 0, t, 256:512], ALU.mult)
                    link(TT(mix[:, t, 256:512], mix[:, t, 256:512], vv[:, 1, t, 256:512], ALU.mult))
                    g4 = mix[:, t, 256:512].rearrange("p (n a) -> p n a", a=64)
                    TT(g4, g4, glag[:, l * 64:(l + 1) * 64].unsqueeze(1).to_broadcast([P, 4, 64]), ALU.mult)
                    TT(m4, m4, diffg[:, l * 128:(l + 1) * 128].unsqueeze(1).to_broadcast([P, 4, 128]), ALU.mult)\
                        .then_inc(sem(f"mixed{l}"), 1)
                for s in streams(l):
                    for j in (GT1, SC2, SH2):
                        taken(dve, ("bc", l, j, s, 0))
                        taken(dve, ("bc", l, j, s, 1))
                for t in range(nt):
                    s = 0 if t < 2 else 1
                    dve.wait_ge(sem(f"rms2_{l}"), t + 1)
                    link(V.reciprocal(st[:, 32 + t:33 + t], st[:, 9 + 2 * t:10 + 2 * t]))
                    link(STT(mix[:, t, :], mix[:, t, :], st[:, 32 + t:33 + t], bc[:, 0, s, :], ALU.mult, ALU.mult))
                    TT(Xt[:, t, :], Xt[:, t, :], mix[:, t, :], ALU.add).then_inc(sem(f"x_mid{l}"), 1)
                    dve.wait_ge(sem(f"rms3_{l}"), t + 1)
                    link(V.reciprocal(st[:, 36 + t:37 + t], st[:, 17 + 2 * t:18 + 2 * t]))
                    h2 = tmp[:, (t % 2) * D:(t % 2 + 1) * D]
                    if t >= 2:
                        product(dve, ("t3", l, t - 2, 1))
                        dve.wait_ge(sem(f"h2_stored{l}"), 16 * (t - 1))
                    link(STT(h2, Xt[:, t, :], st[:, 36 + t:37 + t], bc[:, 1, s, :], ALU.mult, ALU.mult))
                    TT(h2, h2, bc[:, 2, s, :], ALU.add).then_inc(sem(f"h2_{l}"), 1)

                row = const("row")

                def per(a, w):
                    return a.rearrange("p (t a) -> p t a", a=w)

                sig, msk = per(rsc[:, 0:nt * NE], NE), per(rsc[:, 256:256 + nt * NE], NE)
                sel, sc8 = rsc[:, 512:512 + nt * NE], rsc[:, 768:768 + nt * NE]
                taken(dve, ("rt", l))
                link(TT(per(sel, NE), sig, rbias[:, l * NE:(l + 1) * NE].unsqueeze(1).to_broadcast([P, nt, NE]), ALU.add))
                for n in range(nt * NGRP):
                    last = V.max(sc8[:, n * 8:(n + 1) * 8], sel[:, n * 8:(n + 1) * 8])
                link(last)
                top = sc8.rearrange("p (n a) -> p n a", a=8)
                gs = small[:, 320:320 + nt * 8]
                link(TT(gs.unsqueeze(2), top[:, :, 0:1], top[:, :, 1:2], ALU.add))
                gm = small[:, 352:352 + nt * 8]
                for t in range(nt):
                    last = V.max(gm[:, t * 8:(t + 1) * 8], gs[:, t * 8:(t + 1) * 8])
                link(last)
                for t in range(nt):
                    last = V.max_index(gi8[:, t * 8:(t + 1) * 8], gm[:, t * 8:(t + 1) * 8], gs[:, t * 8:(t + 1) * 8])
                link(last)
                gif = small[:, 384:384 + nt * 8]
                link(V.tensor_copy(gif, gi8[:, 0:nt * 8]))
                eq = hreg[:, 0:nt * 32].rearrange("p (t g k) -> p t g k", g=NGRP, k=TOPG)
                link(TT(eq, row[:, 0:8].unsqueeze(1).unsqueeze(3).to_broadcast([P, nt, 8, TOPG]),
                        per(gif, 8)[:, :, 0:TOPG].unsqueeze(2).to_broadcast([P, nt, 8, TOPG]), ALU.is_equal))
                gmask = small[:, 416:416 + nt * 8]
                link(total(gmask, hreg[:, 0:nt * 32].rearrange("p (n k) -> p n k", k=TOPG)))
                link(TS(gmask, gmask, BIG, -BIG, ALU.mult, ALU.add))
                link(TT(top, sel.rearrange("p (n a) -> p n a", a=8), gmask.unsqueeze(2).to_broadcast([P, nt * 8, 8]), ALU.add))
                em = small[:, 448:448 + nt * 8]
                for t in range(nt):
                    last = V.max(em[:, t * 8:(t + 1) * 8], sc8[:, t * NE:(t + 1) * NE])
                link(last)
                for t in range(nt):
                    last = V.max_index(ei8[:, t * 8:(t + 1) * 8], em[:, t * 8:(t + 1) * 8], sc8[:, t * NE:(t + 1) * NE])
                link(last)
                eif = small[:, 480:480 + nt * 8]
                link(V.tensor_copy(eif, ei8[:, 0:nt * 8]))
                e6 = per(eif, 8)[:, :, 0:TOPK]
                n6 = nt * TOPK
                OH = hreg[:, 0:n6 * NE].rearrange("p (t k e) -> p t k e", k=TOPK, e=NE)
                PR = hreg[:, 1536:1536 + n6 * NE]
                PR4 = PR.rearrange("p (t k e) -> p t k e", k=TOPK, e=NE)
                PR3 = PR.rearrange("p (n e) -> p n e", e=NE)
                full4 = [P, nt, TOPK, NE]
                link(TT(OH, row[:, 0:NE].unsqueeze(1).unsqueeze(1).to_broadcast(full4), e6.unsqueeze(3).to_broadcast(full4), ALU.is_equal))
                total(msk, OH.rearrange("p t k e -> p t e k")).then_inc(sem(f"masked{l}"), 1)
                link(TT(PR4, OH, sig.unsqueeze(2).to_broadcast(full4), ALU.mult))
                w6, rk, xs, q6, lo = (small[:, 512 + 24 * i:512 + 24 * i + n6] for i in range(5))
                link(total(w6, PR3))
                link(total(small[:, 4:4 + nt], per(w6, TOPK)))
                link(V.reciprocal(small[:, 8:8 + nt], small[:, 4:4 + nt]))
                link(STT(per(w6, TOPK), per(w6, TOPK), ROUTED_SCALE, small[:, 8:8 + nt].unsqueeze(2).to_broadcast([P, nt, TOPK]),
                         ALU.mult, ALU.mult))
                for m in range(2):
                    taken(dve, ("sh", l, m, 0))
                    key = ("sh", l, m, 1)
                    b = product(dve, key)
                    ins = TT(areg[:, 4096 + m * 512:4096 + m * 512 + ntok], areg[:, 5120 + m * 512:5120 + m * 512 + ntok],
                             b[:, 0:ntok], ALU.mult)
                    release(ins, key)
                    taken(dve, key)
                    dve.sem_inc(sem(f"shared_h{l}"), 1)
                b = product(dve, ("rank", l))
                release(TT(PR4, OH, per(b[:, 0:nt * NE], NE).unsqueeze(2).to_broadcast(full4), ALU.mult), ("rank", l))
                taken(dve, ("rank", l))
                link(total(rk, PR3))
                b = product(dve, ("cnt", l))
                release(V.tensor_copy(small[0:NE, 1:2], b[0:NE, 0:1]), ("cnt", l))
                taken(dve, ("cnt", l))
                K = ntok // SLOTS - 1
                link(TS(small[0:NE, 200:200 + K], row[0:NE, 1:1 + K], float(SLOTS), small[0:NE, 1:2], ALU.mult, ALU.is_lt))
                total(small[0:NE, 0:1], small[0:NE, 200:200 + K]).then_inc(sem(f"xcol{l}"), 1)
                b = product(dve, ("xs", l))
                release(TT(PR4, OH, b[:, 0:NE].unsqueeze(1).unsqueeze(1).to_broadcast(full4), ALU.mult), ("xs", l))
                taken(dve, ("xs", l))
                link(total(xs, PR3))
                b = product(dve, ("xe", l))
                release(V.tensor_copy(small[0:NE, 2:3], b[0:NE, 0:1]), ("xe", l))
                taken(dve, ("xe", l))
                TS(small[0:NE, 128:128 + nx], row[0:NE, 0:nx], small[0:NE, 2:3], None, ALU.is_ge).then_inc(sem(f"ended{l}"), 1)
                b = product(dve, ("nx", l))
                release(V.tensor_copy(small[0:1, 3:4], b[0:1, 0:1]), ("nx", l))
                taken(dve, ("nx", l))
                ngr = nx // NSLOT
                link(TS(small[0:1, 232:232 + ngr], row[0:1, 0:ngr], float(NSLOT), small[0:1, 3:4], ALU.mult, ALU.is_lt))
                link(total(small[0:1, 12:13], small[0:1, 232:232 + ngr]))
                V.tensor_copy(ngt[:, :], small[0:1, 12:13])
                b = product(dve, ("be", l))
                release(TS(small[0:1, 256:256 + nx], b[0:1, 0:nx], float(NE - 1), None, ALU.min), ("be", l))
                taken(dve, ("be", l))
                V.tensor_copy(tab[:, NE:NE + nx], small[0:1, 256:256 + nx])
                V.tensor_copy(tab[:, 0:NE], row[0:1, 0:NE])
                link(TS(q6, rk, float(SLOTS), None, ALU.is_ge))
                for j in range(2, K + 1):
                    link(STT(q6, rk, float(SLOTS * j), q6, ALU.is_ge, ALU.add))
                STT(lo, q6, -float(SLOTS), rk, ALU.mult, ALU.add)
                link(TT(xs, xs, q6, ALU.add))
                link(STT(per(xs, TOPK), per(xs, TOPK), float(NE - 1), e6, ALU.add, ALU.subtract))
                link(STT(xs, q6, 0.0, xs, ALU.is_gt, ALU.mult))
                link(TT(per(xs, TOPK), per(xs, TOPK), e6, ALU.add))
                link(STT(rk, xs, float(SLOTS), lo, ALU.mult, ALU.add))
                V.tensor_copy(back[:, 0:n6], rk)
                link(TS(q6, xs, 0.5, -0.25, ALU.mult, ALU.add))
                link(TS(q6, q6, ROUND, None, ALU.add))
                link(TS(q6, q6, -ROUND, None, ALU.add))
                link(STT(lo, q6, -2.0 * SLOTS, rk, ALU.mult, ALU.add))
                Lh = hreg[:, 0:n6 * P].rearrange("p (n s) -> p n s", s=P)
                TT(Lh, row[:, :].unsqueeze(1).to_broadcast([P, n6, P]), lo.unsqueeze(2).to_broadcast([P, n6, P]), ALU.is_equal)
                Hh = tmp[:, 2048:2048 + n6 * npr]
                H3 = Hh.rearrange("p (n a) -> p n a", a=npr)
                link(TT(H3, row[:, 0:npr].unsqueeze(1).to_broadcast([P, n6, npr]), q6.unsqueeze(2).to_broadcast([P, n6, npr]),
                        ALU.is_equal))
                H4 = Hh.rearrange("p (t a) -> p t a", t=nt)
                TT(H4, H4, const("tok1")[:, 0:nt].unsqueeze(2).to_broadcast([P, nt, TOPK * npr]), ALU.mult)\
                    .then_inc(sem(f"onehots{l}"), 1)
                key = ("slot", l)
                b = product(dve, key)
                link(TS(rsc[:, 512:512 + npr], b[:, 0:npr], -1.0, 0.0, ALU.add, ALU.max))
                release(V.tensor_copy(idx[:, 0:npr], rsc[:, 512:512 + npr]), key)
                taken(dve, key)
                dve.sem_inc(sem(f"routed{l}"), 1)
                dve.wait_ge(sem(f"routed{l}"), 1)
                dve.wait_ge(sem(f"h2_stored{l}"), 16 * nt)
                ng = dve.value_load(ngt[0:1, 0:1], min_val=0, max_val=nx // NSLOT) + NE // NSLOT

                def copy_T(q, par):
                    ge(dve, sem(f"xT{l}"), q + 1)
                    ge(dve, sem(f"gate_up{l}"), 2 * q - 2)
                    V.tensor_copy(xTb[par][:, 512:1024], bank[1][:, :]).then_inc(sem(f"xT1_copied{l}"), 1)

                def hidden(b, j):
                    ge(dve, sem(f"gated{l}"), b + 1)
                    ge(dve, sem(f"hidT{l}"), b - 1)
                    TT(hidb[j % 2], silub[j % 2], bank[2 + j % 2][:, P:2 * P], ALU.mult).then_inc(sem(f"hidden{l}"), 1)

                def hidden_T(b, j):
                    ge(dve, sem(f"hidT{l}"), b + 1)
                    ge(dve, sem(f"down{l}"), b - 1)
                    V.tensor_copy(hidTb[j % 2], bank[4 + j % 2][:, 0:P]).then_inc(sem(f"hidT_copied{l}"), 1)

                def y_out(b, g, j):
                    ge(dve, sem(f"down{l}"), b + 1)
                    ge(dve, sem(f"y_stored{l}_{j}"), g * 32)
                    V.tensor_copy(yb[j], bank[6 + j % 2][:, :]).then_inc(sem(f"y_out{l}"), 1)

                def group(g):
                    for j in range(NSLOT):
                        b = g * NSLOT + j
                        first = isinstance(b, int) and b == 0
                        if j % 2:
                            copy_T(g * 2 + (j + 1) // 2, (j + 1) // 2 % 2)
                        if not first:
                            hidden_T(b - 1, (j - 1) % NSLOT)
                        hidden(b, j)
                        if not first:
                            y_out(b - 1, g if j else g - 1, (j - 1) % NSLOT)

                copy_T(0, 0)
                group(0)
                with dve.Fori(1, ng) as g:
                    group(g)
                hidden_T(ng * NSLOT - 1, NSLOT - 1)
                y_out(ng * NSLOT - 1, ng - 1, NSLOT - 1)
                for t in range(nt):
                    taken(dve, ("sd", l, t, 0))
                    taken(dve, ("sd", l, t, 1))
                    for k in range(TOPK):
                        i = t * TOPK + k
                        dve.wait_ge(sem(f"back{l}_{i % NBACK}"), 16 * (i // NBACK + 1))
                        f = areg[:, t * D:(t + 1) * D]
                        STT(f, backb[i % NBACK], w6[:, i:i + 1], f, ALU.mult, ALU.add).then_inc(sem(f"added{l}"), 1)
                        dve.wait_ge(sem(f"added{l}"), i + 1)
                for s in streams(l):
                    taken(dve, ("bc", l, GT2, s, 0))
                    taken(dve, ("bc", l, GT2, s, 1))
                for t in range(nt):
                    s = 0 if t < 2 else 1
                    dve.wait_ge(sem(f"rms4_{l}"), t + 1)
                    link(V.reciprocal(st[:, 40 + t:41 + t], st[:, 25 + 2 * t:26 + 2 * t]))
                    f = areg[:, t * D:(t + 1) * D]
                    link(STT(f, f, st[:, 40 + t:41 + t], qkreg[:, s * D:(s + 1) * D], ALU.mult, ALU.mult))
                    TT(Xt[:, t, :], Xt[:, t, :], f, ALU.add).then_inc(sem(f"x_done{l}"), 1)

        @block.gpsimd
        def _(pool):
            G = nc.gpsimd
            pool.wait_ge(sem("zeroed"), 1)
            pool.wait_ge(sem("modded0"), 1)
            for l in range(DEPTH):
                n = extra_blocks(nt_of(l) * P) * SLOTS // P
                pool.dma_start(yd[l][NE * SLOTS:, :].rearrange("(p n) (h a) -> p (n h) a", p=P, h=2),
                               areg[:, 0:512].unsqueeze(1).to_broadcast([P, 2 * n, 512])).then_inc(sem("cleared"), 16)
                pool.wait_ge(sem("cleared"), 16 * (l + 1))
            for l in range(DEPTH):
                nt = nt_of(l)
                nx = extra_blocks(nt * P)
                for t in range(nt):
                    pool.wait_ge(sem(f"h2_{l}"), t + 1)
                    pool.dma_start(h2d[l][t * P:(t + 1) * P, :], tmp[:, (t % 2) * D:(t % 2 + 1) * D])\
                        .then_inc(sem(f"h2_stored{l}"), 16)
                    pool.wait_ge(sem(f"h2_stored{l}"), 16 * (t + 1))
                pool.wait_ge(sem(f"routed{l}"), 1)
                ng = pool.value_load(ngt[0:1, 0:1], min_val=0, max_val=nx // NSLOT) + NE // NSLOT

                def waited():
                    pool.sem_inc(sem(f"turns{l}"), 1)

                def gather(q, par):
                    ge(pool, sem(f"xT{l}"), q - 1)
                    G.tensor_copy(idxb[:, par:par + 1], idx[:, bass.ds(q, 1)]).then_inc(sem(f"picked{l}"), 1)
                    ge(pool, sem(f"picked{l}"), q + 1)
                    waited()
                    G.indirect_dma_start(xgb[par], None, h2d[l], bass.IndirectOffsetOnAxis(ap=idxb[:, par:par + 1], axis=0))\
                        .then_inc(sem(f"gathered{l}_{par}"), 16)

                gather(0, 0)
                gather(1, 1)
                with pool.Fori(1, ng) as g:
                    for par in range(2):
                        gather(g * 2 + par, par)
                for par in range(2):
                    gather(ng * 2 + par, par)
                for j in range(NSLOT):
                    pool.wait_ge(sem(f"y_stored{l}_{j}"), ng * 32)
                for par in range(2):
                    pool.wait_ge(sem(f"gathered{l}_{par}"), (ng + 1) * 16)
                pool.wait_ge(sem(f"down{l}"), ng * NSLOT)
                waited()
                for i in range(nt * TOPK):
                    if i >= NBACK:
                        pool.wait_ge(sem(f"added{l}"), i - NBACK + 1)
                    G.indirect_dma_start(backb[i % NBACK], None, yd[l], bass.IndirectOffsetOnAxis(ap=back[:, i:i + 1], axis=0))\
                        .then_inc(sem(f"back{l}_{i % NBACK}"), 16)


_INS = ['x', 'c', 'ctx', 'c_ctx', 'w_mod', 'b_mod', 'g_pre_mix', 'g_post_mix', 'g_pre_ffn', 'g_post_ffn', 'w_in',
        'w_out', 'ret_decay_logit', 'gla_w_gate', 'gla_b_gate', 'gla_norm_g', 'diff_lambda', 'diff_norm_g',
        'w_router', 'router_bias', 'w_exp_gate', 'w_exp_up', 'w_exp_down', 'w_sh_gate', 'w_sh_up', 'w_sh_down']


def kernel(**inputs):
    import concourse.bacc as bacc
    from concourse.bass_utils import run_bass_kernel_spmd

    nc = bacc.Bacc("TRN2", target_bir_lowering=False, num_devices=1)
    arrays = {name: np.ascontiguousarray(inputs[name]) for name in _INS}
    arrays["shape_tables"] = np.ascontiguousarray(np.concatenate(list(CONSTS.values()), axis=1))
    arrays["level_masks"] = MASKS
    args = [nc.dram_tensor(f"in_{n}", a.shape, mybir.dt.from_np(a.dtype), kind="ExternalInput").ap()
            for n, a in arrays.items()]
    out = nc.dram_tensor("out", (1, SEQ, D), mybir.dt.float32, kind="ExternalOutput").ap()
    hybrid_block(nc, *args, out)
    r = run_bass_kernel_spmd(nc, [{f"in_{n}": a for n, a in arrays.items()}], core_ids=[0])
    return r.results[0]["out"]
```

```python
import math
from contextlib import ExitStack

import numpy as np
import concourse.bass as bass
from concourse import mybir

D = 1024
P = 128
KO = D // P
DEPTH = 2
SEQ = 256
CTX = 256
TOK = SEQ + CTX
TILES = TOK // P
GRID_W = 64
N_IN = 3088
NE = 64
TOPK = 6
NGRP = 8
TOPG = 4
DE = 256
LOWRANK = 16
SLOTS = 64
SLOTW = 3 * KO * DE
NSLOT = 4
EPS = 1e-6
LEVELS = (64, 32, 16, 8, 4, 2, 1)
RET_SCALE = 32 ** -0.5
GLA_SCALE = 32 ** -0.5
DIFF_SCALE = 64 ** -0.5
TAU = 16.0
ROUTED_SCALE = 2.5
IN_LOADS = ((0, 768), (768, 768), (1536, 528), (2064, 512), (2576, 512))
BIG = 1e30
ROUND = 2.0 ** 23


def lam_init(layer):
    return 0.8 - 0.6 * math.exp(-0.3 * layer)


def extra_blocks(tokens):
    n = tokens * TOPK // SLOTS
    return (n + NSLOT - 1) // NSLOT * NSLOT


def shape_constants():
    f = np.float32
    c = {}
    i = np.arange(P)
    c["ident"] = np.eye(P, dtype=f)

    def rope(dh):
        quarter, half = dh // 4, dh // 2
        dd = i % dh
        which, w = dd // half, dd % half
        freqs = (f(10000.0) ** (-np.arange(quarter, dtype=f) / f(quarter))).astype(f)
        t = np.arange(SEQ)
        pos = np.stack([(t // GRID_W).astype(f), (t % GRID_W).astype(f)])
        ang = (pos[which] * freqs[w % quarter][:, None]).astype(f)
        perm = np.zeros((P, P), f)
        first = w < quarter
        for m in range(P):
            if first[m]:
                perm[m + quarter, m] = -1.0
            else:
                perm[m - quarter, m] = 1.0
        return perm, np.cos(ang).astype(f), np.sin(ang).astype(f)

    c["perm_r"], c["cos_r"], c["sin_r"] = rope(32)
    c["perm_d"], c["cos_d"], c["sin_d"] = rope(64)
    t, j = i[:, None], i[None, :]
    c["inc_f"] = (t <= j).astype(f)
    c["exc_f"] = (t > j).astype(f)
    c["inc_b"] = (t >= j).astype(f)
    c["exc_b"] = (t < j).astype(f)
    c["ones"] = np.ones((P, P), f)
    lev, masks = [], []
    for s in LEVELS:
        blk_t, blk_j = t // (2 * s), j // (2 * s)
        same = blk_t == blk_j
        mid = blk_j * 2 * s + s
        second = (j % (2 * s)) >= s
        qf = same & second & (t >= mid) & (t <= j)
        kf = same & ~second & (t > j) & (t < mid)
        qb = same & ~second & (t >= j) & (t < mid)
        kb = same & second & (t >= mid) & (t < j)
        lev += [qf, kf, qb, kb]
        masks.append(same & ((t % (2 * s) >= s) != second))
    c["levels"] = np.concatenate(lev, 1).astype(f)
    q = np.arange(SEQ)[None, None, :]
    k = (np.arange(2)[None, :, None] * P + i[:, None, None])
    c["dist"] = (q - k).reshape(P, 2 * SEQ).astype(f)
    c["row"] = np.broadcast_to(np.arange(P, dtype=f), (P, P))
    c["tok1"] = (np.arange(TILES)[None, :] * P + i[:, None] + 1).astype(f)
    return c, np.concatenate(masks, 1).astype(f)


CONSTS, MASKS = shape_constants()
EARLY = ("ident", "ones", "row", "tok1")
CONSTS = {k: CONSTS[k] for k in list(EARLY) + [k for k in CONSTS if k not in EARLY]}
COFF, _at = {}, 0
for _k, _v in CONSTS.items():
    COFF[_k] = (_at, _v.shape[1])
    _at += _v.shape[1]
CWIDTH = _at
EARLY_WIDTH = sum(COFF[k][1] for k in EARLY)


def hybrid_block(nc, x, c, ctx, c_ctx, w_mod, b_mod, g_pre_mix, g_post_mix, g_pre_ffn, g_post_ffn,
                 w_in, w_out, ret_decay_logit, gla_w_gate, gla_b_gate, gla_norm_g, diff_lambda,
                 diff_norm_g, w_router, router_bias, w_exp_gate, w_exp_up, w_exp_down,
                 w_sh_gate, w_sh_up, w_sh_down, consts, level_masks, out):
    f32, u32, i32 = mybir.dt.float32, mybir.dt.uint32, mybir.dt.int32
    ALU, ACT, AX = mybir.AluOpType, mybir.ActivationFunctionType, mybir.AxisListType
    stack = ExitStack()
    sems = {}

    def sem(name):
        if name not in sems:
            sems[name] = stack.enter_context(nc.semaphore(name))
        return sems[name]

    def sb(name, width, dt=f32, parts=P):
        return stack.enter_context(nc.sbuf_tensor(name, [parts, width], dt))

    def nt_of(l):
        return TILES if l < DEPTH - 1 else 2

    with stack:
        X = sb("X", TILES * D)
        hreg = sb("hreg", TILES * D)
        wreg = sb("wreg", 2 * SLOTW)
        qkreg = sb("qkreg", SLOTW)
        vreg = sb("vreg", SLOTW)
        areg = sb("areg", SLOTW)
        tmp = sb("tmp", 4096)
        cst = sb("cst", CWIDTH)
        vecs = sb("vecs", DEPTH * (4 * KO + 6 * KO))
        wrt = sb("wrt", DEPTH * KO * NE)
        rbias = sb("rbias", DEPTH * NE)
        glaw = sb("glaw", DEPTH * 2 * P, parts=LOWRANK + 1)
        glab = glaw[LOWRANK:LOWRANK + 1, :]
        glag = sb("glag", DEPTH * 64)
        diffg = sb("diffg", DEPTH * 128)
        retl = sb("retl", DEPTH * 8)
        lamt = sb("lamt", DEPTH * 8)
        cond = sb("cond", KO * 32)
        condr = sb("condr", KO * 2)
        modc = sb("modc", DEPTH * 6 * KO * 2)
        mskt = sb("mskt", len(LEVELS) * P, mybir.dt.uint8)
        retc = sb("retc", DEPTH * 5 * 4)
        st = sb("st", 384)
        glrT = areg[0:LOWRANK + 1, 6144 - TOK:6144]
        rsc = hreg[:, 3072:4096]
        small = tmp[:, 3448:4096]
        idx = sb("idx", (NE + extra_blocks(TOK) + NSLOT) // 2, u32)
        idxb = sb("idxb", 2, u32)
        back = sb("back", TILES * TOPK, u32)
        ei8 = sb("ei8", TILES * 8, u32)
        gi8 = sb("gi8", TILES * 8, u32)
        tab = sb("tab", NE + extra_blocks(TOK), i32, parts=1)
        ngt = sb("ngt", 1, i32, parts=1)
        eps = sb("eps", 1)
        bank = [stack.enter_context(nc.psum_tensor(f"bank{i}", [P, 512], f32)) for i in range(8)]

        def const(name, parts=P):
            at, w = COFF[name]
            return cst[0:parts, at:at + w]

        ident = const("ident")
        h2d = [nc.dram_tensor(f"h2_rows{l}", (nt_of(l) * P, D), f32).ap() for l in range(DEPTH)]
        yd = [nc.dram_tensor(f"expert_rows{l}", ((NE + extra_blocks(nt_of(l) * P)) * SLOTS, D), f32).ap()
              for l in range(DEPTH)]
        xgb = [hreg[:, i * D:(i + 1) * D] for i in range(2)]
        xTb = [hreg[:, (2 + i) * D:(3 + i) * D] for i in range(2)]
        yb = [tmp[:, i * 512:(i + 1) * 512] for i in range(NSLOT)]
        silub, hidb, hidTb = ([tmp[:, at + i * P:at + (i + 1) * P] for i in range(2)] for at in (2048, 2304, 2560))
        NBACK = 8
        backb = [(vreg if i < 4 else qkreg)[:, (2 + i % 4) * D:(3 + i % 4) * D] for i in range(NBACK)]

        Xt = X[:, :].rearrange("p (t d) -> p t d", t=TILES)
        hT = hreg[:, :].rearrange("p (k t) -> p k t", k=KO)
        mix = hreg[:, :].rearrange("p (t d) -> p t d", t=TILES)
        mixT = areg[:, 0:TILES * D].rearrange("p (k t) -> p k t", k=KO)
        slot = [wreg[:, 0:SLOTW], wreg[:, SLOTW:2 * SLOTW], qkreg[:, :], vreg[:, :]]
        qk = qkreg[:, :].rearrange("p (n t) -> p n t", t=TOK)
        RQ, RK, GQ, GK, DQ, DK = 0, 1, 2, 3, 4, 8
        vv = vreg[:, :].rearrange("p (n t w) -> p n t w", n=3, w=512)
        outT = [[mix[:, 2 * i + pr, 512:1024] for pr in range(2)] for i in range(2)]
        bc = qkreg[:, :].rearrange("p (v s d) -> p v s d", v=3, d=D)
        vec = vecs[:, :].rearrange("p (l n k) -> p l n k", l=DEPTH, k=KO)
        mods = modc[:, :].rearrange("p (l j k s) -> p l j k s", l=DEPTH, j=6, s=2)
        modb = [tmp[:, 3072 + i * P:3072 + (i + 1) * P] for i in range(2)]
        SH1, SC1, GT1, SH2, SC2, GT2 = range(6)
        wr = wrt[:, :].rearrange("p (l k e) -> p l k e", l=DEPTH, e=NE)
        cnd = cond[:, :].rearrange("p (k s) -> p k s", s=32)
        la = tmp[:, 0:1024].rearrange("p (t a) -> p t a", t=TILES)
        Eb = tmp[:, 1024:2048].rearrange("p (t a) -> p t a", t=TILES)
        QKb = [tmp[:, 2048 + 1024 * i:3072 + 1024 * i].rearrange("p (a t) -> p a t", a=2) for i in range(2)]
        attd = areg[:, 0:2048].rearrange("p (h t q) -> p h t q", h=4, q=P)
        atto = areg[:, 2048:4096].rearrange("p (h t q) -> p h t q", h=4, q=P)
        attx = areg[:, 4096:6144].rearrange("p (h t q) -> p h t q", h=4, q=SEQ)

        def ratt(h, kt):
            a = h * 1536
            return areg[:, a + kt * 256:a + kt * 256 + 256] if kt < 2 else \
                areg[:, a + 512 + (kt - 2) * 512:a + 1024 + (kt - 2) * 512]

        levels = const("levels").rearrange("p (v a) -> p v a", a=512)
        masks = mskt[:, :].rearrange("p (v a) -> p v a", a=P)

        full = [sem(f"bank{i}_full") for i in range(8)]
        free = [sem(f"bank{i}_free") for i in range(8)]
        uses, where, turn = [0] * 8, {}, {"g": 0, "l": 0, "m": 0}
        pools = {"g": (0, 1, 2, 3, 4, 5), "l": (6,), "m": (7,)}

        def bank_of(pe, key, pool="g"):
            b = pools[pool][turn[pool] % len(pools[pool])]
            turn[pool] += 1
            where[key] = (b, uses[b])
            if uses[b]:
                pe.wait_ge(free[b], uses[b])
            uses[b] += 1
            return bank[b]

        def done(ins, key):
            ins.then_inc(full[where[key][0]], 1)

        def product(eng, key):
            b, n = where[key]
            eng.wait_ge(full[b], n + 1)
            return bank[b]

        def release(ins, key):
            ins.then_inc(free[where[key][0]], 1)

        def taken(eng, key):
            b, n = where[key]
            eng.wait_ge(free[b], n + 1)

        def ge(eng, s, v):
            if not (isinstance(v, int) and v <= 0):
                eng.wait_ge(s, v)

        class Chain:
            def __init__(self, eng, name):
                self.eng, self.s, self.n = eng, sem(name), 0

            def __call__(self, ins):
                self.n += 1
                ins.then_inc(self.s, 1)
                self.eng.wait_ge(self.s, self.n)

            def mark(self, ins):
                self.n += 1
                ins.then_inc(self.s, 1)

            def wait(self):
                if self.n:
                    self.eng.wait_ge(self.s, self.n)

        BOOT_LOADS, LATE_LOADS = 16, 11

        def boot(eng):
            eng.wait_ge(sem("boot_loaded"), 16 * BOOT_LOADS)

        def late(eng):
            eng.wait_ge(sem("late_loaded"), 16 * LATE_LOADS)

        def static_loads(l):
            return [("mod", n, i) for n in ([0] if l == 0 else []) for i in range(12)] + \
                [("in", l, i) for i in range(len(IN_LOADS))] + \
                [("mod", n, i) for n in range(l + 1, min(l + 2, DEPTH)) for i in range(12)] + \
                [("out", l, 0), ("out", l, 1), ("sh", l, 0)]

        def placed(l):
            held, out_ = {}, []
            for m, item in enumerate(static_loads(l)):
                s = item[2] % NSLOT if item[:2] == ("mod", 0) else m % 2
                out_.append((item, s, held.get(s)))
                held[s] = item
            return out_

        def loaded(eng, l, item):
            dmas = 0
            place = {i: s for i, s, _ in placed(l)}
            for i, s, _ in placed(l):
                dmas += (3 if i[0] == "sh" else 1) * (s == place[item])
                if i == item:
                    break
            eng.wait_ge(sem(f"w{l}_{s}_loaded"), 16 * dmas)
            return slot[s]

        def last_use(item):
            kind, l, i = item
            if kind == "mod":
                return "modp", l, i
            if kind == "in":
                return (("qk", l, RK), ("v", l, 1, 3), ("qk", l, DQ + 3), ("qk", l, DK + 3), ("v", l, 2, 3))[i]
            return "m", l, i, nt_of(l) - 1

        block = stack.enter_context(nc.Block())

        def streams(l):
            return (0, 1) if l < DEPTH - 1 else (0,)

        def x_ready(eng, l, t):
            if l == 0:
                boot(eng)
            else:
                eng.wait_ge(sem(f"x_done{l - 1}"), t + 1)

        @block.tensor
        def _(pe):
            mm, tr = nc.tensor.matmul, nc.tensor.transpose
            pe.wait_ge(sem("cond_done"), 1)
            for l in range(DEPTH):
                nt = nt_of(l)
                ntok = nt * P
                mcol = mods[:, l]

                def mod_rows(at, n, i):
                    b = bank_of(pe, ("modp", n, i), "g" if n == 0 else "m")
                    w = loaded(pe, at, ("mod", n, i))[:, 0:4096].rearrange("p (k n c) -> p k c n", k=KO, c=KO)
                    for k in range(KO):
                        for g in range(4):
                            last = mm(b[32 * g:32 * g + 32, 0:P].rearrange("p (a n) -> p a n", a=2), cnd[:, k, :],
                                      w[:, k, 2 * g:2 * g + 2, :], start=(k == 0), stop=(k == KO - 1))
                    done(last, ("modp", n, i))

                def mod_turned(n, i):
                    taken(pe, ("modp", n, i))
                    b = bank_of(pe, ("modt", n, i))
                    r = slice(i % 2 * 64, i % 2 * 64 + 64)
                    pick = ident.rearrange("p (g r) -> p g r", r=32)[:, :, 0:2]
                    for a in range(2):
                        last = mm(b[r, a * 8:(a + 1) * 8].rearrange("p (g s) -> p g s", s=2), modb[i % 2][:, a * 64:(a + 1) * 64],
                                  pick, start=True, stop=True)
                    done(last, ("modt", n, i))

                if l == 0:
                    for i in range(12):
                        mod_rows(0, 0, i)
                        if i == 0:
                            boot(pe)
                        else:
                            mod_turned(0, i - 1)
                    mod_turned(0, 11)

                def project_T(w, col, n, key, cols=TOK):
                    b = bank_of(pe, key)
                    for k in range(KO):
                        last = mm(b[0:n, 0:cols], w[:, k, col:col + n], hT[:, k, 0:cols], start=(k == 0), stop=(k == KO - 1))
                    done(last, key)

                def project(w, col, t, key, cols=512):
                    b = bank_of(pe, key)
                    for k in range(KO):
                        last = mm(b[:, 0:cols], hT[:, k, t * P:(t + 1) * P], w[:, k, col:col + cols],
                                  start=(k == 0), stop=(k == KO - 1))
                    done(last, key)

                w_first = slot[0][:, 0:KO * IN_LOADS[0][1]].rearrange("p (k n) -> p k n", k=KO)

                def first_values(t):
                    if t == 0:
                        loaded(pe, l, ("in", l, 0))
                    taken(pe, ("t1", l, t, 0))
                    taken(pe, ("t1", l, t, 1))
                    project(w_first, 2 * P, t, ("v", l, 0, t), 512 if t < nt else 256)

                for t in range(TILES):
                    pe.wait_ge(sem(f"xn1_{l}"), t + 1)
                    for half in range(2):
                        b = bank_of(pe, ("t1", l, t, half))
                        xn = tmp[:, (t % 2) * D:(t % 2 + 1) * D].rearrange("p (n k) -> p n k", k=KO)
                        for i in range(4):
                            last = tr(b[:, i * P:(i + 1) * P], xn[:, :, half * 4 + i], ident)
                        done(last, ("t1", l, t, half))
                    if t:
                        first_values(t - 1)
                first_values(TILES - 1)

                def rope(n):
                    taken(pe, ("qk", l, n))
                    b = bank_of(pe, ("rope", l, n))
                    done(mm(b[:, 0:SEQ], const("perm_r" if n < 4 else "perm_d"), qk[:, n, 0:SEQ],
                            start=True, stop=True), ("rope", l, n))

                for i, (_, width) in enumerate(IN_LOADS):
                    w = (loaded(pe, l, ("in", l, i)) if i else slot[0])[:, 0:KO * width].rearrange("p (k n) -> p k n", k=KO)
                    if i < 2:
                        project_T(w, 0, P, ("qk", l, 2 * i), ntok)
                        project_T(w, P, P, ("qk", l, 2 * i + 1))
                        for t in range(TILES if i else 0):
                            project(w, 2 * P, t, ("v", l, i, t), 512 if t < nt else 256)
                        if i == 0:
                            if l == 0:
                                late(pe)
                            rope(RQ)
                            rope(RK)
                    elif i == 2:
                        project_T(w, 0, LOWRANK, ("glr", l))
                        for h in range(4):
                            project_T(w, LOWRANK + h * P, P, ("qk", l, DQ + h), ntok)
                        for h in range(4):
                            rope(DQ + h)
                    elif i == 3:
                        for h in range(4):
                            project_T(w, h * P, P, ("qk", l, DK + h))
                        for h in range(4):
                            rope(DK + h)
                    else:
                        taken(pe, ("glr", l))
                        pe.wait_ge(sem(f"ones_row{l}"), 16)
                        for t in range(TILES):
                            b = bank_of(pe, ("z", l, t))
                            done(mm(b[:, 0:256], glrT[:, t * P:(t + 1) * P], glaw[:, l * 256:(l + 1) * 256], start=True, stop=True),
                                 ("z", l, t))
                        for t in range(TILES):
                            project(w, 0, t, ("v", l, 2, t))

                def gla_scores(v, q_of, k_of, tiles):
                    bs = [bank_of(pe, ("gs", l, v, h)) for h in range(4)]
                    for t in range(nt):
                        for h in range(4):
                            r = slice(32 * h, 32 * h + 32)
                            last = mm(bs[h][:, t * P:(t + 1) * P], k_of(r, t), q_of(r, tiles[t]), start=True, stop=True)
                            if t == nt - 1:
                                done(last, ("gs", l, v, h))

                own = list(range(4))
                other = [1, 0, 3, 2]
                taken(pe, ("qk", l, GQ))
                taken(pe, ("qk", l, GK))
                gla_scores("d", lambda r, t: qk[r, GQ, t * P:(t + 1) * P], lambda r, t: qk[r, GK, t * P:(t + 1) * P], own)
                for t in range(TILES):
                    taken(pe, ("z", l, t))

                def decays(v):
                    for p in range(nt // 2):
                        b = bank_of(pe, ("E", l, v, p))
                        for i in range(2):
                            t = 2 * p + i
                            af, ab = la[:, t, 0:P], la[:, t, P:2 * P]
                            o = b[:, i * 256:(i + 1) * 256]
                            if v < len(LEVELS):
                                mm(o, af, levels[:, v, 0:256], start=True, stop=False)
                                last = mm(o, ab, levels[:, v, 256:512], start=False, stop=True)
                            elif i == 0:
                                mm(o[:, 0:P], ab, const("inc_b"), start=True, stop=True)
                                last = mm(o[:, P:256], af, const("exc_f"), start=True, stop=True)
                            else:
                                mm(o[:, 0:P], af, const("inc_f"), start=True, stop=True)
                                last = mm(o[:, P:256], ab, const("exc_b"), start=True, stop=True)
                        done(last, ("E", l, v, p))

                def decays_across():
                    for p in range(2):
                        b = bank_of(pe, ("E", l, "x", p))
                        sides = (("inc_f", "inc_b"), ("exc_f", "exc_b"))[p]
                        for i in range(2):
                            t = 2 * p + i
                            between = ((None, 1), (0, None))[i] if p == 0 else ((3, None), (None, 2))[i]
                            for d in range(2):
                                o = b[:, i * 256 + d * P:i * 256 + (d + 1) * P]
                                whole = between[d]
                                last = mm(o, la[:, t, d * P:(d + 1) * P], const(sides[d]), start=True, stop=whole is None)
                                if whole is not None:
                                    last = mm(o, la[:, whole, d * P:(d + 1) * P], const("ones"), start=False, stop=True)
                        done(last, ("E", l, "x", p))

                NL = len(LEVELS) + 1
                decays(0)
                for v in range(NL):
                    if v + 1 < NL:
                        decays(v + 1)
                    else:
                        decays_across()
                    pe.wait_ge(sem(f"gla_qk{l}"), v + 1)
                    buf = QKb[v % 2]
                    gla_scores(v, lambda r, t: buf[r, 0, t * P:(t + 1) * P],
                               lambda r, t: buf[r, 1, t * P:(t + 1) * P], own if v < NL - 1 else other)
                pe.wait_ge(sem(f"gla_qk{l}"), NL + 1)
                buf = QKb[NL % 2]
                bs = [bank_of(pe, ("gs", l, "x", h)) for h in range(4)]
                for kt in range(2):
                    for d in range(2):
                        for h in range(4):
                            r = slice(32 * h, 32 * h + 32)
                            last = mm(bs[h][:, kt * SEQ:(kt + 1) * SEQ], buf[r, 1, d * SEQ + kt * P:d * SEQ + (kt + 1) * P],
                                      buf[r, 0, d * SEQ:(d + 1) * SEQ], start=(d == 0), stop=(d == 1))
                            if kt == 1 and d == 1:
                                done(last, ("gs", l, "x", h))
                for h in range(4):
                    taken(pe, ("gs", l, NL - 2, h))
                    taken(pe, ("gs", l, NL - 1, h))
                    taken(pe, ("gs", l, "x", h))
                for t in range(TILES):
                    taken(pe, ("v", l, 1, t))
                def turned_back(i, key):
                    for t in range(nt):
                        b = bank_of(pe, (key, l, t))
                        for pr in range(2):
                            taken(pe, ("oT", l, i, pr))
                            last = tr(b[:, pr * P:(pr + 1) * P], outT[i][pr][:, t * P:(t + 1) * P], ident)
                        done(last, (key, l, t))

                for pr in range(2):
                    b = bank_of(pe, ("oT", l, 1, pr))
                    for kt in range(TILES):
                        for half in range(2):
                            h = 2 * pr + half
                            o = b[half * 64:(half + 1) * 64, :]
                            v = vv[:, 1, kt, h * 64:(h + 1) * 64]
                            if kt < nt:
                                last = mm(o[:, kt * P:(kt + 1) * P], v, attd[:, h, kt, :], start=(kt == 0), stop=False)
                    for kt in range(TILES):
                        for half in range(2):
                            h = 2 * pr + half
                            o = b[half * 64:(half + 1) * 64, :]
                            v = vv[:, 1, kt, h * 64:(h + 1) * 64]
                            if kt >= 2:
                                last = mm(o[:, 0:SEQ], v, attx[:, h, kt - 2, :], start=False, stop=(kt == TILES - 1 and kt >= nt))
                            if kt < nt:
                                q = kt ^ 1
                                last = mm(o[:, q * P:(q + 1) * P], v, atto[:, h, kt, :], start=False, stop=(kt == TILES - 1))
                    done(last, ("oT", l, 1, pr))
                turned_back(1, "og")

                pe.wait_ge(sem(f"roped{l}"), 2)
                for h in range(4):
                    r = slice(32 * h, 32 * h + 32)
                    for kt in range(TILES):
                        b = bank_of(pe, ("rs", l, h, kt))
                        n = SEQ if kt < 2 else ntok
                        done(mm(b[:, 0:n], qk[r, RK, kt * P:(kt + 1) * P], qk[r, RQ, 0:n], start=True, stop=True),
                             ("rs", l, h, kt))
                for t in range(TILES):
                    taken(pe, ("v", l, 0, t))
                    for h in range(4):
                        taken(pe, ("rs", l, h, t))
                for pr in range(2):
                    b = bank_of(pe, ("oT", l, 0, pr))
                    for n, kt in enumerate((2, 3, 0, 1)):
                        for half in range(2):
                            h = 2 * pr + half
                            w = SEQ if kt < 2 else ntok
                            last = mm(b[half * 64:(half + 1) * 64, 0:w], vv[:, 0, kt, h * 64:(h + 1) * 64], ratt(h, kt)[:, 0:w],
                                      start=(n == 0), stop=(n == 3))
                    done(last, ("oT", l, 0, pr))
                turned_back(0, "or")

                pe.wait_ge(sem(f"roped{l}"), 10)
                units = [(t, h) for t in range(nt) for h in range(4)]

                def diff_scores(t, h):
                    k0 = 0 if t < 2 else SEQ
                    for m in range(2):
                        b = bank_of(pe, ("ds", l, t, h, m))
                        r = slice(64 * m, 64 * m + 64)
                        done(mm(b[:, 0:TOK - k0], qk[r, DQ + h, t * P:(t + 1) * P], qk[r, DK + h, k0:TOK],
                                start=True, stop=True), ("ds", l, t, h, m))

                def mix_T(t):
                    pe.wait_ge(sem(f"mixed{l}"), t + 1)
                    for half in range(2):
                        b = bank_of(pe, ("t2", l, t, half))
                        mv = mix[:, t, :].rearrange("p (n k) -> p n k", k=KO)
                        for i in range(4):
                            last = tr(b[:, i * P:(i + 1) * P], mv[:, :, half * 4 + i], ident)
                        done(last, ("t2", l, t, half))

                def diff_out(u):
                    t, h = units[u]
                    kts = (0, 1, 2, 3) if t < 2 else (2, 3)
                    if h == 0:
                        bank_of(pe, ("do", l, t), "l")
                    ob = bank[where[("do", l, t)][0]]
                    taken(pe, ("wt", l, u))
                    WT = tmp[:, 2048 + (u % 2) * 512:2560 + (u % 2) * 512]
                    for n, kt in enumerate(kts):
                        last = mm(ob[:, h * P:(h + 1) * P], WT[:, n * P:(n + 1) * P], vv[:, 2, kt, h * P:(h + 1) * P],
                                  start=(n == 0), stop=(n == len(kts) - 1))
                    if h == 3:
                        done(last, ("do", l, t))
                    else:
                        last.then_inc(sem(f"diff_o{l}"), 1)

                diff_scores(*units[0])
                diff_scores(*units[1])
                for t in range(TILES):
                    taken(pe, ("v", l, 2, t))
                for u, (t, h) in enumerate(units):
                    kts = (0, 1, 2, 3) if t < 2 else (2, 3)
                    if u + 2 < len(units):
                        diff_scores(*units[u + 2])
                    pe.wait_ge(sem(f"diff_w{l}"), u + 1)
                    b = bank_of(pe, ("wt", l, u))
                    for n in range(len(kts)):
                        last = tr(b[:, n * P:(n + 1) * P], tmp[:, (u % 2) * 1024:(u % 2) * 1024 + 512][:, n * P:(n + 1) * P], ident)
                    done(last, ("wt", l, u))
                    if l + 1 < DEPTH and u < 12:
                        mod_rows(l, l + 1, u)
                    if l + 1 < DEPTH and 0 < u <= 12:
                        mod_turned(l + 1, u - 1)
                    if h == 1 and t >= 2:
                        mix_T(t - 2)
                    if u:
                        diff_out(u - 1)
                diff_out(len(units) - 1)
                mix_T(nt - 2)

                def broadcast(j, s, key):
                    for half in range(2):
                        b = bank_of(pe, key + (half,))
                        for i in range(4):
                            last = mm(b[:, i * P:(i + 1) * P], mcol[:, j, half * 4 + i, s:s + 1].to_broadcast([P, P]),
                                      ident, start=True, stop=True)
                        done(last, key + (half,))

                for j in (GT1, SC2, SH2):
                    for s in streams(l):
                        broadcast(j, s, ("bc", l, j, s))
                w2 = [loaded(pe, l, ("out", l, half))[:, 0:4096].rearrange("p (k n) -> p k n", k=KO) for half in range(2)]

                def h2_T(t):
                    pe.wait_ge(sem(f"h2_{l}"), t + 1)
                    for half in range(2):
                        b = bank_of(pe, ("t3", l, t, half))
                        hv = tmp[:, (t % 2) * D:(t % 2 + 1) * D].rearrange("p (n k) -> p n k", k=KO)
                        for i in range(4):
                            last = tr(b[:, i * P:(i + 1) * P], hv[:, :, half * 4 + i], ident)
                        done(last, ("t3", l, t, half))

                for t in range(nt):
                    taken(pe, ("t2", l, t, 0))
                    taken(pe, ("t2", l, t, 1))
                    for half in range(2):
                        b = bank_of(pe, ("m", l, half, t))
                        for k in range(KO):
                            last = mm(b[:, :], mixT[:, k, t * P:(t + 1) * P], w2[half][:, k, :], start=(k == 0), stop=(k == KO - 1))
                        done(last, ("m", l, half, t))
                    if t == 0:
                        mix_T(nt - 1)
                    else:
                        h2_T(t - 1)
                rt = bank_of(pe, ("rt", l))
                for t in range(nt):
                    if t == nt - 1:
                        h2_T(t)
                    taken(pe, ("t3", l, t, 0))
                    taken(pe, ("t3", l, t, 1))
                    for k in range(KO):
                        last = mm(rt[:, t * NE:(t + 1) * NE], mixT[:, k, t * P:(t + 1) * P], wr[:, l, k, :],
                                  start=(k == 0), stop=(k == KO - 1))
                done(last, ("rt", l))
                wsh = loaded(pe, l, ("sh", l, 0))
                wgu = wsh[:, 0:4096].rearrange("p (w k n m) -> p w k n m", w=2, k=KO, m=2)

                def shared_gate_up(m, w):
                    b = bank_of(pe, ("sh", l, m, w))
                    for k in range(KO):
                        last = mm(b[:, 0:ntok], wgu[:, w, k, :, m], mixT[:, k, 0:ntok], start=(k == 0), stop=(k == KO - 1))
                    done(last, ("sh", l, m, w))

                def shared_down(t):
                    for half in range(2):
                        b = bank_of(pe, ("sd", l, t, half))
                        for m in range(2):
                            last = mm(b[:, :], areg[:, 4096 + m * 512 + t * P:4096 + m * 512 + (t + 1) * P],
                                      wd[:, m, half * 512:(half + 1) * 512], start=(m == 0), stop=(m == 1))
                        done(last, ("sd", l, t, half))

                shared_gate_up(0, 0)
                shared_gate_up(0, 1)
                msk = rsc[:, 256:512]
                pe.wait_ge(sem(f"masked{l}"), 1)
                b = bank_of(pe, ("rank", l))
                for t in range(nt):
                    for n, u in enumerate(range(t + 1)):
                        last = mm(b[:, t * NE:(t + 1) * NE], const("exc_b") if u == t else const("ones"),
                                  msk[:, u * NE:(u + 1) * NE], start=(n == 0), stop=(n == t))
                done(last, ("rank", l))
                b = bank_of(pe, ("cnt", l))
                for t in range(nt):
                    last = mm(b[0:NE, 0:1], msk[:, t * NE:(t + 1) * NE], const("ones")[:, 0:1], start=(t == 0), stop=(t == nt - 1))
                done(last, ("cnt", l))
                shared_gate_up(1, 0)
                nx = extra_blocks(ntok)
                npr = (NE + nx + NSLOT) // 2
                xcol = small[0:NE, 0:1]
                pe.wait_ge(sem(f"xcol{l}"), 1)
                b = bank_of(pe, ("xs", l))
                done(mm(b[:, 0:NE], xcol.to_broadcast([NE, P]), const("exc_b", NE)[:, 0:NE], start=True, stop=True), ("xs", l))
                b = bank_of(pe, ("xe", l))
                done(mm(b[0:NE, 0:1], const("inc_f", NE)[:, 0:NE], xcol, start=True, stop=True), ("xe", l))
                b = bank_of(pe, ("nx", l))
                done(mm(b[0:1, 0:1], xcol, const("ones", NE)[:, 0:1], start=True, stop=True), ("nx", l))
                shared_gate_up(1, 1)
                pe.wait_ge(sem(f"ended{l}"), 1)
                b = bank_of(pe, ("be", l))
                done(mm(b[0:1, 0:nx], const("ones", NE)[:, 0:1], small[0:NE, 128:128 + nx], start=True, stop=True), ("be", l))
                wd = wsh[:, 4096:6144].rearrange("p (m n) -> p m n", m=2)
                pe.wait_ge(sem(f"shared_h{l}"), 2)
                for t in range(nt // 2):
                    shared_down(t)
                b = bank_of(pe, ("slot", l), "l")
                Lh = hreg[:, 0:nt * TOPK * P].rearrange("p (n s) -> p n s", s=P)
                Hh = tmp[:, 2048:2048 + nt * TOPK * npr].rearrange("p (n a) -> p n a", a=npr)
                for i in range(nt * TOPK):
                    if i % TOPK == 0:
                        pe.wait_ge(sem(f"onehots{l}"), i // TOPK + 1)
                    last = mm(b[:, 0:npr], Lh[:, i, :], Hh[:, i, :], start=(i == 0), stop=(i == nt * TOPK - 1))
                done(last, ("slot", l))
                for t in range(nt // 2, nt):
                    shared_down(t)

                for i in range(8):
                    pe.wait_ge(free[i], uses[i])
                pe.wait_ge(sem(f"routed{l}"), 1)
                ng = pe.value_load(ngt[0:1, 0:1], min_val=0, max_val=nx // NSLOT) + NE // NSLOT

                def tokens_T(q, par):
                    ge(pe, sem(f"gathered{l}_{par}"), (q + 2 - par) * 8)
                    ge(pe, sem(f"xT0_copied{l}"), q)
                    ge(pe, sem(f"xT1_copied{l}"), q)
                    xg = xgb[par].rearrange("p (n k) -> p n k", k=KO)
                    mm(bank[0][:, 0:P], xg[:, :, 0], ident, start=True, stop=True)
                    for k in range(1, KO):
                        last = tr(bank[k // 4][:, k % 4 * P:(k % 4 + 1) * P], xg[:, :, k], ident)
                    last.then_inc(sem(f"xT{l}"), 1)

                def gate_up(b, j, ks):
                    w = slot[j][:, 0:4096].rearrange("p (a k n) -> p a k n", a=2, k=KO)
                    xT = xTb[j // 2].rearrange("p (k s) -> p k s", k=KO)[:, :, j % 2 * SLOTS:(j % 2 + 1) * SLOTS]
                    for k in ks:
                        for m in range(2):
                            last = mm(bank[2 + j % 2][m * SLOTS:(m + 1) * SLOTS, 0:2 * P].rearrange("p (a n) -> p a n", a=2),
                                      xT[:, k, :], w[:, :, k, m * P:(m + 1) * P], start=(k == 0), stop=(k == KO - 1))
                    return last

                def hidden_T(b, j):
                    ge(pe, sem(f"hidden{l}"), b + 1)
                    ge(pe, sem(f"hidT_copied{l}"), b - 1)
                    mm(bank[4 + j % 2][:, 0:P], hidb[j % 2], ident, start=True, stop=True).then_inc(sem(f"hidT{l}"), 1)

                def down(b, j):
                    ge(pe, sem(f"hidT_copied{l}"), b + 1)
                    ge(pe, sem(f"y_out{l}"), b - 1)
                    w = slot[j][:, 4096:6144].rearrange("p (m n) -> p m n", m=2)
                    for m in range(2):
                        for half in range(2):
                            last = mm(bank[6 + j % 2][half * SLOTS:(half + 1) * SLOTS, :], hidTb[j % 2][:, m * SLOTS:(m + 1) * SLOTS],
                                      w[:, m, half * 512:(half + 1) * 512], start=(m == 0), stop=(m == 1))
                    last.then_inc(sem(f"down{l}"), 1)

                def group(g):
                    for j in range(NSLOT):
                        b = g * NSLOT + j
                        first = isinstance(b, int) and b == 0
                        if j % 2:
                            tokens_T(g * 2 + (j + 1) // 2, (j + 1) // 2 % 2)
                        pe.wait_ge(sem(f"we{l}_{j}_loaded"), (g + 1) * 48)
                        if j % 2 == 0:
                            ge(pe, sem(f"xT0_copied{l}"), g * 2 + j // 2 + 1)
                            ge(pe, sem(f"xT1_copied{l}"), g * 2 + j // 2 + 1)
                        ge(pe, sem(f"hidden{l}"), b - 1)
                        gate_up(b, j, range(KO // 2))
                        if not first:
                            hidden_T(b - 1, (j - 1) % NSLOT)
                        gate_up(b, j, range(KO // 2, KO)).then_inc(sem(f"gate_up{l}"), 1)
                        if not first:
                            down(b - 1, (j - 1) % NSLOT)

                tokens_T(0, 0)
                group(0)
                with pe.Fori(1, ng) as g:
                    group(g)
                hidden_T(ng * NSLOT - 1, NSLOT - 1)
                down(ng * NSLOT - 1, NSLOT - 1)
                pe.wait_ge(sem(f"y_out{l}"), ng * NSLOT)
                pe.wait_ge(sem(f"hidT_copied{l}"), ng * NSLOT)
                pe.wait_ge(sem(f"xT0_copied{l}"), ng * 2 + 1)
                pe.wait_ge(sem(f"xT1_copied{l}"), ng * 2 + 1)
                for s in streams(l):
                    broadcast(GT2, s, ("bc", l, GT2, s))

        @block.sync
        def _(sp):
            n = {"boot_loaded": 0, "late_loaded": 0}

            def load(dst, src, name="boot_loaded"):
                n[name] += 1
                sp.dma_start(dst, src).then_inc(sem(name), 16)

            cr = condr[:, :].rearrange("p (s k) -> p s k", s=2)
            sp.dma_start(cr[:, 0, :], c[0].rearrange("(p k) -> p k", k=KO)).then_inc(sem("cond_loaded"), 16)
            sp.dma_start(cr[:, 1, :], c_ctx.rearrange("(p k) -> p k", k=KO)).then_inc(sem("cond_loaded"), 16)

            def boot_loads():
                load(Xt[:, 0:2, :], x[0].rearrange("(t p) d -> p t d", p=P))
                load(cst[:, 0:EARLY_WIDTH], consts[:, 0:EARLY_WIDTH])
                load(Xt[:, 2:4, :], ctx[0].rearrange("(t p) d -> p t d", p=P))
                for i, g in enumerate((g_pre_mix, g_post_mix, g_pre_ffn, g_post_ffn)):
                    load(vec[:, :, i, :], g.rearrange("l (p k) -> p l k", k=KO))
                for l in range(DEPTH):
                    load(vec[:, l, 4:10, :], b_mod[l].rearrange("(j p k) -> p j k", j=6, k=KO))
                    load(diffg[:, l * 128:(l + 1) * 128], diff_norm_g[l].partition_broadcast(P))
                    load(tmp[:, l * 256:(l + 1) * 256], diff_lambda[l].rearrange("a b -> (a b)").partition_broadcast(P))
                    load(retl[:, l * 8:(l + 1) * 8], ret_decay_logit[l].rearrange("a b -> (a b)").partition_broadcast(P))
                load(hreg[:, 0:len(LEVELS) * P], level_masks)

            def late_loads():
                name = "late_loaded"
                load(cst[:, EARLY_WIDTH:CWIDTH], consts[:, EARLY_WIDTH:CWIDTH], name)
                for l in range(DEPTH):
                    load(glaw[0:LOWRANK, l * 256:(l + 1) * 256].rearrange("r (d a) -> r d a", d=2),
                         gla_w_gate[l].rearrange("d r a -> r d a"), name)
                    load(glab[:, l * 256:(l + 1) * 256], gla_b_gate[l].rearrange("(o d) a -> o (d a)", o=1), name)
                    load(glag[:, l * 64:(l + 1) * 64], gla_norm_g[l].partition_broadcast(P), name)
                    load(wr[:, l, :, :], w_router[l].rearrange("(p k) e -> p k e", k=KO), name)
                    load(rbias[:, l * NE:(l + 1) * NE], router_bias[l].partition_broadcast(P), name)

            for l in range(DEPTH):
                nt = nt_of(l)
                for m, (item, s_, before) in enumerate(placed(l)):
                    if before:
                        product(sp, last_use(before))
                    elif l:
                        sp.wait_ge(sem(f"down{l - 1}"), ng_before * NSLOT - (NSLOT - 1 - m))
                        if m:
                            sp.wait_ge(sem(f"added{l - 1}"), 16)
                    kind, lw, i = item
                    to, s = slot[s_], sem(f"w{l}_{s_}_loaded")
                    if kind == "mod":
                        sp.dma_start(to[:, 0:4096].rearrange("p (k n) -> p k n", k=KO),
                                     w_mod[lw].rearrange("(p k) n -> p k n", k=KO)[:, :, i * 512:(i + 1) * 512]).then_inc(s, 16)
                    elif kind == "in":
                        col, width = IN_LOADS[i]
                        sp.dma_start(to[:, 0:KO * width].rearrange("p (k n) -> p k n", k=KO),
                                     w_in[l].rearrange("(p k) n -> p k n", k=KO)[:, :, col:col + width]).then_inc(s, 16)
                    elif kind == "out":
                        sp.dma_start(to[:, 0:4096].rearrange("p (k n) -> p k n", k=KO),
                                     w_out[l].rearrange("(p k) n -> p k n", k=KO)[:, :, i * 512:(i + 1) * 512]).then_inc(s, 16)
                    else:
                        for dst, src in ((to[:, 0:2048], w_sh_gate[l].rearrange("(p k) n -> p (k n)", k=KO)),
                                         (to[:, 2048:4096], w_sh_up[l].rearrange("(p k) n -> p (k n)", k=KO)),
                                         (to[:, 4096:6144], w_sh_down[l].rearrange("(p m) n -> p (m n)", m=2))):
                            sp.dma_start(dst, src).then_inc(s, 16)
                    if l == 0 and m == 3:
                        boot_loads()
                    if l == 0 and item == ("in", 0, 0):
                        late_loads()
                        assert (n["boot_loaded"], n["late_loaded"]) == (BOOT_LOADS, LATE_LOADS)

                def expert(e, j):
                    for at, w in ((0, w_exp_gate), (2048, w_exp_up)):
                        sp.dma_start(slot[j][:, at:at + 2048], w[l, bass.ds(e, 1)].rearrange("o (p k) n -> p (o k n)", k=KO))\
                            .then_inc(sem(f"we{l}_{j}_loaded"), 16)
                    sp.dma_start(slot[j][:, 4096:6144].rearrange("p (m n) -> p m n", m=2), w_exp_down[l, bass.ds(e, 1)].rearrange("o (m p) n -> p (o m) n", m=2))\
                        .then_inc(sem(f"we{l}_{j}_loaded"), 16)

                product(sp, ("m", l, 1, nt - 1))
                expert(0, 0)
                sp.wait_ge(sem(f"h2_{l}"), nt)
                expert(2, 2)
                expert(3, 3)
                product(sp, ("sd", l, nt - 1, 1))
                expert(1, 1)
                HAND = NE // NSLOT - 1
                with sp.Fori(1, HAND) as g:
                    for j in range(NSLOT):
                        sp.wait_ge(sem(f"down{l}"), (g - 1) * NSLOT + j + 1)
                        expert(g * NSLOT + j, j)
                sp.wait_ge(sem(f"routed{l}"), 1)
                ng = sp.value_load(ngt[0:1, 0:1], min_val=0, max_val=extra_blocks(nt * P) // NSLOT) + NE // NSLOT
                with sp.Fori(HAND, ng) as g:
                    for j in range(NSLOT):
                        e = sp.value_load(tab[0:1, bass.ds(g * NSLOT + j, 1)], min_val=0, max_val=NE - 1)
                        sp.wait_ge(sem(f"down{l}"), (g - 1) * NSLOT + j + 1)
                        expert(e, j)
                ng_before = ng
            for t in range(2):
                sp.wait_ge(sem(f"x_done{DEPTH - 1}"), t + 1)
                sp.dma_start(out[0, t * P:(t + 1) * P, :], Xt[:, t, :]).then_inc(sem("stored"), 16)
            sp.wait_ge(sem("stored"), 32)

        @block.scalar
        def _(act):
            A = nc.scalar.activation
            chain = Chain(act, "act_chain")
            act.wait_ge(sem("cond_loaded"), 32)
            act.wait_ge(sem("cond_padded"), 1)
            A(cnd[:, :, 0:2].rearrange("p k s -> p s k"), condr[:, :].rearrange("p (s k) -> p s k", s=2), ACT.Silu)\
                .then_inc(sem("cond_done"), 1)
            act.wait_ge(sem("boot_sums"), 1)
            chain(A(small[:, 0:16], small[:, 0:16], ACT.Exp))
            A(small[:, 0:16], small[:, 0:16], ACT.Ln, bias=1.0)
            A(lamt[:, 4:8], lamt[:, 0:4], ACT.Exp).then_inc(sem("boot_exps"), 1)
            act.wait_ge(sem("boot_ready"), 1)
            for l in range(DEPTH):
                nt = nt_of(l)
                ntok = nt * P
                nx = extra_blocks(ntok)

                def copy(out_, in_, key, scale=1.0, func=ACT.Copy):
                    release(A(out_, in_, func, scale=scale), key)

                def root_mean_square(src, junk, s, name):
                    chain(A(junk, src, ACT.Square, accum_out=st[:, s:s + 1]))
                    A(st[:, s + 1:s + 2], st[:, s:s + 1], ACT.Sqrt, scale=1.0 / D, bias=eps[:, 0:1])\
                        .then_inc(sem(name), 1)

                def stats(l, t):
                    x_ready(act, l, t)
                    root_mean_square(Xt[:, t, :], tmp[:, 2048:3072], 2 * t, f"rms1_{l}")

                def enter(l, t):
                    s = 0 if t < 2 else 1
                    for half in range(2):
                        key = ("t1", l, t, half)
                        b = product(act, key)
                        for i in range(4):
                            k = half * 4 + i
                            last = A(hT[:, k, t * P:(t + 1) * P], b[:, i * P:(i + 1) * P], ACT.Identity,
                                     scale=mods[:, l, SC1, k, s:s + 1], bias=mods[:, l, SH1, k, s:s + 1])
                        release(last, key)

                def read_v(l, i, t):
                    key = ("v", l, i, t)
                    b = product(act, key)
                    if t < nt_of(l):
                        A(vv[:, i, t, 256:512], b[:, 256:512], ACT.Silu)
                    copy(vv[:, i, t, 0:256], b[:, 0:256], key)

                def enter_tile(l, t):
                    enter(l, t)
                    if t >= 2:
                        read_v(l, 0, t - 2)
                    if t == TILES - 1:
                        read_v(l, 0, t - 1)
                        read_v(l, 0, t)

                def row_of_ones(l):
                    ones_at = COFF["ones"][0]
                    act.dma_start(glrT[LOWRANK:LOWRANK + 1, :].rearrange("o (n a) -> o n a", a=P),
                                  consts[0:1, ones_at:ones_at + P].unsqueeze(1).to_broadcast([1, TILES, P]))\
                        .then_inc(sem(f"ones_row{l}"), 16)

                if l == 0:
                    for t in range(TILES):
                        stats(0, t)
                    row_of_ones(0)
                    act.wait_ge(sem("modded0"), 1)
                    for t in range(TILES):
                        enter_tile(0, t)
                for i in range(2):
                    copy(qk[:, 2 * i, 0:ntok], product(act, ("qk", l, 2 * i))[:, 0:ntok], ("qk", l, 2 * i), GLA_SCALE if i else 1.0)
                    copy(qk[:, 2 * i + 1, :], product(act, ("qk", l, 2 * i + 1))[:, :], ("qk", l, 2 * i + 1), 1.0 if i else RET_SCALE)
                    for t in range(TILES if i else 0):
                        read_v(l, i, t)
                copy(glrT[0:LOWRANK, :], product(act, ("glr", l))[0:LOWRANK, :], ("glr", l))
                for n in range(4):
                    copy(qk[:, DQ + n, 0:ntok], product(act, ("qk", l, DQ + n))[:, 0:ntok], ("qk", l, DQ + n))
                for n in range(4):
                    copy(qk[:, DK + n, :], product(act, ("qk", l, DK + n))[:, :], ("qk", l, DK + n))
                lnz = tmp[:, 1024:2048]
                for t in range(TILES):
                    last = A(lnz[:, t * 256:(t + 1) * 256], product(act, ("z", l, t))[:, 0:256], ACT.Abs)
                chain(last)
                chain(A(lnz, lnz, ACT.Exp, scale=-1.0))
                A(lnz, lnz, ACT.Ln, bias=1.0).then_inc(sem(f"lnz{l}"), 1)
                for t in range(TILES):
                    copy(vv[:, 2, t, :], product(act, ("v", l, 2, t))[:, :], ("v", l, 2, t))
                NL = len(LEVELS) + 1
                for t in range(TILES):
                    taken(act, ("z", l, t))
                for v in list(range(NL)) + ["x"]:
                    n = NL if v == "x" else v
                    ge(act, sem(f"gla_qk{l}"), n)
                    for p in range(2 if v == "x" else nt // 2):
                        key = ("E", l, v, p)
                        copy(Eb[:, 2 * p:2 * p + 2, :], product(act, key)[:, :].rearrange("p (t a) -> p t a", t=2), key,
                             1.0 / TAU, ACT.Exp)
                def read_outT(i):
                    for pr in range(2):
                        key = ("oT", l, i, pr)
                        copy(outT[i][pr][:, 0:ntok], product(act, key)[:, 0:ntok], key)

                dist = const("dist")
                if l == 0:
                    late(act)
                act.wait_ge(sem(f"ret_dist{l}"), 1)
                product(act, ("gs", l, "x", 3))
                for h in range(4):
                    if h == 1:
                        read_outT(1)
                        for t in range(nt):
                            copy(mix[:, t, 256:512], product(act, ("og", l, t))[:, 0:256], ("og", l, t))
                    if h >= 1:
                        act.wait_ge(sem(f"ret_D{l}"), h)
                    lgf, lgb, nlb, c256f, c256b = (retc[:, (l * 5 + a) * 4 + h:(l * 5 + a) * 4 + h + 1] for a in range(5))
                    E4 = tmp[:, 2048:4096].rearrange("p (n a) -> p n a", n=4)
                    A(E4[:, 0, :], tmp[:, 0:512], ACT.Exp, scale=lgf)
                    A(E4[:, 1, :], tmp[:, 512:1024], ACT.Exp, scale=lgb)
                    A(E4[:, 2, :], dist, ACT.Exp, scale=lgf, bias=c256f)
                    A(E4[:, 3, :], dist, ACT.Exp, scale=nlb, bias=c256b).then_inc(sem(f"ret_E{l}"), 1)
                read_outT(0)
                for t in range(nt):
                    copy(mix[:, t, 0:256], product(act, ("or", l, t))[:, 0:256], ("or", l, t))
                units = [(t, h) for t in range(nt) for h in range(4)]

                def exps(u):
                    t, h = units[u]
                    nk = TOK if t < 2 else CTX
                    if u >= 2:
                        product(act, ("wt", l, u - 2))
                    for m in range(2):
                        key = ("ds", l, t, h, m)
                        act.wait_ge(sem(f"diff_max{l}"), u + 1)
                        last = A(tmp[:, (u % 2) * 1024 + m * 512:(u % 2) * 1024 + m * 512 + nk], product(act, key)[:, 0:nk],
                                 ACT.Exp, scale=DIFF_SCALE, bias=st[:, 64 + 8 * u + m:65 + 8 * u + m],
                                 accum_out=st[:, 66 + 8 * u + m:67 + 8 * u + m])
                        release(last, key)

                def diff_read(t):
                    copy(mix[:, t, 512:1024], product(act, ("do", l, t))[:, :], ("do", l, t))

                def squares(t):
                    taken(act, ("og", l, t))
                    taken(act, ("or", l, t))
                    taken(act, ("do", l, t))
                    if t >= 2:
                        act.wait_ge(sem(f"head_ss{l}"), t - 1)
                    A(areg[:, 4096 + (t % 2) * D:4096 + (t % 2 + 1) * D], mix[:, t, :], ACT.Square).then_inc(sem(f"head_sq{l}"), 1)

                def roots(t):
                    act.wait_ge(sem(f"head_ss{l}"), t + 1)
                    o = 256 + 32 * t
                    A(st[:, o + 12:o + 20], st[:, o:o + 8], ACT.Sqrt, scale=1.0 / 64, bias=eps[:, 0:1])
                    A(st[:, o + 20:o + 24], st[:, o + 8:o + 12], ACT.Sqrt, scale=1.0 / 128, bias=eps[:, 0:1])\
                        .then_inc(sem(f"head_rms{l}"), 1)

                def read_mix_T(t):
                    for half in range(2):
                        key = ("t2", l, t, half)
                        copy(mixT[:, half * 4:half * 4 + 4, t * P:(t + 1) * P],
                             product(act, key)[:, :].rearrange("p (k n) -> p k n", k=4), key)

                def finish(u):
                    for t in range(nt):
                        if u == 4 * t + 4:
                            diff_read(t)
                        if u == 4 * t + 5:
                            squares(t)
                        if u == 4 * t + 7:
                            roots(t)
                        if u == 4 * t + 9 and t < nt - 1:
                            read_mix_T(t)

                exps(0)
                for u, (t, h) in enumerate(units):
                    if u + 1 < len(units):
                        exps(u + 1)
                    nk = TOK if t < 2 else CTX
                    key = ("wt", l, u)
                    b = product(act, key)
                    if u >= 2:
                        if units[u - 2][1] == 3:
                            product(act, ("do", l, units[u - 2][0]))
                        else:
                            act.wait_ge(sem(f"diff_o{l}"), 3 * units[u - 2][0] + units[u - 2][1] + 1)
                    copy(tmp[:, 2048 + (u % 2) * 512:2048 + (u % 2) * 512 + nk], b[:, 0:nk], key)
                    finish(u)
                for u in range(len(units), len(units) + 6):
                    finish(u)

                def read_row(dst, key):
                    for half in range(2):
                        k = key + (half,)
                        copy(dst.rearrange("p (n k) -> p k n", k=KO)[:, half * 4:half * 4 + 4, :],
                             product(act, k)[:, :].rearrange("p (k n) -> p k n", k=4), k)

                def read_h2_T(t):
                    for half in range(2):
                        key = ("t3", l, t, half)
                        copy(mixT[:, half * 4:half * 4 + 4, t * P:(t + 1) * P],
                             product(act, key)[:, :].rearrange("p (k n) -> p k n", k=4), key)

                for v, j in enumerate((GT1, SC2, SH2)):
                    for s in streams(l):
                        read_row(bc[:, v, s, :], ("bc", l, j, s))
                for t in range(nt):
                    for half in range(2):
                        key = ("m", l, half, t)
                        copy(mix[:, t, half * 512:(half + 1) * 512], product(act, key)[:, :], key)
                    if t == 0:
                        read_mix_T(nt - 1)
                    taken(act, ("m", l, 0, t))
                    taken(act, ("m", l, 1, t))
                    root_mean_square(mix[:, t, :], tmp[:, 3072:4096], 8 + 2 * t, f"rms2_{l}")
                    act.wait_ge(sem(f"x_mid{l}"), t + 1)
                    root_mean_square(Xt[:, t, :], tmp[:, 2048:3072], 16 + 2 * t, f"rms3_{l}")
                    if t:
                        read_h2_T(t - 1)
                read_h2_T(nt - 1)
                copy(rsc[:, 0:nt * NE], product(act, ("rt", l))[:, 0:nt * NE], ("rt", l), func=ACT.Sigmoid)
                for m in range(2):
                    key = ("sh", l, m, 0)
                    copy(areg[:, 5120 + m * 512:5120 + m * 512 + ntok], product(act, key)[:, 0:ntok], key, func=ACT.Silu)
                for t in range(nt):
                    for half in range(2):
                        key = ("sd", l, t, half)
                        copy(areg[:, t * D + half * 512:t * D + (half + 1) * 512], product(act, key)[:, :], key)
                    taken(act, ("sd", l, t, 1))
                act.wait_ge(sem(f"h2_stored{l}"), 16 * nt)
                act.wait_ge(sem(f"routed{l}"), 1)
                ng = act.value_load(ngt[0:1, 0:1], min_val=0, max_val=nx // NSLOT) + NE // NSLOT

                def copy_T(q, par):
                    ge(act, sem(f"xT{l}"), q + 1)
                    ge(act, sem(f"gate_up{l}"), 2 * q - 2)
                    A(xTb[par][:, 0:512], bank[0][:, :], ACT.Copy).then_inc(sem(f"xT0_copied{l}"), 1)

                def gate(b, j):
                    act.wait_ge(sem(f"gate_up{l}"), b + 1)
                    ge(act, sem(f"hidden{l}"), b - 1)
                    A(silub[j % 2], bank[2 + j % 2][:, 0:P], ACT.Silu).then_inc(sem(f"gated{l}"), 1)

                def store(b, j):
                    ge(act, sem(f"y_out{l}"), b + 1)
                    for half in range(2):
                        act.dma_start(yd[l][bass.ds(b * SLOTS, SLOTS), half * 512:(half + 1) * 512],
                                      yb[j][half * SLOTS:(half + 1) * SLOTS, :]).then_inc(sem(f"y_stored{l}_{j}"), 16)

                def group(g):
                    for j in range(NSLOT):
                        b = g * NSLOT + j
                        if j % 2:
                            copy_T(g * 2 + (j + 1) // 2, (j + 1) // 2 % 2)
                        gate(b, j)
                        if not (isinstance(b, int) and b == 0):
                            store(b - 1, (j - 1) % NSLOT)

                copy_T(0, 0)
                group(0)
                with act.Fori(1, ng) as g:
                    group(g)
                store(ng * NSLOT - 1, NSLOT - 1)
                act.wait_ge(sem(f"down{l}"), ng * NSLOT)
                for s in streams(l):
                    read_row(qkreg[:, s * D:(s + 1) * D], ("bc", l, GT2, s))
                if l + 1 < DEPTH:
                    row_of_ones(l + 1)
                    act.wait_ge(sem(f"modded{l + 1}"), 1)
                for t in range(nt):
                    act.wait_ge(sem(f"added{l}"), (t + 1) * TOPK)
                    root_mean_square(areg[:, t * D:(t + 1) * D], tmp[:, 2048:3072], 24 + 2 * t, f"rms4_{l}")
                    if l + 1 < DEPTH:
                        stats(l + 1, t)
                        enter_tile(l + 1, t)

        @block.vector
        def _(dve):
            V = nc.vector
            TT, TS, STT = V.tensor_tensor, V.tensor_scalar, V.scalar_tensor_tensor
            link = Chain(dve, "dve_chain")

            def total(out_, in_):
                return V.tensor_reduce(out_, in_, AX.X, ALU.add)

            V.memset(cond[:, :], 0.0).then_inc(sem("cond_padded"), 1)
            V.memset(eps[:, :], EPS)
            V.memset(areg[:, 0:512], 0.0).then_inc(sem("zeroed"), 1)
            boot(dve)
            V.tensor_copy(mskt[:, :], hreg[:, 0:len(LEVELS) * P])
            STT(small[:, 0:16], retl[:, :], -1.0, retl[:, :], ALU.mult, ALU.min)
            TS(small[:, 16:32], retl[:, :], 0.0, None, ALU.min)
            lp = tmp[:, 0:512].rearrange("p (n two a) -> p n two a", two=2, a=64)
            prod4 = tmp[:, 512:768].rearrange("p (n a) -> p n a", a=64)
            link(TT(prod4, lp[:, :, 0, :], lp[:, :, 1, :], ALU.mult))
            total(lamt[:, 0:4], prod4).then_inc(sem("boot_sums"), 1)
            dve.wait_ge(sem("boot_exps"), 1)
            r5 = retc[:, :].rearrange("p (l a h) -> p l a h", l=DEPTH, a=5)
            zmin = small[:, 16:32].rearrange("p (l a h) -> p l a h", l=DEPTH, a=2)
            lnz = small[:, 0:16].rearrange("p (l a h) -> p l a h", l=DEPTH, a=2)
            e4 = lamt[:, 4:8].rearrange("p (l a) -> p l a", l=DEPTH)
            for l in range(DEPTH):
                TT(lamt[:, 8 + l:9 + l], e4[:, l, 1:2], e4[:, l, 0:1], ALU.subtract)
                TS(diffg[:, l * 128:(l + 1) * 128], diffg[:, l * 128:(l + 1) * 128], 1.0 - lam_init(l), None, ALU.mult)
                link(TT(r5[:, l, 0:2, :], zmin[:, l], lnz[:, l], ALU.subtract))
                TS(lamt[:, 8 + l:9 + l], lamt[:, 8 + l:9 + l], -lam_init(l), None, ALU.add)
                TS(r5[:, l, 2, :], r5[:, l, 1, :], -1.0, None, ALU.mult)
                last = TS(r5[:, l, 3:5, :], r5[:, l, 0:2, :], float(SEQ), None, ALU.mult)
            link(last)
            dve.sem_inc(sem("boot_ready"), 1)

            for l in range(DEPTH):
                nt = nt_of(l)
                ntok = nt * P
                nx = extra_blocks(ntok)
                npr = (NE + nx + NSLOT) // 2

                def normalised(l, t):
                    dve.wait_ge(sem(f"rms1_{l}"), t + 1)
                    link(V.reciprocal(st[:, 32 + t:33 + t], st[:, 2 * t + 1:2 * t + 2]))
                    if t >= 2:
                        product(dve, ("t1", l, t - 2, 1))
                    TS(tmp[:, (t % 2) * D:(t % 2 + 1) * D], Xt[:, t, :], st[:, 32 + t:33 + t], None, ALU.mult)\
                        .then_inc(sem(f"xn1_{l}"), 1)

                def mod_copy(n, i):
                    key = ("modp", n, i)
                    b = product(dve, key)
                    if i >= 2:
                        product(dve, ("modt", n, i - 2))
                    release(V.tensor_copy(modb[i % 2], b[:, 0:P]), key)

                def mod_column(n, i):
                    key = ("modt", n, i)
                    b = product(dve, key)
                    r = slice(i % 2 * 64, i % 2 * 64 + 64)
                    release(TT(mods[r, n, i // 2].rearrange("p (g a) s -> p a g s", a=2),
                               b[r, 0:16].rearrange("p (a g s) -> p a g s", a=2, s=2),
                               vec[r, n, 4 + i // 2, :].rearrange("p (g a) -> p a g", a=2).unsqueeze(3).to_broadcast([64, 2, 4, 2]),
                               ALU.add), key)

                def mod_gains(n):
                    for i in range(12):
                        taken(dve, ("modt", n, i))
                    for j, g in ((SC1, 0), (GT1, 1), (SC2, 2), (GT2, 3)):
                        gain = vec[:, n, g, :].unsqueeze(2).to_broadcast([P, KO, 2])
                        last = STT(mods[:, n, j], mods[:, n, j], 1.0 if j in (SC1, SC2) else 0.0, gain, ALU.add, ALU.mult)
                    last.then_inc(sem(f"modded{n}"), 1)

                if l == 0:
                    normalised(0, 0)
                    normalised(0, 1)
                    for i in range(12):
                        mod_copy(0, i)
                        if i:
                            mod_column(0, i - 1)
                    mod_column(0, 11)
                    mod_gains(0)
                    normalised(0, 2)
                    normalised(0, 3)
                if l == 0:
                    late(dve)
                for i, n in enumerate((RQ, RK, 4, 5, 6, 7, 8, 9, 10, 11)):
                    key = ("rope", l, n)
                    b = product(dve, key)
                    part = tmp[:, 2048 + 256 * (i % 2):2304 + 256 * (i % 2)]
                    c_, s_ = (const("cos_r"), const("sin_r")) if n < 4 else (const("cos_d"), const("sin_d"))
                    release(TT(part, b[:, 0:SEQ], s_, ALU.mult), key)
                    link(TT(qk[:, n, 0:SEQ], qk[:, n, 0:SEQ], c_, ALU.mult))
                    taken(dve, key)
                    TT(qk[:, n, 0:SEQ], qk[:, n, 0:SEQ], part, ALU.add).then_inc(sem(f"roped{l}"), 1)
                for t in range(TILES):
                    key = ("z", l, t)
                    dve.wait_ge(sem(f"lnz{l}"), 1)
                    b = product(dve, key)
                    a = 1024 + t * 256
                    release(STT(la[:, t, :], b[:, 0:256], 0.0, tmp[:, a:a + 256], ALU.min, ALU.subtract), key)
                if l == 0:
                    dve.wait_ge(sem("cleared"), 16 * DEPTH)
                for h in range(4):
                    key = ("gs", l, "d", h)
                    b = product(dve, key)
                    release(STT(attd[:, h, 0:nt, :], b[:, 0:ntok].rearrange("p (t a) -> p t a", t=nt), 2.0,
                                ident.unsqueeze(1).to_broadcast([P, nt, P]), ALU.mult, ALU.mult), key)
                NL = len(LEVELS) + 1

                def tiles_of(a):
                    return a.rearrange("p (t a) -> p t a", a=P)

                def decayed(v):
                    for p in range(nt // 2):
                        taken(dve, ("E", l, v, p))
                    buf = QKb[v % 2]
                    TT(tiles_of(buf[:, 0, 0:ntok]), Eb[:, 0:nt, 0:P], tiles_of(qk[:, GQ, 0:ntok]), ALU.mult)
                    TT(tiles_of(buf[:, 1, 0:ntok]), Eb[:, 0:nt, P:2 * P], tiles_of(qk[:, GK, 0:ntok]), ALU.mult)\
                        .then_inc(sem(f"gla_qk{l}"), 1)

                def decayed_across():
                    for p in range(2):
                        taken(dve, ("E", l, "x", p))
                    buf = QKb[NL % 2]
                    for d in range(2):
                        TT(tiles_of(buf[:, 0, d * SEQ:(d + 1) * SEQ]), Eb[:, 0:2, d * P:(d + 1) * P],
                           tiles_of(qk[:, GQ, 0:SEQ]), ALU.mult)
                        last = TT(tiles_of(buf[:, 1, d * SEQ:(d + 1) * SEQ]), Eb[:, 2:4, d * P:(d + 1) * P],
                                  tiles_of(qk[:, GK, SEQ:TOK]), ALU.mult)
                    last.then_inc(sem(f"gla_qk{l}"), 1)

                decayed(0)
                for v in range(NL):
                    if v + 1 < NL:
                        decayed(v + 1)
                    else:
                        decayed_across()
                    for h in range(4):
                        key = ("gs", l, v, h)
                        b = product(dve, key)
                        data = b[:, 0:ntok].rearrange("p (t a) -> p t a", t=nt)
                        if v < NL - 1:
                            taken(dve, ("gs", l, v - 1 if v else "d", h))
                            release(V.copy_predicated(attd[:, h, 0:nt, :],
                                                      masks[:, v, :].unsqueeze(1).to_broadcast([P, nt, P]), data), key)
                        else:
                            release(V.tensor_copy(atto[:, h, 0:nt, :], data), key)
                for h in range(4):
                    key = ("gs", l, "x", h)
                    b = product(dve, key)
                    release(V.tensor_copy(attx[:, h, :, :].rearrange("p t q -> p (t q)"), b[:, :]), key)
                dist = const("dist")
                TS(tmp[:, 0:512], dist, 0.0, None, ALU.max)
                TS(tmp[:, 512:1024], dist, -1.0, 0.0, ALU.mult, ALU.max).then_inc(sem(f"ret_dist{l}"), 1)
                D4 = tmp[:, 1024:2048].rearrange("p (a n q) -> p a n q", a=2, n=2)
                E4 = tmp[:, 2048:4096].rearrange("p (n a q) -> p n a q", n=4, a=2)
                for h in range(4):
                    dve.wait_ge(sem(f"ret_E{l}"), h + 1)
                    if h:
                        taken(dve, ("rs", l, h - 1, 2))
                        taken(dve, ("rs", l, h - 1, 3))
                    e0, e1 = tmp[:, 2048:2560], tmp[:, 2560:3072]
                    TT(D4[:, :, 0, :], E4[:, 2], E4[:, 3], ALU.add)
                    STT(e0, dist, 0.0, e0, ALU.is_ge, ALU.mult)
                    link(STT(e1, dist, 0.0, e1, ALU.is_le, ALU.mult))
                    link(TT(D4[:, :, 1, :], E4[:, 0], E4[:, 1], ALU.add))
                    dve.sem_inc(sem(f"ret_D{l}"), 1)
                    if h == 0:
                        product(dve, ("oT", l, 1, 1))
                    for kt in range(TILES):
                        key = ("rs", l, h, kt)
                        b = product(dve, key)
                        if kt < 2:
                            ins = TT(ratt(h, kt), b[:, 0:SEQ], D4[:, kt, 1, :], ALU.mult)
                        else:
                            at = 1024 + (kt - 2) * 512
                            ins = TT(ratt(h, kt)[:, 0:ntok], b[:, 0:ntok], tmp[:, at:at + ntok], ALU.mult)
                        release(ins, key)
                units = [(t, h) for t in range(nt) for h in range(4)]

                def maxima(u):
                    t, h = units[u]
                    nk = TOK if t < 2 else CTX
                    o = 64 + 8 * u
                    for m in range(2):
                        b = product(dve, ("ds", l, t, h, m))
                        last = V.tensor_reduce(st[:, o + 4 + m:o + 5 + m], b[:, 0:nk], AX.X, ALU.max)
                    link(last)
                    TS(st[:, o:o + 2], st[:, o + 4:o + 6], -DIFF_SCALE, None, ALU.mult).then_inc(sem(f"diff_max{l}"), 1)

                def head_sums(t):
                    dve.wait_ge(sem(f"head_sq{l}"), t + 1)
                    sq = areg[:, 4096 + (t % 2) * D:4096 + (t % 2 + 1) * D]
                    o = 256 + 32 * t
                    total(st[:, o:o + 8], sq[:, 0:512].rearrange("p (n a) -> p n a", a=64))
                    total(st[:, o + 8:o + 12], sq[:, 512:1024].rearrange("p (n a) -> p n a", a=128))\
                        .then_inc(sem(f"head_ss{l}"), 1)

                def head_norms(t):
                    o = 256 + 32 * t
                    dve.wait_ge(sem(f"head_rms{l}"), t + 1)
                    link(V.reciprocal(st[:, o + 12:o + 24], st[:, o + 12:o + 24]))
                    m8 = mix[:, t, 0:512].rearrange("p (n a) -> p n a", a=64)
                    m4 = mix[:, t, 512:1024].rearrange("p (n a) -> p n a", a=128)
                    TT(m8, m8, st[:, o + 12:o + 20].unsqueeze(2).to_broadcast([P, 8, 64]), ALU.mult)
                    link(TT(m4, m4, st[:, o + 20:o + 24].unsqueeze(2).to_broadcast([P, 4, 128]), ALU.mult))
                    TT(mix[:, t, 0:256], mix[:, t, 0:256], vv[:, 0, t, 256:512], ALU.mult)
                    link(TT(mix[:, t, 256:512], mix[:, t, 256:512], vv[:, 1, t, 256:512], ALU.mult))
                    g4 = mix[:, t, 256:512].rearrange("p (n a) -> p n a", a=64)
                    TT(g4, g4, glag[:, l * 64:(l + 1) * 64].unsqueeze(1).to_broadcast([P, 4, 64]), ALU.mult)
                    TT(m4, m4, diffg[:, l * 128:(l + 1) * 128].unsqueeze(1).to_broadcast([P, 4, 128]), ALU.mult)\
                        .then_inc(sem(f"mixed{l}"), 1)

                def finish(u):
                    for t in range(nt):
                        if u == 4 * t + 6:
                            head_sums(t)
                        if u == 4 * t + 8:
                            head_norms(t)

                maxima(0)
                for u, (t, h) in enumerate(units):
                    if u + 1 < len(units):
                        maxima(u + 1)
                    nk = TOK if t < 2 else CTX
                    o = 64 + 8 * u
                    taken(dve, ("ds", l, t, h, 0))
                    taken(dve, ("ds", l, t, h, 1))
                    link(V.reciprocal(st[:, o + 6:o + 8], st[:, o + 2:o + 4]))
                    link(TS(st[:, o + 7:o + 8], st[:, o + 7:o + 8], lamt[:, 8 + l:9 + l], None, ALU.mult))
                    p0 = tmp[:, (u % 2) * 1024:(u % 2) * 1024 + nk]
                    p1 = tmp[:, (u % 2) * 1024 + 512:(u % 2) * 1024 + 512 + nk]
                    link(TS(p1, p1, st[:, o + 7:o + 8], None, ALU.mult))
                    STT(p0, p0, st[:, o + 6:o + 7], p1, ALU.mult, ALU.add).then_inc(sem(f"diff_w{l}"), 1)
                    if l + 1 < DEPTH and 1 <= u <= 12:
                        mod_copy(l + 1, u - 1)
                    if l + 1 < DEPTH and 2 <= u <= 13:
                        mod_column(l + 1, u - 2)
                    finish(u)
                for u in range(len(units), len(units) + 6):
                    finish(u)
                if l + 1 < DEPTH:
                    mod_gains(l + 1)
                for s in streams(l):
                    for j in (GT1, SC2, SH2):
                        taken(dve, ("bc", l, j, s, 0))
                        taken(dve, ("bc", l, j, s, 1))
                for t in range(nt):
                    s = 0 if t < 2 else 1
                    dve.wait_ge(sem(f"rms2_{l}"), t + 1)
                    link(V.reciprocal(st[:, 32 + t:33 + t], st[:, 9 + 2 * t:10 + 2 * t]))
                    link(STT(mix[:, t, :], mix[:, t, :], st[:, 32 + t:33 + t], bc[:, 0, s, :], ALU.mult, ALU.mult))
                    TT(Xt[:, t, :], Xt[:, t, :], mix[:, t, :], ALU.add).then_inc(sem(f"x_mid{l}"), 1)
                    dve.wait_ge(sem(f"rms3_{l}"), t + 1)
                    link(V.reciprocal(st[:, 36 + t:37 + t], st[:, 17 + 2 * t:18 + 2 * t]))
                    h2 = tmp[:, (t % 2) * D:(t % 2 + 1) * D]
                    if t >= 2:
                        product(dve, ("t3", l, t - 2, 1))
                        dve.wait_ge(sem(f"h2_stored{l}"), 16 * (t - 1))
                    link(STT(h2, Xt[:, t, :], st[:, 36 + t:37 + t], bc[:, 1, s, :], ALU.mult, ALU.mult))
                    TT(h2, h2, bc[:, 2, s, :], ALU.add).then_inc(sem(f"h2_{l}"), 1)

                row = const("row")

                def per(a, w):
                    return a.rearrange("p (t a) -> p t a", a=w)

                sig, msk = per(rsc[:, 0:nt * NE], NE), per(rsc[:, 256:256 + nt * NE], NE)
                sel, sc8 = rsc[:, 512:512 + nt * NE], rsc[:, 768:768 + nt * NE]
                taken(dve, ("rt", l))
                link(TT(per(sel, NE), sig, rbias[:, l * NE:(l + 1) * NE].unsqueeze(1).to_broadcast([P, nt, NE]), ALU.add))
                for n in range(nt * NGRP):
                    last = V.max(sc8[:, n * 8:(n + 1) * 8], sel[:, n * 8:(n + 1) * 8])
                link(last)
                top = sc8.rearrange("p (n a) -> p n a", a=8)
                gs = small[:, 320:320 + nt * 8]
                link(TT(gs.unsqueeze(2), top[:, :, 0:1], top[:, :, 1:2], ALU.add))
                gm = small[:, 352:352 + nt * 8]
                for t in range(nt):
                    last = V.max(gm[:, t * 8:(t + 1) * 8], gs[:, t * 8:(t + 1) * 8])
                link(last)
                for t in range(nt):
                    last = V.max_index(gi8[:, t * 8:(t + 1) * 8], gm[:, t * 8:(t + 1) * 8], gs[:, t * 8:(t + 1) * 8])
                link(last)
                gif = small[:, 384:384 + nt * 8]
                link(V.tensor_copy(gif, gi8[:, 0:nt * 8]))
                eq = hreg[:, 0:nt * 32].rearrange("p (t g k) -> p t g k", g=NGRP, k=TOPG)
                link(TT(eq, row[:, 0:8].unsqueeze(1).unsqueeze(3).to_broadcast([P, nt, 8, TOPG]),
                        per(gif, 8)[:, :, 0:TOPG].unsqueeze(2).to_broadcast([P, nt, 8, TOPG]), ALU.is_equal))
                gmask = small[:, 416:416 + nt * 8]
                link(total(gmask, hreg[:, 0:nt * 32].rearrange("p (n k) -> p n k", k=TOPG)))
                link(TS(gmask, gmask, BIG, -BIG, ALU.mult, ALU.add))
                link(TT(top, sel.rearrange("p (n a) -> p n a", a=8), gmask.unsqueeze(2).to_broadcast([P, nt * 8, 8]), ALU.add))
                em = small[:, 448:448 + nt * 8]
                for t in range(nt):
                    last = V.max(em[:, t * 8:(t + 1) * 8], sc8[:, t * NE:(t + 1) * NE])
                link(last)
                for t in range(nt):
                    last = V.max_index(ei8[:, t * 8:(t + 1) * 8], em[:, t * 8:(t + 1) * 8], sc8[:, t * NE:(t + 1) * NE])
                link(last)
                eif = small[:, 480:480 + nt * 8]
                link(V.tensor_copy(eif, ei8[:, 0:nt * 8]))
                e6 = per(eif, 8)[:, :, 0:TOPK]
                n6 = nt * TOPK
                OH = hreg[:, 0:n6 * NE].rearrange("p (t k e) -> p t k e", k=TOPK, e=NE)
                PR = hreg[:, 1536:1536 + n6 * NE]
                PR4 = PR.rearrange("p (t k e) -> p t k e", k=TOPK, e=NE)
                PR3 = PR.rearrange("p (n e) -> p n e", e=NE)
                full4 = [P, nt, TOPK, NE]
                link(TT(OH, row[:, 0:NE].unsqueeze(1).unsqueeze(1).to_broadcast(full4), e6.unsqueeze(3).to_broadcast(full4), ALU.is_equal))
                total(msk, OH.rearrange("p t k e -> p t e k")).then_inc(sem(f"masked{l}"), 1)
                link(TT(PR4, OH, sig.unsqueeze(2).to_broadcast(full4), ALU.mult))
                w6, rk, xs, q6, lo = (small[:, 512 + 24 * i:512 + 24 * i + n6] for i in range(5))
                link(total(w6, PR3))
                link(total(small[:, 4:4 + nt], per(w6, TOPK)))
                link(V.reciprocal(small[:, 8:8 + nt], small[:, 4:4 + nt]))
                link(STT(per(w6, TOPK), per(w6, TOPK), ROUTED_SCALE, small[:, 8:8 + nt].unsqueeze(2).to_broadcast([P, nt, TOPK]),
                         ALU.mult, ALU.mult))

                def shared_hidden(m):
                    taken(dve, ("sh", l, m, 0))
                    key = ("sh", l, m, 1)
                    b = product(dve, key)
                    release(TT(areg[:, 4096 + m * 512:4096 + m * 512 + ntok], areg[:, 5120 + m * 512:5120 + m * 512 + ntok],
                               b[:, 0:ntok], ALU.mult), key)
                    taken(dve, key)
                    dve.sem_inc(sem(f"shared_h{l}"), 1)

                shared_hidden(0)
                b = product(dve, ("rank", l))
                release(TT(PR4, OH, per(b[:, 0:nt * NE], NE).unsqueeze(2).to_broadcast(full4), ALU.mult), ("rank", l))
                taken(dve, ("rank", l))
                link(total(rk, PR3))
                b = product(dve, ("cnt", l))
                release(V.tensor_copy(small[0:NE, 1:2], b[0:NE, 0:1]), ("cnt", l))
                taken(dve, ("cnt", l))
                K = ntok // SLOTS - 1
                link(TS(small[0:NE, 200:200 + K], row[0:NE, 1:1 + K], float(SLOTS), small[0:NE, 1:2], ALU.mult, ALU.is_lt))
                total(small[0:NE, 0:1], small[0:NE, 200:200 + K]).then_inc(sem(f"xcol{l}"), 1)
                b = product(dve, ("xs", l))
                release(TT(PR4, OH, b[:, 0:NE].unsqueeze(1).unsqueeze(1).to_broadcast(full4), ALU.mult), ("xs", l))
                taken(dve, ("xs", l))
                link(total(xs, PR3))
                b = product(dve, ("xe", l))
                release(V.tensor_copy(small[0:NE, 2:3], b[0:NE, 0:1]), ("xe", l))
                taken(dve, ("xe", l))
                TS(small[0:NE, 128:128 + nx], row[0:NE, 0:nx], small[0:NE, 2:3], None, ALU.is_ge).then_inc(sem(f"ended{l}"), 1)
                b = product(dve, ("nx", l))
                release(V.tensor_copy(small[0:1, 3:4], b[0:1, 0:1]), ("nx", l))
                taken(dve, ("nx", l))
                ngr = nx // NSLOT
                link(TS(small[0:1, 232:232 + ngr], row[0:1, 0:ngr], float(NSLOT), small[0:1, 3:4], ALU.mult, ALU.is_lt))
                link(total(small[0:1, 12:13], small[0:1, 232:232 + ngr]))
                V.tensor_copy(ngt[:, :], small[0:1, 12:13])
                b = product(dve, ("be", l))
                release(TS(small[0:1, 256:256 + nx], b[0:1, 0:nx], float(NE - 1), None, ALU.min), ("be", l))
                taken(dve, ("be", l))
                V.tensor_copy(tab[:, NE:NE + nx], small[0:1, 256:256 + nx])
                V.tensor_copy(tab[:, 0:NE], row[0:1, 0:NE])
                shared_hidden(1)
                link(TS(q6, rk, float(SLOTS), None, ALU.is_ge))
                for j in range(2, K + 1):
                    link(STT(q6, rk, float(SLOTS * j), q6, ALU.is_ge, ALU.add))
                STT(lo, q6, -float(SLOTS), rk, ALU.mult, ALU.add)
                link(TT(xs, xs, q6, ALU.add))
                link(STT(per(xs, TOPK), per(xs, TOPK), float(NE - 1), e6, ALU.add, ALU.subtract))
                link(STT(xs, q6, 0.0, xs, ALU.is_gt, ALU.mult))
                link(TT(per(xs, TOPK), per(xs, TOPK), e6, ALU.add))
                link(STT(rk, xs, float(SLOTS), lo, ALU.mult, ALU.add))
                V.tensor_copy(back[:, 0:n6], rk)
                link(TS(q6, xs, 0.5, -0.25, ALU.mult, ALU.add))
                link(TS(q6, q6, ROUND, None, ALU.add))
                link(TS(q6, q6, -ROUND, None, ALU.add))
                link(STT(lo, q6, -2.0 * SLOTS, rk, ALU.mult, ALU.add))
                Lh = hreg[:, 0:n6 * P].rearrange("p (n s) -> p n s", s=P)
                Hh = tmp[:, 2048:2048 + n6 * npr].rearrange("p (n a) -> p n a", a=npr)
                for t in range(nt):
                    u = slice(t * TOPK, (t + 1) * TOPK)
                    TT(Lh[:, u, :], row[:, :].unsqueeze(1).to_broadcast([P, TOPK, P]), lo[:, u].unsqueeze(2).to_broadcast([P, TOPK, P]),
                       ALU.is_equal)
                    link(TT(Hh[:, u, :], row[:, 0:npr].unsqueeze(1).to_broadcast([P, TOPK, npr]),
                            q6[:, u].unsqueeze(2).to_broadcast([P, TOPK, npr]), ALU.is_equal))
                    TS(Hh[:, u, :], Hh[:, u, :], const("tok1")[:, t:t + 1], None, ALU.mult).then_inc(sem(f"onehots{l}"), 1)
                key = ("slot", l)
                b = product(dve, key)
                link(TS(rsc[:, 512:512 + npr], b[:, 0:npr], -1.0, 0.0, ALU.add, ALU.max))
                release(V.tensor_copy(idx[:, 0:npr], rsc[:, 512:512 + npr]), key)
                taken(dve, key)
                dve.sem_inc(sem(f"routed{l}"), 1)
                dve.wait_ge(sem(f"routed{l}"), 1)
                dve.wait_ge(sem(f"h2_stored{l}"), 16 * nt)
                ng = dve.value_load(ngt[0:1, 0:1], min_val=0, max_val=nx // NSLOT) + NE // NSLOT

                def copy_T(q, par):
                    ge(dve, sem(f"xT{l}"), q + 1)
                    ge(dve, sem(f"gate_up{l}"), 2 * q - 2)
                    V.tensor_copy(xTb[par][:, 512:1024], bank[1][:, :]).then_inc(sem(f"xT1_copied{l}"), 1)

                def hidden(b, j):
                    ge(dve, sem(f"gated{l}"), b + 1)
                    ge(dve, sem(f"hidT{l}"), b - 1)
                    TT(hidb[j % 2], silub[j % 2], bank[2 + j % 2][:, P:2 * P], ALU.mult).then_inc(sem(f"hidden{l}"), 1)

                def hidden_T(b, j):
                    ge(dve, sem(f"hidT{l}"), b + 1)
                    ge(dve, sem(f"down{l}"), b - 1)
                    V.tensor_copy(hidTb[j % 2], bank[4 + j % 2][:, 0:P]).then_inc(sem(f"hidT_copied{l}"), 1)

                def y_out(b, g, j):
                    ge(dve, sem(f"down{l}"), b + 1)
                    ge(dve, sem(f"y_stored{l}_{j}"), g * 32)
                    V.tensor_copy(yb[j], bank[6 + j % 2][:, :]).then_inc(sem(f"y_out{l}"), 1)

                def group(g):
                    for j in range(NSLOT):
                        b = g * NSLOT + j
                        first = isinstance(b, int) and b == 0
                        if j % 2:
                            copy_T(g * 2 + (j + 1) // 2, (j + 1) // 2 % 2)
                        if not first:
                            hidden_T(b - 1, (j - 1) % NSLOT)
                        hidden(b, j)
                        if not first:
                            y_out(b - 1, g if j else g - 1, (j - 1) % NSLOT)

                copy_T(0, 0)
                group(0)
                with dve.Fori(1, ng) as g:
                    group(g)
                hidden_T(ng * NSLOT - 1, NSLOT - 1)
                y_out(ng * NSLOT - 1, ng - 1, NSLOT - 1)
                for s in streams(l):
                    taken(dve, ("bc", l, GT2, s, 0))
                    taken(dve, ("bc", l, GT2, s, 1))

                def residual(t):
                    s = 0 if t < 2 else 1
                    dve.wait_ge(sem(f"rms4_{l}"), t + 1)
                    link(V.reciprocal(st[:, 40 + t:41 + t], st[:, 25 + 2 * t:26 + 2 * t]))
                    f = areg[:, t * D:(t + 1) * D]
                    link(STT(f, f, st[:, 40 + t:41 + t], qkreg[:, s * D:(s + 1) * D], ALU.mult, ALU.mult))
                    TT(Xt[:, t, :], Xt[:, t, :], f, ALU.add).then_inc(sem(f"x_done{l}"), 1)

                for t in range(nt):
                    taken(dve, ("sd", l, t, 0))
                    taken(dve, ("sd", l, t, 1))
                    for k in range(TOPK):
                        i = t * TOPK + k
                        dve.wait_ge(sem(f"back{l}_{i % NBACK}"), 16 * (i // NBACK + 1))
                        f = areg[:, t * D:(t + 1) * D]
                        STT(f, backb[i % NBACK], w6[:, i:i + 1], f, ALU.mult, ALU.add).then_inc(sem(f"added{l}"), 1)
                        dve.wait_ge(sem(f"added{l}"), i + 1)
                        if t and k == 1:
                            residual(t - 1)
                        if t and k == 3 and l + 1 < DEPTH:
                            normalised(l + 1, t - 1)
                residual(nt - 1)
                if l + 1 < DEPTH:
                    normalised(l + 1, nt - 1)

        @block.gpsimd
        def _(pool):
            G = nc.gpsimd
            pool.wait_ge(sem("zeroed"), 1)
            pool.wait_ge(sem("roped0"), 2)
            for l in range(DEPTH):
                n = extra_blocks(nt_of(l) * P) * SLOTS // P
                pool.dma_start(yd[l][NE * SLOTS:, :].rearrange("(p n) (h a) -> p (n h) a", p=P, h=2),
                               areg[:, 0:512].unsqueeze(1).to_broadcast([P, 2 * n, 512])).then_inc(sem("cleared"), 16)
                pool.wait_ge(sem("cleared"), 16 * (l + 1))
            for l in range(DEPTH):
                nt = nt_of(l)
                nx = extra_blocks(nt * P)
                for t in range(nt):
                    pool.wait_ge(sem(f"h2_{l}"), t + 1)
                    pool.dma_start(h2d[l][t * P:(t + 1) * P, :], tmp[:, (t % 2) * D:(t % 2 + 1) * D])\
                        .then_inc(sem(f"h2_stored{l}"), 16)
                    pool.wait_ge(sem(f"h2_stored{l}"), 16 * (t + 1))
                pool.wait_ge(sem(f"routed{l}"), 1)
                ng = pool.value_load(ngt[0:1, 0:1], min_val=0, max_val=nx // NSLOT) + NE // NSLOT

                def waited():
                    pool.sem_inc(sem(f"turns{l}"), 1)

                def gather(q, par):
                    ge(pool, sem(f"xT{l}"), q - 1)
                    G.tensor_copy(idxb[:, par:par + 1], idx[:, bass.ds(q, 1)]).then_inc(sem(f"picked{l}"), 1)
                    ge(pool, sem(f"picked{l}"), q + 1)
                    waited()
                    G.indirect_dma_start(xgb[par], None, h2d[l], bass.IndirectOffsetOnAxis(ap=idxb[:, par:par + 1], axis=0))\
                        .then_inc(sem(f"gathered{l}_{par}"), 16)

                gather(0, 0)
                gather(1, 1)
                with pool.Fori(1, ng) as g:
                    for par in range(2):
                        gather(g * 2 + par, par)
                for par in range(2):
                    gather(ng * 2 + par, par)
                for j in range(NSLOT):
                    pool.wait_ge(sem(f"y_stored{l}_{j}"), ng * 32)
                for par in range(2):
                    pool.wait_ge(sem(f"gathered{l}_{par}"), (ng + 1) * 16)
                pool.wait_ge(sem(f"down{l}"), ng * NSLOT)
                waited()
                for i in range(nt * TOPK):
                    if i >= NBACK:
                        pool.wait_ge(sem(f"added{l}"), i - NBACK + 1)
                    G.indirect_dma_start(backb[i % NBACK], None, yd[l], bass.IndirectOffsetOnAxis(ap=back[:, i:i + 1], axis=0))\
                        .then_inc(sem(f"back{l}_{i % NBACK}"), 16)


_INS = ['x', 'c', 'ctx', 'c_ctx', 'w_mod', 'b_mod', 'g_pre_mix', 'g_post_mix', 'g_pre_ffn', 'g_post_ffn', 'w_in',
        'w_out', 'ret_decay_logit', 'gla_w_gate', 'gla_b_gate', 'gla_norm_g', 'diff_lambda', 'diff_norm_g',
        'w_router', 'router_bias', 'w_exp_gate', 'w_exp_up', 'w_exp_down', 'w_sh_gate', 'w_sh_up', 'w_sh_down']


def kernel(**inputs):
    import concourse.bacc as bacc
    from concourse.bass_utils import run_bass_kernel_spmd

    nc = bacc.Bacc("TRN2", target_bir_lowering=False, num_devices=1)
    arrays = {name: np.ascontiguousarray(inputs[name]) for name in _INS}
    arrays["shape_tables"] = np.ascontiguousarray(np.concatenate(list(CONSTS.values()), axis=1))
    arrays["level_masks"] = MASKS
    args = [nc.dram_tensor(f"in_{n}", a.shape, mybir.dt.from_np(a.dtype), kind="ExternalInput").ap()
            for n, a in arrays.items()]
    out = nc.dram_tensor("out", (1, SEQ, D), mybir.dt.float32, kind="ExternalOutput").ap()
    hybrid_block(nc, *args, out)
    r = run_bass_kernel_spmd(nc, [{f"in_{n}": a for n, a in arrays.items()}], core_ids=[0])
    return r.results[0]["out"]
```
